# Optimizing a Trainium2 kernel written in Bass

```python
import math
import jax, jax.numpy as jnp
from jax import lax
import numpy as np

D_MODEL = 1024
BATCH = 1
SEQ = 256
DEPTH = 2
DEC_BATCH = 1
DEC_SEQ = 512
PAST_LEN = 128

N_HEADS = 12
HEAD_DIM = 64
MIX_WIDTH = N_HEADS * HEAD_DIM
DILATED_GROUPS = ((128, 1), (512, 4), (2048, 16))
HEADS_PER_GROUP = N_HEADS // len(DILATED_GROUPS)
N_KV_HEADS = 4
Q_PER_KV = N_HEADS // N_KV_HEADS
KV_WIDTH = N_KV_HEADS * HEAD_DIM
LOCAL_HALF_WINDOW = 128
N_BUCKETS = 32
REL_MAX_DISTANCE = 1024
N_EXPERTS = 16
EC_CAPACITY_FACTOR = 2
D_EXPERT = 1024
N_MIXERS = 2
N_A_LAYERS = (DEPTH + 1) // 2
N_B_LAYERS = DEPTH // 2
RMS_EPS = 1e-6
NEG_INF = -1e30

kernel_name = "hybrid_dilated_local_ec_encoder"

def rms_norm(x, gain):
    xf = x.astype(jnp.float32)
    y = xf * lax.rsqrt(jnp.mean(xf * xf, axis=-1, keepdims=True) + RMS_EPS)
    return (y * gain.astype(jnp.float32)).astype(x.dtype)

def t5_bucket(rel):
    half = N_BUCKETS // 2
    max_exact = half // 2
    n = -rel
    base = np.where(n < 0, half, 0)
    n = np.abs(n)
    large = max_exact + (np.log(np.maximum(n, 1) / max_exact)
                         / math.log(REL_MAX_DISTANCE / max_exact) * (half - max_exact)).astype(np.int32)
    large = np.minimum(large, half - 1)
    return (base + np.where(n < max_exact, n, large)).astype(np.int32)

def band_offsets(block):
    return np.arange(3 * block)[None, :] - block - np.arange(block)[:, None]

def banded_attention(q, k, v, half_window, bias, sink=None):
    B, K, G, n, D = q.shape
    qb_size = half_window
    nb = -(-n // qb_size)
    pad = nb * qb_size - n
    qb = jnp.pad(q, ((0, 0), (0, 0), (0, 0), (0, pad), (0, 0))).reshape(B, K, G, nb, qb_size, D)

    def key_blocks(t):
        tp = jnp.pad(t, ((0, 0), (0, 0), (qb_size, qb_size + pad), (0, 0))).reshape(B, K, nb + 2, qb_size, D)
        return jnp.concatenate([tp[:, :, :-2], tp[:, :, 1:-1], tp[:, :, 2:]], axis=3)

    kb, vb = key_blocks(k), key_blocks(v)
    rel = band_offsets(qb_size)
    key_pos = np.arange(nb)[:, None] * qb_size + np.arange(3 * qb_size)[None, :] - qb_size
    mask = (np.abs(rel) <= half_window)[None] & ((key_pos >= 0) & (key_pos < n))[:, None, :]

    s = jnp.einsum('bkgnqd,bkncd->bkgnqc', qb, kb, preferred_element_type=jnp.float32) * (D ** -0.5)
    s = jnp.where(mask, s + bias[None, :, :, None], NEG_INF)
    lse = jax.nn.logsumexp(s, axis=-1)
    if sink is not None:
        lse = jnp.logaddexp(lse, sink.astype(jnp.float32)[None, :, :, None, None])
    p = jnp.exp(s - lse[..., None])
    out = jnp.einsum('bkgnqc,bkncd->bkgnqd', p.astype(v.dtype), vb)
    out = out.reshape(B, K, G, nb * qb_size, D)[:, :, :, :n]
    lse = lse.reshape(B, K, G, nb * qb_size)[:, :, :, :n]
    return out, lse

def dilated_attention(h, w_in, q_gain, k_gain, w_out, rel_bias):
    B, L, _ = h.shape
    qkv = (h @ w_in).reshape(B, L, 3, N_HEADS, HEAD_DIM)
    q = rms_norm(qkv[:, :, 0], q_gain)
    k = rms_norm(qkv[:, :, 1], k_gain)
    v = qkv[:, :, 2]
    outs, lses = [], []
    for g, (window, dil) in enumerate(DILATED_GROUPS):
        heads = slice(g * HEADS_PER_GROUP, (g + 1) * HEADS_PER_GROUP)
        half = window // (2 * dil)
        n = L // dil

        def fold(t):
            return t.reshape(B, n, dil, HEADS_PER_GROUP, HEAD_DIM).transpose(0, 2, 3, 1, 4).reshape(
                B * dil, HEADS_PER_GROUP, n, HEAD_DIM)

        qg, kg, vg = fold(q[:, :, heads]), fold(k[:, :, heads]), fold(v[:, :, heads])
        bucket = t5_bucket(band_offsets(half) * dil)
        bias = rel_bias[bucket, heads].astype(jnp.float32).transpose(2, 0, 1)[:, None]
        o, lse = banded_attention(qg[:, :, None], kg, vg, half, bias)
        o = o[:, :, 0].reshape(B, dil, HEADS_PER_GROUP, n, HEAD_DIM).transpose(0, 3, 1, 2, 4).reshape(
            B, L, HEADS_PER_GROUP, HEAD_DIM)
        lse = lse[:, :, 0].reshape(B, dil, HEADS_PER_GROUP, n).transpose(0, 3, 1, 2).reshape(
            B, L, HEADS_PER_GROUP)
        outs.append(o)
        lses.append(lse)
    alpha = jax.nn.softmax(jnp.stack(lses), axis=0)
    outs = jnp.stack(outs)
    mixed = (alpha[..., None].astype(outs.dtype) * outs).transpose(1, 2, 0, 3, 4).reshape(B, L, MIX_WIDTH)
    return mixed @ w_out

def local_gqa_attention(h, w_in, q_gain, k_gain, sink, w_out, rel_bias):
    B, L, _ = h.shape
    proj = h @ w_in
    q = proj[..., :MIX_WIDTH].reshape(B, L, N_KV_HEADS, Q_PER_KV, HEAD_DIM)
    k = proj[..., MIX_WIDTH:MIX_WIDTH + KV_WIDTH].reshape(B, L, N_KV_HEADS, HEAD_DIM)
    v = proj[..., MIX_WIDTH + KV_WIDTH:].reshape(B, L, N_KV_HEADS, HEAD_DIM)
    q = rms_norm(q, q_gain).transpose(0, 2, 3, 1, 4)
    k = rms_norm(k, k_gain).transpose(0, 2, 1, 3)
    v = v.transpose(0, 2, 1, 3)
    half = LOCAL_HALF_WINDOW
    bucket = t5_bucket(band_offsets(half))
    bias = rel_bias[bucket].astype(jnp.float32).transpose(2, 0, 1).reshape(N_KV_HEADS, Q_PER_KV, half, 3 * half)
    o, _ = banded_attention(q, k, v, half, bias, sink.reshape(N_KV_HEADS, Q_PER_KV))
    o = o.transpose(0, 3, 1, 2, 4).reshape(B, L, MIX_WIDTH)
    return o @ w_out

def expert_choice_ffn(h, w_router, w_gate, w_up, w_down):
    B, L, Dm = h.shape
    T = B * L
    cap = EC_CAPACITY_FACTOR * T // N_EXPERTS
    tokens = h.reshape(T, Dm)
    affinity = jax.nn.softmax(
        jnp.einsum('td,de->te', tokens, w_router, preferred_element_type=jnp.float32), axis=-1)
    gate, idx = lax.top_k(affinity.T, cap)
    xe = tokens[idx]
    hid = jax.nn.silu(jnp.einsum('ecd,edf->ecf', xe, w_gate)) * jnp.einsum('ecd,edf->ecf', xe, w_up)
    ye = jnp.einsum('ecf,efd->ecd', hid, w_down) * gate[..., None].astype(hid.dtype)
    out = jnp.zeros_like(tokens).at[idx.reshape(-1)].add(ye.reshape(-1, Dm).astype(tokens.dtype))
    return out.reshape(B, L, Dm)

def encoder_trunk(x, rel_bias, norm_mix, norm_ffn, a_w_in, a_q_gain, a_k_gain, a_w_out,
                  b_w_in, b_q_gain, b_k_gain, b_sink, b_w_out,
                  moe_router, moe_w_gate, moe_w_up, moe_w_down):
    for i in range(DEPTH):
        h = rms_norm(x, norm_mix[i])
        j = i // N_MIXERS
        if i % N_MIXERS == 0:
            x = x + dilated_attention(h, a_w_in[j], a_q_gain[j], a_k_gain[j], a_w_out[j], rel_bias)
        else:
            x = x + local_gqa_attention(h, b_w_in[j], b_q_gain[j], b_k_gain[j], b_sink[j], b_w_out[j], rel_bias)
        h = rms_norm(x, norm_ffn[i])
        x = x + expert_choice_ffn(h, moe_router[i], moe_w_gate[i], moe_w_up[i], moe_w_down[i])
    return x

def setup_inputs(seed: int = 0) -> dict:
    key = jax.random.key(seed)
    ks = jax.random.split(key, 20)
    f32 = jnp.float32

    def nrm(k, shape, scale):
        return jax.random.normal(k, shape, f32) * scale

    return {
        "x_prompt": nrm(ks[0], (BATCH, SEQ, D_MODEL), 1.0),
        "x_sample": nrm(ks[1], (DEC_BATCH, DEC_SEQ, D_MODEL), 1.0),
        "rel_bias": nrm(ks[2], (N_BUCKETS, N_HEADS), 0.5),
        "norm_mix": 1.0 + nrm(ks[3], (DEPTH, D_MODEL), 0.02),
        "norm_ffn": 1.0 + nrm(ks[4], (DEPTH, D_MODEL), 0.02),
        "a_w_in": nrm(ks[5], (N_A_LAYERS, D_MODEL, 3 * MIX_WIDTH), D_MODEL ** -0.5),
        "a_q_gain": 1.0 + nrm(ks[6], (N_A_LAYERS, HEAD_DIM), 0.02),
        "a_k_gain": 1.0 + nrm(ks[7], (N_A_LAYERS, HEAD_DIM), 0.02),
        "a_w_out": nrm(ks[8], (N_A_LAYERS, MIX_WIDTH, D_MODEL), MIX_WIDTH ** -0.5),
        "b_w_in": nrm(ks[9], (N_B_LAYERS, D_MODEL, MIX_WIDTH + 2 * KV_WIDTH), D_MODEL ** -0.5),
        "b_q_gain": 1.0 + nrm(ks[10], (N_B_LAYERS, HEAD_DIM), 0.02),
        "b_k_gain": 1.0 + nrm(ks[11], (N_B_LAYERS, HEAD_DIM), 0.02),
        "b_sink": nrm(ks[12], (N_B_LAYERS, N_HEADS), 1.0),
        "b_w_out": nrm(ks[13], (N_B_LAYERS, MIX_WIDTH, D_MODEL), MIX_WIDTH ** -0.5),
        "moe_router": nrm(ks[14], (DEPTH, D_MODEL, N_EXPERTS), D_MODEL ** -0.5),
        "moe_w_gate": nrm(ks[15], (DEPTH, N_EXPERTS, D_MODEL, D_EXPERT), D_MODEL ** -0.5),
        "moe_w_up": nrm(ks[16], (DEPTH, N_EXPERTS, D_MODEL, D_EXPERT), D_MODEL ** -0.5),
        "moe_w_down": nrm(ks[17], (DEPTH, N_EXPERTS, D_EXPERT, D_MODEL), D_EXPERT ** -0.5),
    }

def reference(x_prompt, x_sample, rel_bias, norm_mix, norm_ffn, a_w_in, a_q_gain, a_k_gain, a_w_out,
              b_w_in, b_q_gain, b_k_gain, b_sink, b_w_out, moe_router, moe_w_gate, moe_w_up, moe_w_down):
    y_prompt = encoder_trunk(x_prompt, rel_bias, norm_mix, norm_ffn, a_w_in, a_q_gain, a_k_gain, a_w_out,
                             b_w_in, b_q_gain, b_k_gain, b_sink, b_w_out,
                             moe_router, moe_w_gate, moe_w_up, moe_w_down)
    y_sample = encoder_trunk(x_sample, rel_bias, norm_mix, norm_ffn, a_w_in, a_q_gain, a_k_gain, a_w_out,
                             b_w_in, b_q_gain, b_k_gain, b_sink, b_w_out,
                             moe_router, moe_w_gate, moe_w_up, moe_w_down)
    return (y_prompt, y_sample)


_drawn_inputs = setup_inputs


def setup_inputs(seed=0):
    import zlib

    import numpy as np

    out = dict(_drawn_inputs(seed))
    spreads = {}
    factors = {'norm_mix': 4.642,
     'a_q_gain': 6.992,
     'a_k_gain': 6.471,
     'b_q_gain': 8.0,
     'b_k_gain': 8.0,
     'b_sink': 8.0}
    for name, (base, spread) in spreads.items():
        noise = np.random.default_rng([zlib.crc32(name.encode()), seed]).standard_normal(out[name].shape)
        drawn = base * np.exp(spread * noise) if base else spread * noise
        out[name] = __import__('jax').numpy.asarray(drawn.astype(out[name].dtype))
    for name, factor in factors.items():
        out[name] = (out[name] * factor).astype(out[name].dtype)
    return out
```

```python
import math
from contextlib import ExitStack

import numpy as np

import concourse.bass as bass
from concourse import mybir

F32 = mybir.dt.float32
F32R = mybir.dt.float32r
I32 = mybir.dt.int32
U32 = mybir.dt.uint32
ACT = mybir.ActivationFunctionType
ALU = mybir.AluOpType
AX = mybir.AxisListType

P = 128
BANK = 512
DM = 1024
KM = DM // P
SEQ, DEC_SEQ = 256, 512
TOK = SEQ + DEC_SEQ
NT = TOK // P
PT_ = SEQ // P
LAYERS = 2
HD, NH, NKV = 64, 12, 4
MIX = NH * HD
KX = MIX // P
KVW = NKV * HD
GH = 4
GW = GH * HD
NG = NH // GH
DILATIONS = (1, 4, 16)
HALF_A, HALF_B = 64, 128
BUCKETS, REL_MAX = 32, 1024
EPS = 1e-6
MASKED = -1e30
BAND = 3 * P
ROW = GW + 2 * GH
NE, DE = 16, 1024
CS, CP = 2 * DEC_SEQ // NE, 2 * SEQ // NE
C = CS + CP
PAIRS = NE // 2
PIECES = 12
PW = DE // 4
TAB = {(0, 0): (0, 2 * BAND - 2 * P, HALF_A, 1, 1), (1, 0): (1536, 2 * BAND - 2 * P, HALF_B, 1, 1)}
for _g in (1, 2):
    for _r, _tiles in enumerate((PT_, NT - PT_)):
        TAB[0, _g, _r] = (2 * _g * 256 + 256 * _r, 2 * P, HALF_A, _tiles, DILATIONS[_g] // _tiles)
TABW = 2048
CHUNKS = ([(0, kind, g, n * MIX + g * GW) for g in range(NG) for n, kind in enumerate("qkv")]
          + [(0, "o", None, n * GW) for n in range(DM // GW)]
          + [(1, "k", 0, MIX), (1, "v", 0, MIX + KVW)] + [(1, "q", g, g * GW) for g in range(NG)]
          + [(1, "o", None, n * GW) for n in range(DM // GW)])


def t5_bucket(rel):
    half = BUCKETS // 2
    max_exact = half // 2
    n = -rel
    base = np.where(n < 0, half, 0)
    n = np.abs(n)
    large = max_exact + (np.log(np.maximum(n, 1) / max_exact)
                         / math.log(REL_MAX / max_exact) * (half - max_exact)).astype(np.int32)
    return (base + np.where(n < max_exact, n, np.minimum(large, half - 1))).astype(np.int32)


def shape_constants():
    buckets = np.zeros((BUCKETS + 1, TABW), np.float32)
    for start, width, half, stride, every in TAB.values():
        for i in range(width):
            rel = i - (BAND - P - 1 if width > 2 * P else P - 1)
            if rel % every == 0 and abs(rel) // every <= half:
                buckets[t5_bucket(np.array(rel * stride)), start + i] = 1.0
            else:
                buckets[BUCKETS, start + i] = MASKED
    return {"c_buckets": buckets, "c_ident": np.eye(P, dtype=np.float32),
            "c_iota": np.tile(np.arange(DEC_SEQ, dtype=np.float32), (P, 1))}


def units_of(layer):
    out = []
    for g in range(NG):
        for t in range(NT):
            lo, hi = (0, PT_) if t < PT_ else (PT_, NT)
            if layer == 0 and g > 0:
                out.append((g, t, t, 1))
            else:
                first = max(t - 1, lo)
                out.append((g, t, first, min(t + 2, hi) - first))
    return out


def batches_of(layer, unit):
    g, t, first, n = unit
    if layer == 0 and g > 0:
        return [[(h, t) for h in range(GH)]]
    return [[(h, k) for k in range(first, first + n)] for h in range(GH)]


def tile_rows(ap, layer, g, t):
    base, tiles, n = (0, PT_, t) if t < PT_ else (PT_ * P, NT - PT_, t - PT_)
    if layer == 0 and g > 0:
        return ap[:, base:base + tiles * P].rearrange("p (m r) -> p r m", r=tiles)[:, n, :]
    return ap[:, t * P:(t + 1) * P]


def build_trunk(nc, d, outs):
    ctx = ExitStack()
    with ctx:
        def sb(name, shape, dt=F32, scope=ctx):
            return scope.enter_context(nc.sbuf_tensor(name, shape, dt))

        def sem(name):
            return ctx.enter_context(nc.semaphore(name))

        tab_d = nc.dram_tensor("bias_rows", [NH, TABW], F32)
        tab_ap = tab_d.ap()
        unit_d = nc.dram_tensor("unit_rows", [NG, TOK, ROW], F32).ap()
        h_d = nc.dram_tensor("ffn_rows", [TOK, DM], F32).ap()

        x = sb("x", [P, NT, DM])
        ring_gu = sb("ring_gu", [P, 8, KM, PW])
        gain = sb("gain", [P, DM])
        ident = sb("ident", [P, P])
        head_gain = sb("head_gain", [P, 2 * LAYERS, HD])
        sink = sb("sink", [P, NH])
        minus_half = sb("minus_half", [P, NT * GH])
        sumsq = sb("sumsq", [P, NT])
        var = sb("var", [P, NT])
        rstd = sb("rstd", [P, NT])
        hsum = sb("hsum", [P, NT * GH])
        hvar = sb("hvar", [P, NT * GH])
        hrstd = sb("hrstd", [P, NT * GH])
        mix_top = sb("mix_top", [P, NH])
        mix_arg = sb("mix_arg", [P, 2 * NH])
        mix_exp = sb("mix_exp", [P, 2 * NH])
        mix_w = sb("mix_w", [P, NH])
        mix_den = sb("mix_den", [P, NH])
        mix_rec = sb("mix_rec", [P, NH])
        mix_c = sb("mix_c", [P, NH])
        lmax = sb("lmax", [P, NT])
        lgt = sb("lgt", [P, NT, NE])
        lexp = sb("lexp", [P, NT, NE])
        lsum = sb("lsum", [P, NT])
        lrec = sb("lrec", [P, NT])
        aff = sb("aff", [P, NT, NE])
        slot_s = sb("slot_s", [P, PAIRS])
        slot_p = sb("slot_p", [2 * CP, PAIRS])
        gate_s = sb("gate_s", [P, PAIRS])
        gate_p = sb("gate_p", [2 * CP, PAIRS])
        take_s = sb("take_s", [P, PAIRS], I32)
        take_p = sb("take_p", [2 * CP, PAIRS], I32)

        with ExitStack() as at:
            hT = sb("hT", [P, KM, TOK], scope=at)
            wbuf = sb("wbuf", [P, 2, KM, GW], scope=at)
            qraw = sb("qraw", [P, NT, GW], scope=at)
            kraw = sb("kraw", [P, NT, GW], scope=at)
            v = sb("v", [P, NT, GW], scope=at)
            qT = sb("qT", [P, 2, TOK], scope=at)
            kT = sb("kT", [P, NKV, TOK], scope=at)
            probs = sb("probs", [P, 2, GH * BAND], scope=at)
            probsT = sb("probsT", [P, 2, BANK], scope=at)
            row = sb("row", [P, 3, ROW], scope=at)
            bias = sb("bias", [P, 2, GH * BAND], scope=at)
            sq = probsT[:, :, :].rearrange("p a b -> p (a b)")[:, 0:NT * GW // 2]
            buckets = bias[0:BUCKETS + 1, :, :].rearrange("p a b -> p (a b)")[:, 0:TABW]
            rb = row[0:BUCKETS + 1, 0, 0:NH]
            tab = probs[0:NH, :, :].rearrange("p a b -> p (a b)")[:, 0:TABW]
            mix_in = [qraw[:, :, :].rearrange("p t c -> p (t c)")[:, 0:NG * ROW],
                      kraw[:, :, :].rearrange("p t c -> p (t c)")[:, 0:NG * ROW]]

        with ExitStack() as mo:
            ring_d = sb("ring_d", [P, 4, KM, PW], scope=mo)
            hrow = sb("hrow", [P, 2, DM], scope=mo)
            hTr = sb("hTr", [P, 2, KM, P], scope=mo)
            router = sb("router", [P, KM, NE], scope=mo)
            iota = sb("iota", [P, DEC_SEQ], scope=mo)
            am = sb("am", [48, DEC_SEQ], scope=mo)
            top = sb("top", [48, CS], scope=mo)
            topi = sb("topi", [48, CS], U32, scope=mo)
            pk_i = sb("pk_i", [48, P], scope=mo)
            pk_g = sb("pk_g", [48, P], scope=mo)
            xg_s = sb("xg_s", [P, DM], scope=mo)
            xg_p = sb("xg_p", [2 * CP, DM], scope=mo)
            xeT = sb("xeT", [P, KM, 2, C], scope=mo)
            sg = sb("sg", [P, 2, 2, C], scope=mo)
            hid = sb("hid", [P, 2, KM, C], scope=mo)
            yT = sb("yT", [P, 2, KM, C], scope=mo)
            y_s = sb("y_s", [P, DM], scope=mo)
            y_p = sb("y_p", [2 * CP, DM], scope=mo)
            hi_s = sb("hi_s", [P, DM], F32R, scope=mo)
            hi_p = sb("hi_p", [2 * CP, DM], F32R, scope=mo)
            lo_s = sb("lo_s", [P, DM], F32R, scope=mo)
            lo_p = sb("lo_p", [2 * CP, DM], F32R, scope=mo)
            hot_s = sb("hot_s", [P, DEC_SEQ], F32R, scope=mo)
            hot_p = sb("hot_p", [2 * CP, SEQ], F32R, scope=mo)

        ps = ctx.enter_context(nc.psum_tensor("ps", [P, 8, BANK], F32))

        const_in = sem("const_in")
        tab_in = sem("tab_in")
        rb_set = sem("rb_set")
        tab_mm = sem("tab_mm")
        tab_cp = sem("tab_cp")
        tab_out = sem("tab_out")
        x_in = sem("x_in")
        gain_in = sem("gain_in")
        sumsq_ready = sem("sumsq_ready")
        var_ready = sem("var_ready")
        rstd_ready = sem("rstd_ready")
        h_ready = sem("h_ready")
        h_turned = sem("h_turned")
        hT_ready = sem("hT_ready")
        w_in = [sem(f"w_in{i}") for i in range(2)]
        proj_done = sem("proj_done")
        qkv_taken = sem("qkv_taken")
        head_sums = sem("head_sums")
        hvar_ready = sem("hvar_ready")
        hrstd_ready = sem("hrstd_ready")
        head_normed = sem("head_normed")
        qk_turned = sem("qk_turned")
        qk_taken = sem("qk_taken")
        bias_in = [sem(f"bias_in{i}") for i in range(2)]
        scores_done = sem("scores_done")
        logits_ready = sem("logits_ready")
        negmax_ready = sem("negmax_ready")
        probs_ready = sem("probs_ready")
        probs_turned = sem("probs_turned")
        probsT_ready = sem("probsT_ready")
        unit_done = sem("unit_done")
        row_ready = sem("row_ready")
        row_out = [sem(f"row_out{i}") for i in range(3)]
        mix_in_s = [sem(f"mix_in_s{i}") for i in range(2)]
        mix_step = sem("mix_step")
        mix_arg_ready = sem("mix_arg_ready")
        mix_exp_ready = sem("mix_exp_ready")
        mixed_ready = sem("mixed_ready")
        mix_turned = sem("mix_turned")
        mixT_ready = sem("mixT_ready")
        attn_added = sem("attn_added")
        h_out = [sem(f"h_out{i}") for i in range(2)]
        route_in = sem("route_in")
        route_mm = sem("route_mm")
        route_step = sem("route_step")
        rlog_ready = sem("rlog_ready")
        rexp_ready = sem("rexp_ready")
        aff_ready = sem("aff_ready")
        aff_turned = sem("aff_turned")
        picks_ready = sem("picks_ready")
        picks_turned = sem("picks_turned")
        slots_ready = sem("slots_ready")
        piece_in = [sem(f"piece_in{i}") for i in range(PIECES)]
        xg_s_in = sem("xg_s_in")
        xg_p_in = sem("xg_p_in")
        xe_turned = sem("xe_turned")
        xs_ready = sem("xs_ready")
        xp_ready = sem("xp_ready")
        gu_done = sem("gu_done")
        silu_ready = sem("silu_ready")
        hid_ready = sem("hid_ready")
        down_done = sem("down_done")
        yT_ready = sem("yT_ready")
        y_turned = sem("y_turned")
        ys_ready = sem("ys_ready")
        yp_ready = sem("yp_ready")
        hi_ready = sem("hi_ready")
        lo_ready = sem("lo_ready")
        hot_ready = sem("hot_ready")
        comb_done = sem("comb_done")
        moe_added = sem("moe_added")
        y_out = sem("y_out")

        UNITS = [units_of(0), units_of(1)]
        NU = NG * NT
        UNIT_FOR_GROUP = NT
        LAST_OUT = NT * DM // GW
        ADDS = 2 * NT

        def w_dram(chunk):
            layer, kind, g, col = CHUNKS[chunk]
            w = d[("a" if layer == 0 else "b") + ("_w_out" if kind == "o" else "_w_in")][0]
            return w[:, col:col + GW].rearrange("(k p) n -> p k n", p=P), (KX if kind == "o" else KM)

        def chunk_at(layer, kind, g):
            return CHUNKS.index(next(c for c in CHUNKS if c[:3] == (layer, kind, g)))

        FIRST_CHUNK = [0, chunk_at(1, "k", 0)]
        FIRST_OUT = [chunk_at(0, "o", None), chunk_at(1, "o", None)]

        def unit_rows(layer, g, t):
            base, tiles, n = (0, PT_, t) if t < PT_ else (PT_ * P, NT - PT_, t - PT_)
            if layer == 0 and g > 0:
                return unit_d[g, base:base + tiles * P, :].rearrange("(m r) c -> r m c", r=tiles)[tiles - 1 - n]
            at = base + (tiles - 1 - n) * P
            return unit_d[g, at:at + P, :]

        def mirror(t):
            return PT_ - 1 - t if t < PT_ else PT_ + NT - 1 - t

        def unit_rank(layer, n):
            return layer * NU + n

        def row_out_of(u):
            return row_out[u % 3], 16 * (u // 3 + 1)

        BIAS_LOADS = [1, 2, 2, 1, 1, 1]

        def bias_value(n):
            return 16 * sum(BIAS_LOADS[n % 2:n + 1:2])

        def bias_view(layer, unit):
            g, t, first, n = unit
            buf = bias[:, (layer * NG + g) % 2, :]
            if layer == 0 and g > 0:
                kind = 0 if t < PT_ else 1
                return buf[:, kind * GH * P:(kind + 1) * GH * P].rearrange("p (h c) -> p h c", h=GH)
            at = (first - (t - 1)) * P
            return buf.rearrange("p (h c) -> p h c", h=GH)[:, :, at:at + n * P]

        def unit_view(buf, unit, layer, pitch):
            g, t, first, n = unit
            at = 0 if layer == 0 and g > 0 else (first - (t - 1)) * P
            return buf[:, 0:GH * pitch].rearrange("p (h c) -> p h c", h=GH)[:, :, at:at + n * P]

        def block_view(buf, unit, layer, pitch, h, k):
            g, t, first, n = unit
            at = h * pitch + (0 if layer == 0 and g > 0 else (k - (t - 1)) * P)
            return buf[:, at:at + P]

        s_bank = ps[:, 0:GH, :].rearrange("p b n -> p (b n)")
        u_bank = ps[:, 7, GW:2 * GW]

        block = ctx.enter_context(nc.Block())

        @block.sync
        def _(sp):
            def load_chunk(chunk):
                if chunk >= 2:
                    sp.wait_ge(proj_done, NT * (chunk - 1))
                if chunk == FIRST_CHUNK[1] or chunk == FIRST_CHUNK[1] + 1:
                    sp.wait_ge(moe_added, ADDS * PAIRS)
                src, k = w_dram(chunk)
                sp.dma_start(wbuf[:, chunk % 2, 0:k, :], src).then_inc(w_in[chunk % 2], 16)

            def load_bias(layer, g):
                n = layer * NG + g
                if n >= 2:
                    sp.wait_ge(logits_ready, NT * (n - 1))
                if layer and g == 0:
                    sp.wait_ge(moe_added, ADDS * PAIRS)
                buf = bias[:, n % 2, :]
                for r in range(BIAS_LOADS[n]):
                    if BIAS_LOADS[n] == 1:
                        start, cols = TAB[layer, 0][0], BAND
                    else:
                        start, cols = TAB[layer, g, r][0], P
                    dst = buf[:, r * GH * cols:(r + 1) * GH * cols].rearrange("p (h c) -> p h c", h=GH)
                    src = bass.AP(tab_ap.tensor, g * GH * TABW + start, [[1, P], [TABW, GH], [1, cols]])
                    sp.dma_start(dst, src).then_inc(bias_in[n % 2], 16)

            def load_piece(layer, e, i, behind=None):
                if behind is not None and i < 8:
                    sp.wait_ge(gu_done, 4 * behind + (i // 2 + 1))
                elif behind is not None:
                    sp.wait_ge(down_done, 4 * behind + (i - 7))
                if i < 8:
                    w = d["moe_w_gate" if i % 2 == 0 else "moe_w_up"]
                    dst, col = ring_gu[:, i], (i // 2) * PW
                else:
                    w = d["moe_w_down"]
                    dst, col = ring_d[:, i - 8], (i - 8) * PW
                w = w[layer].rearrange("e (k p) n -> e p k n", p=P)
                src = w[bass.ds(e, 1), :, :, col:col + PW].rearrange("o p k n -> p (o k) n")
                sp.dma_start(dst, src).then_inc(piece_in[i], 16)

            sp.dma_start(x[:, 0, :], d["x_prompt"][0, 0:P, :]).then_inc(x_in, 16)
            for t in range(1, NT):
                src = (d["x_prompt"][0, t * P:(t + 1) * P, :] if t < PT_
                       else d["x_sample"][0, (t - PT_) * P:(t - PT_ + 1) * P, :])
                sp.dma_start(x[:, t, :], src).then_inc(x_in, 16)
            sp.dma_start(gain[:], bass.AP(d["norm_mix"].tensor, 0, [[0, P], [1, DM]])).then_inc(gain_in, 16)
            sp.dma_start(ident[:], d["c_ident"]).then_inc(const_in, 16)
            for n, name in enumerate(("a_q_gain", "a_k_gain", "b_q_gain", "b_k_gain")):
                sp.dma_start(head_gain[:, n, :], bass.AP(d[name].tensor, 0, [[0, P], [1, HD]])).then_inc(const_in, 16)
            sp.dma_start(sink[:], bass.AP(d["b_sink"].tensor, 0, [[0, P], [1, NH]])).then_inc(const_in, 16)
            sp.dma_start(buckets, d["c_buckets"]).then_inc(tab_in, 16)
            sp.wait_ge(rb_set, 1)
            sp.dma_start(rb[0:BUCKETS], d["rel_bias"]).then_inc(tab_in, 16)
            load_chunk(0)
            load_chunk(1)
            sp.wait_ge(tab_cp, 1)
            sp.dma_start(tab_ap, tab).then_inc(tab_out, 16)
            sp.wait_ge(tab_out, 16)

            for layer in range(LAYERS):
                load_bias(layer, 0)
                load_bias(layer, 1)
                first = FIRST_CHUNK[layer]
                chunk = first
                if layer == 0:
                    chunk = 2
                else:
                    load_chunk(first)
                    load_chunk(first + 1)
                    sp.dma_start(gain[:], bass.AP(d["norm_mix"].tensor, DM, [[0, P], [1, DM]])).then_inc(gain_in, 16)
                    chunk = first + 2
                for i in range(8):
                    load_piece(layer, 0, i, behind=None if layer == 0 else NE * layer - 1)
                units = UNITS[layer]
                for g in range(NG):
                    while chunk < FIRST_OUT[layer] and chunk - 2 <= chunk_at(layer, "q", g) + (2 if layer == 0 else 0):
                        load_chunk(chunk)
                        chunk += 1
                    if g == 2:
                        load_bias(layer, 2)
                    for n in range(g * NT, (g + 1) * NT):
                        u = unit_rank(layer, n)
                        sp.wait_ge(row_ready, u + 1)
                        sp.dma_start(unit_rows(layer, units[n][0], units[n][1]),
                                     row[:, u % 3, :]).then_inc(row_out_of(u)[0], 16)
                while chunk < FIRST_OUT[layer] + 2:
                    load_chunk(chunk)
                    chunk += 1
                last = unit_rank(layer, NU - 1)
                for u in range(last - 2, last + 1):
                    sp.wait_ge(*row_out_of(u))
                for t in range(NT):
                    if t >= 2:
                        sp.wait_ge(mixed_ready, layer * NT + t - 1)
                    sp.dma_start(mix_in[t % 2].rearrange("p (g c) -> p g c", g=NG),
                                 unit_d[:, mirror(t) * P:(mirror(t) + 1) * P, :].rearrange("g p c -> p g c")).then_inc(mix_in_s[t % 2], 16)
                sp.wait_ge(h_ready, NT * (2 * layer + 1))
                sp.dma_start(gain[:], bass.AP(d["norm_ffn"].tensor, layer * DM, [[0, P], [1, DM]])).then_inc(gain_in, 16)
                for c in range(chunk, FIRST_OUT[layer] + DM // GW):
                    load_chunk(c)

                sp.wait_ge(attn_added, LAST_OUT * (layer + 1))
                sp.dma_start(router[:], d["moe_router"][layer].rearrange("(k p) e -> p k e", p=P)).then_inc(route_in, 16)
                sp.dma_start(iota[:], d["c_iota"]).then_inc(route_in, 16)
                for i in range(8, PIECES):
                    load_piece(layer, 0, i)
                for t in range(NT):
                    sp.wait_ge(h_ready, NT * (2 * layer + 1) + t + 1)
                    sp.dma_start(h_d[t * P:(t + 1) * P, :], hrow[:, t % 2, :]).then_inc(h_out[t % 2], 16)
                with sp.Fori(1, NE) as e:
                    for i in range(PIECES):
                        load_piece(layer, e, i, behind=e + (NE * layer - 1))
            sp.wait_ge(moe_added, ADDS * PAIRS * LAYERS)
            for t in range(NT):
                dst = outs[0][0, t * P:(t + 1) * P, :] if t < PT_ else outs[1][0, (t - PT_) * P:(t - PT_ + 1) * P, :]
                sp.dma_start(dst, x[:, t, :]).then_inc(y_out, 16)
            sp.wait_ge(y_out, 16 * NT)

        @block.gpsimd
        def _(pool):
            hnorms = 0
            for layer in range(LAYERS):
                def row_rstd(step):
                    pool.wait_ge(var_ready, step + 1)
                    nc.gpsimd.tensor_tensor(rstd[:], var[:], minus_half[:, 0:NT], ALU.pow).then_inc(rstd_ready, 1)

                row_rstd(2 * layer)
                for _ in range(2 * NG if layer == 0 else NG + 1):
                    hnorms += 1
                    pool.wait_ge(hvar_ready, hnorms)
                    nc.gpsimd.tensor_tensor(hrstd[:], hvar[:], minus_half[:], ALU.pow).then_inc(hrstd_ready, 1)
                row_rstd(2 * layer + 1)
                pool.wait_ge(slots_ready, layer + 1)
                for t in range(2):
                    pool.wait_ge(h_out[t], 16 * NT // 2 * (layer + 1))
                for j in range(PAIRS):
                    n = layer * PAIRS + j
                    if j >= 1:
                        pool.wait_ge(xe_turned, n)
                    nc.gpsimd.indirect_dma_start(
                        out=xg_s[:], out_offset=None, in_=h_d,
                        in_offset=bass.IndirectOffsetOnAxis(ap=take_s[:, j:j + 1], axis=0)).then_inc(xg_s_in, 16)
                    nc.gpsimd.indirect_dma_start(
                        out=xg_p[:], out_offset=None, in_=h_d,
                        in_offset=bass.IndirectOffsetOnAxis(ap=take_p[:, j:j + 1], axis=0)).then_inc(xg_p_in, 16)

        @block.scalar
        def _(act):
            turned = 0
            lots = 0
            taken = 0
            for layer in range(LAYERS):
                def sums_of_squares(step):
                    for t in range(NT):
                        n = step * NT + t
                        if step == 0:
                            act.wait_ge(x_in, 16 * NT)
                        elif step % 2:
                            act.wait_ge(attn_added, LAST_OUT * layer + LAST_OUT - NT + t + 1)
                        else:
                            act.wait_ge(moe_added, ADDS * PAIRS * layer)
                        if n >= 1:
                            act.wait_ge(sumsq_ready, n)
                        if t == 0 and step:
                            act.wait_ge(rstd_ready, step)
                        nc.scalar.activation(ps[:, 4:6, :].rearrange("p b n -> p (b n)"), x[:, t, :], ACT.Square,
                                             accum_out=sumsq[:, t:t + 1]).then_inc(sumsq_ready, 1)

                def take_transposed(step, dst):
                    for t in range(NT):
                        n = step * NT + t
                        act.wait_ge(h_turned, n + 1)
                        b = 2 * (t % 2)
                        nc.scalar.activation(dst(t), ps[:, b:b + 2, :].rearrange("p b (k n) -> p (b k) n", n=P),
                                             ACT.Copy).then_inc(hT_ready, 1)

                sums_of_squares(2 * layer)
                take_transposed(2 * layer, lambda t: hT[:, :, t * P:(t + 1) * P])

                def take_chunk(chunk):
                    kind = CHUNKS[chunk][1]
                    nonlocal taken
                    for t in range(NT):
                        n = chunk * NT + t
                        act.wait_ge(proj_done, n + 1)
                        dst = {"q": qraw, "k": kraw, "v": v}[kind]
                        taken += 1
                        nc.scalar.activation(dst[:, t, :], ps[:, 6 + n % 2, 0:GW], ACT.Copy).then_inc(qkv_taken, 1)

                def take_turned(kind):
                    nonlocal turned
                    for b in range(NT // 2):
                        act.wait_ge(qk_turned, turned + 1)
                        src = ps[:, 4 + turned % 2, :].rearrange("p (t a n) -> p t a n", t=2, n=P)
                        cols = slice(b * 2 * P, (b + 1) * 2 * P)
                        if kind == "k" and layer == 1:
                            for half in range(2):
                                for to in range(2):
                                    dst = kT[to * 64:(to + 1) * 64, half::2, cols].rearrange("p a (t n) -> p t a n", t=2)
                                    ins = nc.scalar.activation(dst, src[half * 64:(half + 1) * 64], ACT.Copy)
                        else:
                            buf = qT if kind == "q" else kT
                            dst = buf[:, 0:2, cols].rearrange("p a (t n) -> p t a n", t=2)
                            if kind == "q":
                                dst = dst[:, :, :, ::-1]
                            ins = nc.scalar.activation(dst, src, ACT.Copy)
                        ins.then_inc(qk_taken, 1)
                        turned += 1

                for g in range(NG):
                    if layer == 0:
                        for kind in "qkv":
                            take_chunk(chunk_at(0, kind, g))
                        take_turned("q")
                        take_turned("k")
                    else:
                        if g == 0:
                            take_chunk(chunk_at(1, "k", 0))
                            take_chunk(chunk_at(1, "v", 0))
                        take_chunk(chunk_at(1, "q", g))
                        if g == 0:
                            take_turned("k")
                        take_turned("q")
                    for n in range(g * NT, (g + 1) * NT):
                        unit = UNITS[layer][n]
                        u = unit_rank(layer, n)
                        act.wait_ge(negmax_ready, u + 1)
                        p = unit_view(probs[:, u % 2, :], unit, layer, BAND)
                        for h in range(GH):
                            ins = nc.scalar.activation(p[:, h, :], p[:, h, :], ACT.Exp,
                                                       bias=row[:, u % 3, GW + h:GW + h + 1],
                                                       accum_out=row[:, u % 3, GW + GH + h:GW + GH + h + 1])
                        ins.then_inc(probs_ready, 1)
                        for lot in batches_of(layer, unit):
                            act.wait_ge(probs_turned, lots + 1)
                            w = len(lot) * P
                            nc.scalar.activation(probsT[:, lots % 2, 0:w], ps[:, 4 + lots % 2, 0:w],
                                                 ACT.Copy).then_inc(probsT_ready, 1)
                            lots += 1

                for t in range(NT):
                    n = layer * NT + t
                    act.wait_ge(mix_arg_ready, n + 1)
                    w = NH if layer == 0 else 2 * NH
                    nc.scalar.activation(mix_exp[:, 0:w], mix_arg[:, 0:w], ACT.Exp).then_inc(mix_exp_ready, 1)
                    act.wait_ge(mix_turned, n + 1)
                    b = 2 * (t % 2)
                    nc.scalar.activation(hT[:, 0:KX, t * P:(t + 1) * P][:, :, ::-1],
                                         ps[:, b:b + 2, :].rearrange("p b n -> p (b n)")[:, 0:MIX].rearrange("p (k n) -> p k n", n=P),
                                         ACT.Copy).then_inc(mixT_ready, 1)

                sums_of_squares(2 * layer + 1)
                take_transposed(2 * layer + 1, lambda t: hTr[:, t % 2, :, :])
                act.wait_ge(rlog_ready, layer + 1)
                nc.scalar.activation(lexp[:], lgt[:], ACT.Exp).then_inc(rexp_ready, 1)

                def turn_in(pair):
                    act.wait_ge(xe_turned, pair + 1)
                    nc.scalar.activation(xeT[:, :, :, CS:C],
                                         ps[:, 6, :].rearrange("p (k e c) -> p k e c", k=KM, e=2),
                                         ACT.Copy).then_inc(xp_ready, 1)

                def silus(e, par):
                    for i in range(4):
                        act.wait_ge(gu_done, 4 * e + (i + 1))
                        nc.scalar.activation(sg[:, i % 2, :, :], ps[:, i % 2, 0:2 * C].rearrange("p (a c) -> p a c", a=2),
                                             ACT.Silu).then_inc(silu_ready, 1)

                def downs(e, par):
                    for i in range(4):
                        act.wait_ge(down_done, 4 * e + (i + 1))
                        nc.scalar.activation(yT[:, par, 2 * i:2 * i + 2, :],
                                             ps[:, 2 + i % 2, 0:2 * C].rearrange("p (a c) -> p a c", a=2),
                                             ACT.Copy).then_inc(yT_ready, 1)

                def take_y(e, par):
                    act.wait_ge(y_turned, e + 1)
                    nc.scalar.activation(y_s[par * CS:(par + 1) * CS, :],
                                         ps[0:CS, 4:6, :].rearrange("p b n -> p (b n)"), ACT.Copy).then_inc(ys_ready, 1)

                def high_parts(pair, j):
                    act.wait_ge(ys_ready, 2 * pair + 2)
                    act.wait_ge(yp_ready, 2 * pair + 2)
                    nc.scalar.activation(hi_s[:], y_s[:], ACT.Copy, scale=gate_s[:, bass.ds(j, 1)]).then_inc(hi_ready, 1)
                    nc.scalar.activation(hi_p[:], y_p[:], ACT.Copy, scale=gate_p[:, bass.ds(j, 1)]).then_inc(hi_ready, 1)

                def pair_body(j, first, last):
                    pair = j + layer * PAIRS
                    e = 2 * pair
                    silus(e, 0)
                    if not first:
                        take_y(e - 1, 1)
                        high_parts(pair - 1, j - 1)
                    downs(e, 0)
                    silus(e + 1, 1)
                    if not first:
                        act.wait_ge(lo_ready, 2 * pair)
                    take_y(e, 0)
                    if not last:
                        turn_in(pair + 1)
                    downs(e + 1, 1)

                turn_in(layer * PAIRS)
                pair_body(0, True, False)
                with act.Fori(1, PAIRS - 1) as j:
                    pair_body(j, False, False)
                pair_body(PAIRS - 1, False, True)
                take_y(2 * PAIRS * (layer + 1) - 1, 1)
                high_parts(PAIRS * (layer + 1) - 1, PAIRS - 1)

        @block.vector
        def _(dve):
            steps = {}

            def step(ins, on):
                steps[on.name] = steps.get(on.name, 0) + 1
                ins.then_inc(on, 1)
                dve.wait_ge(on, steps[on.name])

            nc.vector.memset(minus_half[:], -0.5)
            nc.vector.memset(rb, 1.0).then_inc(rb_set, 1)
            dve.wait_ge(tab_mm, 1)
            nc.vector.tensor_copy(tab, ps[0:NH, 0:TABW // BANK, :].rearrange("p b n -> p (b n)")).then_inc(tab_cp, 1)
            dve.wait_ge(const_in, 16 * 6)

            hn = 0
            gains = 0
            for layer in range(LAYERS):
                def norm_rows(s, dst):
                    nonlocal gains
                    dve.wait_ge(sumsq_ready, NT * (s + 1))
                    nc.vector.tensor_scalar(var[:], sumsq[:], 1.0 / DM, EPS, ALU.mult, ALU.add).then_inc(var_ready, 1)
                    gains += 1
                    dve.wait_ge(gain_in, 16 * gains)
                    dve.wait_ge(rstd_ready, s + 1)
                    for t in range(NT):
                        n = NT * s + t
                        if t >= 2:
                            dve.wait_ge(h_turned, n - 1)
                            if s % 2:
                                dve.wait_ge(h_out[t % 2], 16 * (layer * NT // 2 + t // 2))
                        nc.vector.scalar_tensor_tensor(dst(t), x[:, t, :], rstd[:, t:t + 1], gain[:],
                                                       ALU.mult, ALU.mult).then_inc(h_ready, 1)

                if layer == 0:
                    dve.wait_ge(tab_out, 16)
                norm_rows(2 * layer, lambda t: probs[:, t % 2, 0:DM])

                def norm_heads(kind):
                    nonlocal hn
                    hn += 1
                    raw = (qraw if kind == "q" else kraw)[:, :, :].rearrange("p t c -> p (t c)")
                    w = NT * GW // 2
                    for i in range(2):
                        part = raw[:, i * w:(i + 1) * w]
                        step(nc.vector.tensor_tensor(sq, part, part, ALU.mult), head_sums)
                        step(nc.vector.tensor_reduce(hsum[:, i * w // HD:(i + 1) * w // HD],
                                                     sq.rearrange("p (h n) -> p h n", n=HD), AX.X, ALU.add), head_sums)
                    nc.vector.tensor_scalar(hvar[:], hsum[:], 1.0 / HD, EPS, ALU.mult, ALU.add).then_inc(hvar_ready, 1)
                    dve.wait_ge(hrstd_ready, hn)
                    heads = raw.rearrange("p (h n) -> p h n", n=HD)
                    step(nc.vector.tensor_tensor(heads, heads, hrstd[:].unsqueeze(2).to_broadcast([P, NT * GH, HD]), ALU.mult),
                         head_sums)
                    which = 2 * layer + (0 if kind == "q" else 1)
                    nc.vector.tensor_tensor(heads, heads, head_gain[:, which, :].unsqueeze(1).to_broadcast([P, NT * GH, HD]),
                                            ALU.mult).then_inc(head_normed, 1)

                def take_unit(n):
                    u = unit_rank(layer, n)
                    dve.wait_ge(unit_done, u + 1)
                    nc.vector.tensor_copy(row[:, u % 3, 0:GW], u_bank).then_inc(row_ready, 1)

                for g in range(NG):
                    if layer == 0:
                        for kind in "qk":
                            dve.wait_ge(qkv_taken, NT * (chunk_at(0, kind, g) + 1))
                            norm_heads(kind)
                    else:
                        before = FIRST_OUT[0]
                        if g == 0:
                            dve.wait_ge(qkv_taken, NT * (before + 1))
                            norm_heads("k")
                        dve.wait_ge(qkv_taken, NT * (before + 3 + g))
                        norm_heads("q")
                    n = layer * NG + g
                    dve.wait_ge(bias_in[n % 2], bias_value(n))
                    for n in range(g * NT, (g + 1) * NT):
                        unit = UNITS[layer][n]
                        u = unit_rank(layer, n)
                        dve.wait_ge(scores_done, u + 1)
                        p = unit_view(probs[:, u % 2, :], unit, layer, BAND)
                        nc.vector.scalar_tensor_tensor(p, unit_view(s_bank, unit, layer, BANK), HD ** -0.5,
                                                       bias_view(layer, unit), ALU.mult, ALU.add).then_inc(logits_ready, 1)
                        if u >= 3:
                            dve.wait_ge(*row_out_of(u - 3))
                        dve.wait_ge(logits_ready, u + 1)
                        nc.vector.tensor_reduce(row[:, u % 3, GW:GW + GH], p, AX.X, ALU.max, negate=True).then_inc(negmax_ready, 1)
                        if n > g * NT:
                            take_unit(n - 1)
                    take_unit((g + 1) * NT - 1)

                def mix(t):
                    n = layer * NT + t
                    dve.wait_ge(mix_in_s[t % 2], 16 * (n // 2 + 1))
                    mi = mix_in[t % 2].rearrange("p (g c) -> p g c", g=NG)
                    out4 = mi[:, :, 0:GW].rearrange("p g (h n) -> p g h n", n=HD)
                    neg, sums = mi[:, :, GW:GW + GH], mi[:, :, GW + GH:ROW]
                    by_group = lambda ap: ap[:, 0:NH].rearrange("p (g h) -> p g h", g=NG)
                    if layer == 0:
                        step(nc.vector.tensor_tensor(mix_top[:, 0:GH], neg[:, 0, :], neg[:, 1, :], ALU.min), mix_step)
                        step(nc.vector.tensor_tensor(mix_top[:, 0:GH], mix_top[:, 0:GH], neg[:, 2, :], ALU.min), mix_step)
                        nc.vector.tensor_tensor(by_group(mix_arg), mix_top[:, 0:GH].unsqueeze(1).to_broadcast([P, NG, GH]),
                                                neg, ALU.subtract).then_inc(mix_arg_ready, 1)
                        dve.wait_ge(mix_exp_ready, n + 1)
                        step(nc.vector.tensor_tensor(by_group(mix_w), by_group(mix_exp), sums, ALU.mult), mix_step)
                        step(nc.vector.tensor_reduce(mix_den[:, 0:GH], mix_w[:].rearrange("p (g h) -> p h g", g=NG), AX.X,
                                                     ALU.add), mix_step)
                        step(nc.vector.reciprocal(mix_rec[:, 0:GH], mix_den[:, 0:GH]), mix_step)
                        step(nc.vector.tensor_tensor(by_group(mix_c), by_group(mix_exp),
                                                     mix_rec[:, 0:GH].unsqueeze(1).to_broadcast([P, NG, GH]), ALU.mult), mix_step)
                    else:
                        if t == 0:
                            step(nc.vector.tensor_scalar(sink[:], sink[:], -1.0, None, ALU.mult), mix_step)
                        step(nc.vector.tensor_tensor(by_group(mix_top), neg, by_group(sink), ALU.min), mix_step)
                        step(nc.vector.tensor_tensor(by_group(mix_arg), by_group(mix_top), neg, ALU.subtract), mix_step)
                        nc.vector.tensor_tensor(mix_arg[:, NH:2 * NH], mix_top[:], sink[:], ALU.subtract).then_inc(mix_arg_ready, 1)
                        dve.wait_ge(mix_exp_ready, n + 1)
                        step(nc.vector.tensor_tensor(by_group(mix_w), by_group(mix_exp), sums, ALU.mult), mix_step)
                        step(nc.vector.tensor_tensor(mix_den[:], mix_w[:], mix_exp[:, NH:2 * NH], ALU.add), mix_step)
                        step(nc.vector.reciprocal(mix_rec[:], mix_den[:]), mix_step)
                        step(nc.vector.tensor_tensor(mix_c[:], mix_exp[:, 0:NH], mix_rec[:], ALU.mult), mix_step)
                    if t >= 2:
                        dve.wait_ge(mix_turned, n - 1)
                    nc.vector.tensor_tensor(probs[:, t % 2, 0:MIX].rearrange("p (g h n) -> p g h n", g=NG, n=HD), out4,
                                            by_group(mix_c).unsqueeze(3).to_broadcast([P, NG, GH, HD]),
                                            ALU.mult).then_inc(mixed_ready, 1)

                def add_out(c, t):
                    n = NT * (FIRST_OUT[layer] + c) + t
                    dve.wait_ge(proj_done, n + 1)
                    xs = x[:, t, c * GW:(c + 1) * GW]
                    nc.vector.tensor_tensor(xs, ps[:, 6 + n % 2, 0:GW], xs, ALU.add).then_inc(attn_added, 1)

                for t in range(NT):
                    mix(t)
                    if t >= 2:
                        add_out(0, t - 2)
                add_out(0, NT - 2)
                add_out(0, NT - 1)
                for c in range(1, DM // GW):
                    for t in range(NT):
                        add_out(c, t)

                dve.wait_ge(attn_added, LAST_OUT * (layer + 1))
                norm_rows(2 * layer + 1, lambda t: hrow[:, t % 2, :])
                dve.wait_ge(route_mm, NT * (layer + 1))
                lp = ps[:, 6, 0:NT * NE].rearrange("p (t e) -> p t e", e=NE)
                step(nc.vector.tensor_reduce(lmax[:], lp, AX.X, ALU.max, negate=True), route_step)
                nc.vector.tensor_tensor(lgt[:], lp, lmax[:].unsqueeze(2).to_broadcast([P, NT, NE]), ALU.add).then_inc(rlog_ready, 1)
                dve.wait_ge(rexp_ready, layer + 1)
                step(nc.vector.tensor_reduce(lsum[:], lexp[:], AX.X, ALU.add), route_step)
                step(nc.vector.reciprocal(lrec[:], lsum[:]), route_step)
                nc.vector.tensor_tensor(aff[:], lexp[:], lrec[:].unsqueeze(2).to_broadcast([P, NT, NE]),
                                        ALU.mult).then_inc(aff_ready, 1)
                nc.vector.memset(pk_i[:], 0.0)
                nc.vector.memset(pk_g[:], 0.0)
                step(nc.vector.memset(am[:], -1.0), route_step)
                dve.wait_ge(aff_turned, layer + 1)
                nc.vector.tensor_copy(am[0:NE, :], ps[0:NE, 4, :])
                step(nc.vector.tensor_copy(am[32:32 + NE, 0:SEQ], ps[0:NE, 5, 0:SEQ]), route_step)
                for r in range(CS // 8):
                    best = top[:, 8 * r:8 * r + 8]
                    step(nc.vector.max(best, am[:]), route_step)
                    step(nc.vector.max_index(topi[:, 8 * r:8 * r + 8], best, am[:]), route_step)
                    if r < CS // 8 - 1:
                        step(nc.vector.match_replace(am[:], best, am[:], -1.0), route_step)
                for dst, src in ((pk_i, topi), (pk_g, top)):
                    for n in range(2):
                        nc.vector.tensor_copy(dst[0:NE, n * CS:(n + 1) * CS], src[0:NE, :])
                        ins = nc.vector.tensor_copy(dst[32:32 + NE, n * CP:(n + 1) * CP], src[32:32 + NE, 0:CP])
                ins.then_inc(picks_ready, 1)
                dve.wait_ge(picks_turned, layer + 1)
                for n, (a, b) in enumerate(((slot_s, slot_p), (gate_s, gate_p))):
                    src = ps[:, 4, n * 64:n * 64 + 48]
                    for par in range(2):
                        nc.vector.tensor_copy(a[par * CS:(par + 1) * CS, :], src[par * CS:(par + 1) * CS, par:NE:2])
                        ins = nc.vector.tensor_copy(b[par * CP:(par + 1) * CP, :], src[par * CP:(par + 1) * CP, 32 + par:48:2])
                step(ins, route_step)
                nc.vector.tensor_scalar(take_s[:], slot_s[:], float(SEQ), None, ALU.add)
                nc.vector.tensor_copy(take_p[:], slot_p[:]).then_inc(slots_ready, 1)
                dve.wait_ge(route_in, 32 * (layer + 1))

                def turn_in(pair):
                    dve.wait_ge(xe_turned, pair + 1)
                    nc.vector.tensor_copy(xeT[:, :, :, 0:CS],
                                          ps[:, 4:6, :].rearrange("p b (k e c) -> p (b k) e c", e=2, c=CS)).then_inc(xs_ready, 1)

                def products(e, par):
                    for i in range(4):
                        dve.wait_ge(silu_ready, 4 * e + (i + 1))
                        nc.vector.tensor_tensor(hid[:, par, 2 * i:2 * i + 2, :], sg[:, i % 2, :, :],
                                                ps[:, i % 2, 2 * C:4 * C].rearrange("p (a c) -> p a c", a=2),
                                                ALU.mult).then_inc(hid_ready, 1)

                def take_y(e, par):
                    dve.wait_ge(y_turned, e + 1)
                    nc.vector.tensor_copy(y_p[par * CP:(par + 1) * CP, :],
                                          ps[CS:C, 4:6, :].rearrange("p b n -> p (b n)")).then_inc(yp_ready, 1)

                def low_parts(pair, j):
                    col = bass.ds(j, 1)
                    nc.vector.tensor_scalar(hot_s[:], iota[:], slot_s[:, col], None, ALU.is_equal)
                    nc.vector.tensor_scalar(hot_p[:], iota[0:2 * CP, 0:SEQ], slot_p[:, col], None, ALU.is_equal).then_inc(hot_ready, 1)
                    dve.wait_ge(hi_ready, 2 * pair + 1)
                    nc.vector.scalar_tensor_tensor(lo_s[:], y_s[:], gate_s[:, col], hi_s[:].bitcast(F32),
                                                   ALU.mult, ALU.subtract).then_inc(lo_ready, 1)
                    dve.wait_ge(hi_ready, 2 * pair + 2)
                    nc.vector.scalar_tensor_tensor(lo_p[:], y_p[:], gate_p[:, col], hi_p[:].bitcast(F32),
                                                   ALU.mult, ALU.subtract).then_inc(lo_ready, 1)

                def add_rows(pair):
                    for n in range(ADDS):
                        t, half = (n // 2 + PT_) % NT, n % 2
                        dve.wait_ge(comb_done, ADDS * pair + (n + 1))
                        xs = x[:, t, half * BANK:(half + 1) * BANK]
                        nc.vector.tensor_tensor(xs, ps[:, 6 + n % 2, :], xs, ALU.add).then_inc(moe_added, 1)

                def pair_body(j, first, last):
                    pair = j + layer * PAIRS
                    e = 2 * pair
                    products(e, 0)
                    if not first:
                        take_y(e - 1, 1)
                        low_parts(pair - 1, j - 1)
                        add_rows(pair - 1)
                    products(e + 1, 1)
                    take_y(e, 0)
                    if not last:
                        turn_in(pair + 1)

                turn_in(layer * PAIRS)
                pair_body(0, True, False)
                with dve.Fori(1, PAIRS - 1) as j:
                    pair_body(j, False, False)
                pair_body(PAIRS - 1, False, True)
                take_y(2 * PAIRS * (layer + 1) - 1, 1)
                low_parts(PAIRS * (layer + 1) - 1, PAIRS - 1)
                add_rows(PAIRS * (layer + 1) - 1)

        @block.tensor
        def _(pe):
            pe.wait_ge(tab_in, 32)
            pe.wait_ge(rb_set, 1)
            for b in range(TABW // BANK):
                ins = nc.tensor.matmul(ps[0:NH, b, :], rb, buckets[:, b * BANK:(b + 1) * BANK], start=True, stop=True)
            ins.then_inc(tab_mm, 1)
            pe.wait_ge(const_in, 16 * 6)
            pe.wait_ge(tab_cp, 1)

            turned = 0
            lots = 0
            normed = 0
            for layer in range(LAYERS):
                def turn_rows(s, src, then=None):
                    for t in range(NT):
                        n = NT * s + t
                        pe.wait_ge(h_ready, n + 1)
                        if t >= 2:
                            pe.wait_ge(hT_ready, n - 1)
                        for k in range(KM):
                            ins = nc.tensor.transpose(ps[:, 2 * (t % 2) + k // 4, (k % 4) * P:(k % 4 + 1) * P],
                                                      src(t)[:, k * P:(k + 1) * P], ident[:])
                        ins.then_inc(h_turned, 1)
                        if then is not None and t >= 1:
                            then(t - 1)
                    if then is not None:
                        then(NT - 1)

                turn_rows(2 * layer, lambda t: probs[:, t % 2, 0:DM])
                pe.wait_ge(hT_ready, NT * (2 * layer + 1))

                def project(chunk, tiles=range(NT)):
                    l, kind, g, _ = CHUNKS[chunk]
                    pe.wait_ge(w_in[chunk % 2], 16 * (chunk // 2 + 1))
                    units_before = layer * NU + (0 if g in (None, 0) else g * NT)
                    if units_before:
                        pe.wait_ge(row_ready, units_before)
                    for t in tiles:
                        n = chunk * NT + t
                        if n >= 2:
                            c = (n - 2) // NT
                            outs_before = sum(1 for i in range(c) if CHUNKS[i][1] == "o")
                            if CHUNKS[c][1] == "o":
                                pe.wait_ge(attn_added, outs_before * NT + (n - 2) % NT + 1)
                            else:
                                pe.wait_ge(qkv_taken, (c - outs_before) * NT + (n - 2) % NT + 1)
                        if kind == "o":
                            pe.wait_ge(mixT_ready, layer * NT + t + 1)
                        for k in range(KX if kind == "o" else KM):
                            cols = hT[:, k, t * P:(t + 1) * P] if kind == "o" else tile_rows(hT[:, k, :], l, g, t)
                            ins = nc.tensor.matmul(ps[:, 6 + n % 2, 0:GW], cols, wbuf[:, chunk % 2, k, :],
                                                   start=(k == 0), stop=(k == (KX if kind == "o" else KM) - 1))
                        ins.then_inc(proj_done, 1)

                def turn_heads(buf):
                    nonlocal turned, normed
                    normed += 1
                    pe.wait_ge(head_normed, normed)
                    for b in range(NT // 2):
                        if turned >= 2:
                            pe.wait_ge(qk_taken, turned - 1)
                        for i in range(4):
                            t, a = 2 * b + i // 2, i % 2
                            ins = nc.tensor.transpose(ps[:, 4 + turned % 2, i * P:(i + 1) * P],
                                                      buf[:, t, a * P:(a + 1) * P], ident[:])
                        ins.then_inc(qk_turned, 1)
                        turned += 1

                def scores(n):
                    unit = g, t, first, count = UNITS[layer][n]
                    u = unit_rank(layer, n)
                    if u >= 1:
                        pe.wait_ge(logits_ready, u)
                    for h in range(GH):
                        half = slice((h % 2) * HD, (h % 2 + 1) * HD)
                        kv = h // 2 if layer == 0 else (g * GH + h) // (NH // NKV)
                        for k in range(first, first + count):
                            ins = nc.tensor.matmul(block_view(s_bank, unit, layer, BANK, h, k), qT[half, h // 2, t * P:(t + 1) * P],
                                                   kT[half, kv, k * P:(k + 1) * P], start=True, stop=True)
                    ins.then_inc(scores_done, 1)

                def outputs(n):
                    nonlocal lots
                    unit = g, t, first, count = UNITS[layer][n]
                    u = unit_rank(layer, n)
                    batches = batches_of(layer, unit)
                    pe.wait_ge(probs_ready, u + 1)

                    def turn(i):
                        if lots + i >= 2:
                            pe.wait_ge(probsT_ready, lots + i - 1)
                        for m, (h, k) in enumerate(batches[i]):
                            ins = nc.tensor.transpose(ps[:, 4 + (lots + i) % 2, m * P:(m + 1) * P],
                                                      block_view(probs[:, u % 2, :], unit, layer, BAND, h, k), ident[:])
                        ins.then_inc(probs_turned, 1)

                    def times_v(i):
                        pe.wait_ge(probsT_ready, lots + i + 1)
                        if i == 0 and u >= 1:
                            pe.wait_ge(row_ready, u)
                        for m, (h, k) in enumerate(batches[i]):
                            kv = h if layer == 0 else (g * GH + h) // (NH // NKV)
                            heads = [b for b, (hh, _) in enumerate(batches[i]) if hh == h]
                            ins = nc.tensor.matmul(u_bank[:, h * HD:(h + 1) * HD], probsT[:, (lots + i) % 2, m * P:(m + 1) * P],
                                                   v[:, k, kv * HD:(kv + 1) * HD], start=(m == heads[0]), stop=(m == heads[-1]))
                        return ins

                    turn(0)
                    for i in range(len(batches)):
                        if i + 1 < len(batches):
                            turn(i + 1)
                        ins = times_v(i)
                    ins.then_inc(unit_done, 1)
                    lots += len(batches)

                for g in range(NG):
                    if layer == 0:
                        for kind in "qkv":
                            project(chunk_at(0, kind, g))
                        if lots:
                            pe.wait_ge(probsT_ready, lots)
                        turn_heads(qraw)
                        turn_heads(kraw)
                    else:
                        if g == 0:
                            project(chunk_at(1, "k", 0))
                            project(chunk_at(1, "v", 0))
                        project(chunk_at(1, "q", g))
                        pe.wait_ge(probsT_ready, lots)
                        if g == 0:
                            turn_heads(kraw)
                        turn_heads(qraw)
                    pe.wait_ge(qk_taken, turned)
                    scores(g * NT)
                    for n in range(g * NT, (g + 1) * NT):
                        if n + 1 < (g + 1) * NT:
                            scores(n + 1)
                        outputs(n)

                pe.wait_ge(row_ready, (layer + 1) * NU)

                def turn_mix(t):
                    n = layer * NT + t
                    pe.wait_ge(mixed_ready, n + 1)
                    if t >= 2:
                        pe.wait_ge(mixT_ready, n - 1)
                    for k in range(KX):
                        ins = nc.tensor.transpose(ps[:, 2 * (t % 2) + k // 4, (k % 4) * P:(k % 4 + 1) * P],
                                                  probs[:, t % 2, k * P:(k + 1) * P], ident[:])
                    ins.then_inc(mix_turned, 1)

                turn_mix(0)
                for t in range(NT):
                    if t + 1 < NT:
                        turn_mix(t + 1)
                    project(FIRST_OUT[layer], [t])
                for c in range(1, DM // GW):
                    project(FIRST_OUT[layer] + c)

                def route(t):
                    n = layer * NT + t
                    pe.wait_ge(hT_ready, NT * (2 * layer + 1) + t + 1)
                    for k in range(KM):
                        ins = nc.tensor.matmul(ps[:, 6, t * NE:(t + 1) * NE], hTr[:, t % 2, k, :], router[:, k, :],
                                               start=(k == 0), stop=(k == KM - 1))
                    ins.then_inc(route_mm, 1)

                pe.wait_ge(route_in, 32 * (layer + 1))
                turn_rows(2 * layer + 1, lambda t: hrow[:, t % 2, :], route)
                pe.wait_ge(aff_ready, layer + 1)
                for t in range(NT):
                    bank, at = (5, t) if t < PT_ else (4, t - PT_)
                    ins = nc.tensor.transpose(ps[0:NE, bank, at * P:(at + 1) * P], aff[:, t, :], ident[:])
                ins.then_inc(aff_turned, 1)
                pe.wait_ge(picks_ready, layer + 1)
                nc.tensor.transpose(ps[:, 4, 0:48], pk_i[:], ident[0:48, 0:48])
                nc.tensor.transpose(ps[:, 4, 64:112], pk_g[:], ident[0:48, 0:48]).then_inc(picks_turned, 1)
                pe.wait_ge(slots_ready, layer + 1)

                def turn_in(pair):
                    pe.wait_ge(xg_s_in, 16 * pair + 16)
                    pe.wait_ge(xg_p_in, 16 * pair + 16)
                    for k in range(KM):
                        nc.tensor.transpose(ps[:, 4 + k // 4, (k % 4) * P:(k % 4 + 1) * P], xg_s[:, k * P:(k + 1) * P], ident[:])
                    for k in range(KM):
                        ins = nc.tensor.transpose(ps[:, 6, k * 2 * CP:(k + 1) * 2 * CP], xg_p[:, k * P:(k + 1) * P],
                                                  ident[0:2 * CP, 0:2 * CP])
                    ins.then_inc(xe_turned, 1)

                def piece(e, i):
                    pe.wait_ge(piece_in[i], 16 * e + 16)

                def gate_up(e, par, i, skip_wait=False):
                    if not skip_wait:
                        pe.wait_ge(hid_ready, 4 * e + (i - 1))
                    for side in range(2):
                        piece(e, 2 * i + side)
                        for a in range(2):
                            at = (2 * side + a) * C
                            for k in range(KM):
                                ins = nc.tensor.matmul(ps[:, i % 2, at:at + C], ring_gu[:, 2 * i + side, k, a * P:(a + 1) * P],
                                                       xeT[:, k, par, :], start=(k == 0), stop=(k == KM - 1))
                    ins.then_inc(gu_done, 1)

                def down(e, par, i, skip_wait=False):
                    if not skip_wait:
                        pe.wait_ge(yT_ready, 4 * e + (i - 1))
                    piece(e, 8 + i)
                    for a in range(2):
                        for k in range(KM):
                            ins = nc.tensor.matmul(ps[:, 2 + i % 2, a * C:(a + 1) * C], ring_d[:, i, k, a * P:(a + 1) * P],
                                                   hid[:, par, k, :], start=(k == 0), stop=(k == KM - 1))
                    ins.then_inc(down_done, 1)

                def turn_y(e, par):
                    pe.wait_ge(yT_ready, 4 * e + 4)
                    for k in range(KM):
                        ins = nc.tensor.transpose(ps[0:C, 4 + k // 4, (k % 4) * P:(k % 4 + 1) * P], yT[:, par, k, :], ident[:])
                    ins.then_inc(y_turned, 1)

                def combine(pair):
                    pe.wait_ge(hot_ready, pair + 1)
                    pe.wait_ge(hi_ready, 2 * pair + 2)
                    pe.wait_ge(lo_ready, 2 * pair + 2)
                    for n in range(ADDS):
                        t, half = (n // 2 + PT_) % NT, n % 2
                        if n >= 2:
                            pe.wait_ge(moe_added, ADDS * pair + (n - 1))
                        cols = slice(half * BANK, (half + 1) * BANK)
                        hot, hi, lo = ((hot_p[:, t * P:(t + 1) * P], hi_p, lo_p) if t < PT_
                                       else (hot_s[:, (t - PT_) * P:(t - PT_ + 1) * P], hi_s, lo_s))
                        nc.tensor.matmul(ps[:, 6 + n % 2, :], hot, hi[:, cols], start=True, stop=False)
                        nc.tensor.matmul(ps[:, 6 + n % 2, :], hot, lo[:, cols], start=False, stop=True).then_inc(comb_done, 1)

                def pair_body(j, first, last):
                    pair = j + layer * PAIRS
                    e = 2 * pair
                    pe.wait_ge(xs_ready, pair + 1)
                    pe.wait_ge(xp_ready, pair + 1)
                    for i in range(4):
                        gate_up(e, 0, i, skip_wait=first and i < 2)
                        if i == 0 and not first:
                            turn_y(e - 1, 1)
                    if not first:
                        combine(pair - 1)
                    pe.wait_ge(hid_ready, 4 * e + 4)
                    for i in range(4):
                        down(e, 0, i, skip_wait=first and i < 2)
                    for i in range(4):
                        gate_up(e + 1, 1, i)
                        if i == 1:
                            if not first:
                                pe.wait_ge(ys_ready, e)
                                pe.wait_ge(yp_ready, e)
                            turn_y(e, 0)
                    if not last:
                        pe.wait_ge(ys_ready, e + 1)
                        pe.wait_ge(yp_ready, e + 1)
                        if not first:
                            pe.wait_ge(moe_added, ADDS * pair)
                        turn_in(pair + 1)
                    pe.wait_ge(hid_ready, 4 * e + 8)
                    for i in range(4):
                        down(e + 1, 1, i)

                turn_in(layer * PAIRS)
                pair_body(0, True, False)
                with pe.Fori(1, PAIRS - 1) as j:
                    pair_body(j, False, False)
                pair_body(PAIRS - 1, False, True)
                pe.wait_ge(ys_ready, NE * (layer + 1) - 1)
                pe.wait_ge(yp_ready, NE * (layer + 1) - 1)
                turn_y(2 * PAIRS * (layer + 1) - 1, 1)
                combine(PAIRS * (layer + 1) - 1)
                pe.wait_ge(moe_added, ADDS * PAIRS * (layer + 1))


_OUTS = [((1, SEQ, DM), "float32"), ((1, DEC_SEQ, DM), "float32")]


def kernel(**inputs):
    import concourse.bacc as bacc
    from concourse.bass_utils import run_bass_kernel_spmd

    nc = bacc.Bacc("TRN2", target_bir_lowering=False, num_devices=1)
    arrays, tensors = {}, {}
    for name, a in {**inputs, **shape_constants()}.items():
        a = np.ascontiguousarray(a)
        arrays[f"in_{name}"] = a
        tensors[name] = nc.dram_tensor(f"in_{name}", a.shape, mybir.dt.from_np(a.dtype), kind="ExternalInput").ap()
    outs = [nc.dram_tensor(f"out_{i}", shape, mybir.dt.from_np(np.dtype(dtype)), kind="ExternalOutput").ap()
            for i, (shape, dtype) in enumerate(_OUTS)]
    build_trunk(nc, tensors, outs)
    r = run_bass_kernel_spmd(nc, [arrays], core_ids=[0])
    return tuple(r.results[0][f"out_{i}"] for i in range(len(_OUTS)))
```

```python
import math
from contextlib import ExitStack

import numpy as np

import concourse.bass as bass
from concourse import mybir

F32 = mybir.dt.float32
F32R = mybir.dt.float32r
I32 = mybir.dt.int32
U32 = mybir.dt.uint32
ACT = mybir.ActivationFunctionType
ALU = mybir.AluOpType
AX = mybir.AxisListType

P = 128
BANK = 512
DM = 1024
KM = DM // P
SEQ, DEC_SEQ = 256, 512
TOK = SEQ + DEC_SEQ
NT = TOK // P
PT_ = SEQ // P
LAYERS = 2
HD, NH, NKV = 64, 12, 4
MIX = NH * HD
KX = MIX // P
KVW = NKV * HD
GH = 4
GW = GH * HD
NG = NH // GH
DILATIONS = (1, 4, 16)
HALF_A, HALF_B = 64, 128
BUCKETS, REL_MAX = 32, 1024
EPS = 1e-6
MASKED = -1e30
BAND = 3 * P
ROW = GW + 2 * GH
NE, DE = 16, 1024
CS, CP = 2 * DEC_SEQ // NE, 2 * SEQ // NE
C = CS + CP
PAIRS = NE // 2
PIECES = 12
RAW, SPLIT = 6, 4
AHEAD = 2
PW = DE // 4
COMB = 6
TAB = {(0, 0): (0, 2 * BAND - 2 * P, HALF_A, 1, 1), (1, 0): (1536, 2 * BAND - 2 * P, HALF_B, 1, 1)}
for _g in (1, 2):
    for _r, _tiles in enumerate((PT_, NT - PT_)):
        TAB[0, _g, _r] = (2 * _g * 256 + 256 * _r, 2 * P, HALF_A, _tiles, DILATIONS[_g] // _tiles)
TABW = 2048
CHUNKS = ([(0, kind, g, n * MIX + g * GW) for g in range(NG) for n, kind in enumerate("qkv")]
          + [(0, "o", None, n * GW) for n in range(DM // GW)]
          + [(1, "k", 0, MIX), (1, "v", 0, MIX + KVW)] + [(1, "q", g, g * GW) for g in range(NG)]
          + [(1, "o", None, n * GW) for n in range(DM // GW)])


def t5_bucket(rel):
    half = BUCKETS // 2
    max_exact = half // 2
    n = -rel
    base = np.where(n < 0, half, 0)
    n = np.abs(n)
    large = max_exact + (np.log(np.maximum(n, 1) / max_exact)
                         / math.log(REL_MAX / max_exact) * (half - max_exact)).astype(np.int32)
    return (base + np.where(n < max_exact, n, np.minimum(large, half - 1))).astype(np.int32)


def shape_constants():
    buckets = np.zeros((BUCKETS + 1, TABW), np.float32)
    for start, width, half, stride, every in TAB.values():
        for i in range(width):
            rel = i - (BAND - P - 1 if width > 2 * P else P - 1)
            if rel % every == 0 and abs(rel) // every <= half:
                buckets[t5_bucket(np.array(rel * stride)), start + i] = 1.0
            else:
                buckets[BUCKETS, start + i] = MASKED
    return {"c_buckets": buckets, "c_ident": np.eye(P, dtype=np.float32),
            "c_iota": np.tile(np.arange(DEC_SEQ, dtype=np.float32), (P, 1))}


def units_of(layer):
    out = []
    for g in range(NG):
        for t in range(NT):
            lo, hi = (0, PT_) if t < PT_ else (PT_, NT)
            if layer == 0 and g > 0:
                out.append((g, t, t, 1))
            else:
                first = max(t - 1, lo)
                out.append((g, t, first, min(t + 2, hi) - first))
    return out


def batches_of(layer, unit):
    g, t, first, n = unit
    if layer == 0 and g > 0:
        return [[(h, t) for h in range(GH)]]
    return [[(h, k) for k in range(first, first + n)] for h in range(GH)]


def tile_rows(ap, layer, g, t):
    base, tiles, n = (0, PT_, t) if t < PT_ else (PT_ * P, NT - PT_, t - PT_)
    if layer == 0 and g > 0:
        return ap[:, base:base + tiles * P].rearrange("p (m r) -> p r m", r=tiles)[:, n, :]
    return ap[:, t * P:(t + 1) * P]


def build_trunk(nc, d, outs):
    ctx = ExitStack()
    with ctx:
        def sb(name, shape, dt=F32, scope=ctx):
            return scope.enter_context(nc.sbuf_tensor(name, shape, dt))

        def sem(name):
            return ctx.enter_context(nc.semaphore(name))

        tab_d = nc.dram_tensor("bias_rows", [NH, TABW], F32)
        tab_ap = tab_d.ap()
        unit_d = nc.dram_tensor("unit_rows", [NG, TOK, ROW], F32).ap()
        h_d = nc.dram_tensor("ffn_rows", [TOK, DM], F32).ap()

        x = sb("x", [P, NT, DM])
        gain = sb("gain", [P, DM])
        ident = sb("ident", [P, P])
        head_gain = sb("head_gain", [P, 2 * LAYERS, HD])
        sink = sb("sink", [P, NH])
        minus_half = sb("minus_half", [P, NT * GH])
        sumsq = sb("sumsq", [P, NT])
        var = sb("var", [P, NT])
        rstd = sb("rstd", [P, NT])
        hsum = sb("hsum", [P, NT * GH])
        hvar = sb("hvar", [P, NT * GH])
        hrstd = sb("hrstd", [P, NT * GH])
        mix_top = sb("mix_top", [P, NH])
        mix_arg = sb("mix_arg", [P, 2 * NH])
        mix_exp = sb("mix_exp", [P, 2 * NH])
        mix_w = sb("mix_w", [P, NH])
        mix_den = sb("mix_den", [P, NH])
        mix_rec = sb("mix_rec", [P, NH])
        mix_c = sb("mix_c", [P, NH])
        lmax = sb("lmax", [P, NT])
        lgt = sb("lgt", [P, NT, NE])
        lexp = sb("lexp", [P, NT, NE])
        lsum = sb("lsum", [P, NT])
        lrec = sb("lrec", [P, NT])
        aff = sb("aff", [P, NT, NE])
        slot_s = sb("slot_s", [P, PAIRS])
        slot_p = sb("slot_p", [2 * CP, PAIRS])
        gate_s = sb("gate_s", [P, PAIRS])
        gate_p = sb("gate_p", [2 * CP, PAIRS])
        take = sb("take", [C, NE], I32)

        with ExitStack() as at:
            hT = sb("hT", [P, KM, TOK], scope=at)
            wbuf = sb("wbuf", [P, 2, KM, GW], scope=at)
            qraw = sb("qraw", [P, NT, GW], scope=at)
            kraw = sb("kraw", [P, NT, GW], scope=at)
            v = sb("v", [P, NT, GW], scope=at)
            qT = sb("qT", [P, 2, TOK], scope=at)
            kT = sb("kT", [P, NKV, TOK], scope=at)
            probs = sb("probs", [P, 2, GH * BAND], scope=at)
            probsT = sb("probsT", [P, 2, BANK], scope=at)
            row = sb("row", [P, 3, ROW], scope=at)
            bias = sb("bias", [P, 2, GH * BAND], scope=at)
            sq = probsT[:, :, :].rearrange("p a b -> p (a b)")[:, 0:NT * GW // 2]
            buckets = bias[0:BUCKETS + 1, :, :].rearrange("p a b -> p (a b)")[:, 0:TABW]
            rb = row[0:BUCKETS + 1, 0, 0:NH]
            tab = probs[0:NH, :, :].rearrange("p a b -> p (a b)")[:, 0:TABW]
            mix_in = [qraw[:, :, :].rearrange("p t c -> p (t c)")[:, 0:NG * ROW],
                      kraw[:, :, :].rearrange("p t c -> p (t c)")[:, 0:NG * ROW]]

        with ExitStack() as mo:
            ring = sb("ring", [P, RAW, KM, PW], scope=mo)
            w_hi = sb("w_hi", [P, SPLIT, KM, PW], F32R, scope=mo)
            w_lo = sb("w_lo", [P, SPLIT, KM, PW], F32R, scope=mo)
            router = sb("router", [P, KM, NE], scope=mo)
            iota = sb("iota", [P, DEC_SEQ], scope=mo)
            xg = sb("xg", [C, 2, DM], scope=mo)
            xe_hi = sb("xe_hi", [P, 2, KM, C], F32R, scope=mo)
            xe_lo = sb("xe_lo", [P, 2, KM, C], F32R, scope=mo)
            with ExitStack() as ro:
                hrow = sb("hrow", [P, 2, DM], scope=ro)
                hTr = sb("hTr", [P, 2, KM, P], scope=ro)
                am = sb("am", [48, DEC_SEQ], scope=ro)
                top = sb("top", [48, CS], scope=ro)
                topi = sb("topi", [48, CS], U32, scope=ro)
                pk_i = sb("pk_i", [48, P], scope=ro)
                pk_g = sb("pk_g", [48, P], scope=ro)
            sg = sb("sg", [C, 2, PW], scope=mo)
            hid = sb("hid", [C, DE], scope=mo)
            hid_hi = sb("hid_hi", [P, KM, C], F32R, scope=mo)
            hid_lo = sb("hid_lo", [P, KM, C], F32R, scope=mo)
            y_s = sb("y_s", [P, DM], scope=mo)
            y_p = sb("y_p", [2 * CP, DM], scope=mo)
            hi_s = sb("hi_s", [P, DM], F32R, scope=mo)
            hi_p = sb("hi_p", [2 * CP, DM], F32R, scope=mo)
            lo_s = sb("lo_s", [P, DM], F32R, scope=mo)
            lo_p = sb("lo_p", [2 * CP, DM], F32R, scope=mo)
            hot_s = sb("hot_s", [P, DEC_SEQ], F32R, scope=mo)
            hot_p = sb("hot_p", [2 * CP, SEQ], F32R, scope=mo)

        ps = ctx.enter_context(nc.psum_tensor("ps", [P, 8, BANK], F32))

        const_in = sem("const_in")
        tab_in = sem("tab_in")
        rb_set = sem("rb_set")
        tab_mm = sem("tab_mm")
        tab_cp = sem("tab_cp")
        tab_out = sem("tab_out")
        x_in = sem("x_in")
        gain_in = sem("gain_in")
        sumsq_ready = sem("sumsq_ready")
        var_ready = sem("var_ready")
        rstd_ready = sem("rstd_ready")
        h_ready = sem("h_ready")
        h_turned = sem("h_turned")
        hT_ready = sem("hT_ready")
        w_in = [sem(f"w_in{i}") for i in range(2)]
        proj_done = sem("proj_done")
        qkv_taken = sem("qkv_taken")
        head_sums = sem("head_sums")
        hvar_ready = sem("hvar_ready")
        hrstd_ready = sem("hrstd_ready")
        head_normed = sem("head_normed")
        qk_turned = sem("qk_turned")
        qk_taken = sem("qk_taken")
        bias_in = [sem(f"bias_in{i}") for i in range(2)]
        scores_done = sem("scores_done")
        logits_ready = sem("logits_ready")
        negmax_ready = sem("negmax_ready")
        probs_ready = sem("probs_ready")
        probs_turned = sem("probs_turned")
        probsT_ready = sem("probsT_ready")
        unit_done = sem("unit_done")
        row_ready = sem("row_ready")
        row_out = [sem(f"row_out{i}") for i in range(3)]
        mix_in_s = [sem(f"mix_in_s{i}") for i in range(2)]
        mix_step = sem("mix_step")
        mix_arg_ready = sem("mix_arg_ready")
        mix_exp_ready = sem("mix_exp_ready")
        mixed_ready = sem("mixed_ready")
        mix_turned = sem("mix_turned")
        mixT_ready = sem("mixT_ready")
        attn_added = sem("attn_added")
        h_out = [sem(f"h_out{i}") for i in range(2)]
        route_in = sem("route_in")
        route_mm = sem("route_mm")
        route_step = sem("route_step")
        rlog_ready = sem("rlog_ready")
        rexp_ready = sem("rexp_ready")
        aff_ready = sem("aff_ready")
        aff_turned = sem("aff_turned")
        picks_ready = sem("picks_ready")
        picks_turned = sem("picks_turned")
        slots_ready = sem("slots_ready")
        piece_in = [sem(f"piece_in{i}") for i in range(RAW)]
        hi_split = sem("hi_split")
        lo_split = sem("lo_split")
        piece_used = sem("piece_used")
        xg_in = [sem(f"xg_in{i}") for i in range(2)]
        xe_turned = sem("xe_turned")
        xe_hi_ready = sem("xe_hi_ready")
        xe_lo_ready = sem("xe_lo_ready")
        silu_ready = sem("silu_ready")
        hid_ready = sem("hid_ready")
        hid_turned = sem("hid_turned")
        hid_hi_ready = sem("hid_hi_ready")
        hid_lo_ready = sem("hid_lo_ready")
        y_ready = sem("y_ready")
        hi_ready = sem("hi_ready")
        lo_ready = sem("lo_ready")
        hot_ready = sem("hot_ready")
        comb_done = sem("comb_done")
        moe_added = sem("moe_added")
        y_out = sem("y_out")

        UNITS = [units_of(0), units_of(1)]
        NU = NG * NT
        UNIT_FOR_GROUP = NT
        LAST_OUT = NT * DM // GW
        ADDS = 2 * NT
        LAST_BANKS = (6, 7, 0, 1, 4, 5)

        def w_dram(chunk):
            layer, kind, g, col = CHUNKS[chunk]
            w = d[("a" if layer == 0 else "b") + ("_w_out" if kind == "o" else "_w_in")][0]
            return w[:, col:col + GW].rearrange("(k p) n -> p k n", p=P), (KX if kind == "o" else KM)

        def chunk_at(layer, kind, g):
            return CHUNKS.index(next(c for c in CHUNKS if c[:3] == (layer, kind, g)))

        FIRST_CHUNK = [0, chunk_at(1, "k", 0)]
        FIRST_OUT = [chunk_at(0, "o", None), chunk_at(1, "o", None)]

        def unit_rows(layer, g, t):
            base, tiles, n = (0, PT_, t) if t < PT_ else (PT_ * P, NT - PT_, t - PT_)
            if layer == 0 and g > 0:
                return unit_d[g, base:base + tiles * P, :].rearrange("(m r) c -> r m c", r=tiles)[tiles - 1 - n]
            at = base + (tiles - 1 - n) * P
            return unit_d[g, at:at + P, :]

        def stream(layer, j, q):
            at = AHEAD + q
            return layer * NE * PIECES + j * (2 * PIECES) + at, at % RAW, at % SPLIT

        def piece_of(q, last=False):
            if q < 0:
                return 0, AHEAD + q
            par, c = q // PIECES, q % PIECES
            if c < 6:
                return par, AHEAD + c
            if last and par == 1:
                return par, c + 2
            return (par + 1, c - 6) if c < 8 else (par, c)

        def mirror(t):
            return PT_ - 1 - t if t < PT_ else PT_ + NT - 1 - t

        def unit_rank(layer, n):
            return layer * NU + n

        def row_out_of(u):
            return row_out[u % 3], 16 * (u // 3 + 1)

        BIAS_LOADS = [1, 2, 2, 1, 1, 1]

        def bias_value(n):
            return 16 * sum(BIAS_LOADS[n % 2:n + 1:2])

        def bias_view(layer, unit):
            g, t, first, n = unit
            buf = bias[:, (layer * NG + g) % 2, :]
            if layer == 0 and g > 0:
                kind = 0 if t < PT_ else 1
                return buf[:, kind * GH * P:(kind + 1) * GH * P].rearrange("p (h c) -> p h c", h=GH)
            at = (first - (t - 1)) * P
            return buf.rearrange("p (h c) -> p h c", h=GH)[:, :, at:at + n * P]

        def unit_view(buf, unit, layer, pitch):
            g, t, first, n = unit
            at = 0 if layer == 0 and g > 0 else (first - (t - 1)) * P
            return buf[:, 0:GH * pitch].rearrange("p (h c) -> p h c", h=GH)[:, :, at:at + n * P]

        def block_view(buf, unit, layer, pitch, h, k):
            g, t, first, n = unit
            at = h * pitch + (0 if layer == 0 and g > 0 else (k - (t - 1)) * P)
            return buf[:, at:at + P]

        s_bank = ps[:, 0:GH, :].rearrange("p b n -> p (b n)")
        u_bank = ps[:, 7, GW:2 * GW]

        block = ctx.enter_context(nc.Block())

        @block.sync
        def _(sp):
            def load_chunk(chunk):
                if chunk >= 2:
                    sp.wait_ge(proj_done, NT * (chunk - 1))
                if chunk == FIRST_CHUNK[1] or chunk == FIRST_CHUNK[1] + 1:
                    sp.wait_ge(moe_added, ADDS * PAIRS)
                src, k = w_dram(chunk)
                sp.dma_start(wbuf[:, chunk % 2, 0:k, :], src).then_inc(w_in[chunk % 2], 16)

            def load_bias(layer, g):
                n = layer * NG + g
                if n >= 2:
                    sp.wait_ge(logits_ready, NT * (n - 1))
                if layer and g == 0:
                    sp.wait_ge(moe_added, ADDS * PAIRS)
                buf = bias[:, n % 2, :]
                for r in range(BIAS_LOADS[n]):
                    if BIAS_LOADS[n] == 1:
                        start, cols = TAB[layer, 0][0], BAND
                    else:
                        start, cols = TAB[layer, g, r][0], P
                    dst = buf[:, r * GH * cols:(r + 1) * GH * cols].rearrange("p (h c) -> p h c", h=GH)
                    src = bass.AP(tab_ap.tensor, g * GH * TABW + start, [[1, P], [TABW, GH], [1, cols]])
                    sp.dma_start(dst, src).then_inc(bias_in[n % 2], 16)

            def load_piece(layer, e, q, first=False, last=False, base=0):
                at, slot, _ = stream(layer, 0, q)
                if not first or AHEAD + q >= RAW:
                    sp.wait_ge(lo_split, e * PIECES + (base * PIECES + at + 1 - RAW))
                par, i = piece_of(q, last)
                w, col = ((d["moe_w_down"], (i - 8) * PW) if i >= 8
                          else (d["moe_w_gate" if i % 2 == 0 else "moe_w_up"], (i // 2) * PW))
                w = w[layer, base + par:].rearrange("e (k p) n -> e p k n", p=P)
                src = w[bass.ds(e, 1), :, :, col:col + PW].rearrange("o p k n -> p (o k) n")
                sp.dma_start(ring[:, slot], src).then_inc(piece_in[slot], 16)

            sp.dma_start(x[:, 0, :], d["x_prompt"][0, 0:P, :]).then_inc(x_in, 16)
            for t in range(1, NT):
                src = (d["x_prompt"][0, t * P:(t + 1) * P, :] if t < PT_
                       else d["x_sample"][0, (t - PT_) * P:(t - PT_ + 1) * P, :])
                sp.dma_start(x[:, t, :], src).then_inc(x_in, 16)
            sp.dma_start(gain[:], bass.AP(d["norm_mix"].tensor, 0, [[0, P], [1, DM]])).then_inc(gain_in, 16)
            sp.dma_start(ident[:], d["c_ident"]).then_inc(const_in, 16)
            for n, name in enumerate(("a_q_gain", "a_k_gain", "b_q_gain", "b_k_gain")):
                sp.dma_start(head_gain[:, n, :], bass.AP(d[name].tensor, 0, [[0, P], [1, HD]])).then_inc(const_in, 16)
            sp.dma_start(sink[:], bass.AP(d["b_sink"].tensor, 0, [[0, P], [1, NH]])).then_inc(const_in, 16)
            sp.dma_start(buckets, d["c_buckets"]).then_inc(tab_in, 16)
            sp.wait_ge(rb_set, 1)
            sp.dma_start(rb[0:BUCKETS], d["rel_bias"]).then_inc(tab_in, 16)
            load_chunk(0)
            load_chunk(1)
            sp.wait_ge(tab_cp, 1)
            sp.dma_start(tab_ap, tab).then_inc(tab_out, 16)
            sp.wait_ge(tab_out, 16)

            for layer in range(LAYERS):
                load_bias(layer, 0)
                load_bias(layer, 1)
                first = FIRST_CHUNK[layer]
                chunk = first
                if layer == 0:
                    chunk = 2
                else:
                    load_chunk(first)
                    load_chunk(first + 1)
                    sp.dma_start(gain[:], bass.AP(d["norm_mix"].tensor, DM, [[0, P], [1, DM]])).then_inc(gain_in, 16)
                    chunk = first + 2
                units = UNITS[layer]
                for g in range(NG):
                    while chunk < FIRST_OUT[layer] and chunk - 2 <= chunk_at(layer, "q", g) + (2 if layer == 0 else 0):
                        load_chunk(chunk)
                        chunk += 1
                    if g == 2:
                        load_bias(layer, 2)
                    for n in range(g * NT, (g + 1) * NT):
                        u = unit_rank(layer, n)
                        sp.wait_ge(row_ready, u + 1)
                        sp.dma_start(unit_rows(layer, units[n][0], units[n][1]),
                                     row[:, u % 3, :]).then_inc(row_out_of(u)[0], 16)
                while chunk < FIRST_OUT[layer] + 2:
                    load_chunk(chunk)
                    chunk += 1
                last = unit_rank(layer, NU - 1)
                for u in range(last - 2, last + 1):
                    sp.wait_ge(*row_out_of(u))
                for t in range(NT):
                    if t >= 2:
                        sp.wait_ge(mixed_ready, layer * NT + t - 1)
                    sp.dma_start(mix_in[t % 2].rearrange("p (g c) -> p g c", g=NG),
                                 unit_d[:, mirror(t) * P:(mirror(t) + 1) * P, :].rearrange("g p c -> p g c")).then_inc(mix_in_s[t % 2], 16)
                sp.wait_ge(h_ready, NT * (2 * layer + 1))
                sp.dma_start(gain[:], bass.AP(d["norm_ffn"].tensor, layer * DM, [[0, P], [1, DM]])).then_inc(gain_in, 16)
                for c in range(chunk, FIRST_OUT[layer] + DM // GW):
                    load_chunk(c)

                sp.wait_ge(attn_added, LAST_OUT * (layer + 1))
                sp.dma_start(router[:], d["moe_router"][layer].rearrange("(k p) e -> p k e", p=P)).then_inc(route_in, 16)
                sp.dma_start(iota[:], d["c_iota"]).then_inc(route_in, 16)
                for q in range(-AHEAD, RAW - AHEAD):
                    load_piece(layer, 0, q, first=True)
                for t in range(NT):
                    sp.wait_ge(h_ready, NT * (2 * layer + 1) + t + 1)
                    sp.dma_start(h_d[t * P:(t + 1) * P, :], hrow[:, t % 2, :]).then_inc(h_out[t % 2], 16)
                for q in range(RAW - AHEAD, 2 * PIECES):
                    load_piece(layer, 0, q, first=True)
                with sp.Fori(0, NE - 4, 2) as e:
                    for q in range(2 * PIECES):
                        load_piece(layer, e, q, base=2)
                for q in range(2 * PIECES - AHEAD):
                    load_piece(layer, NE - 2, q, last=True)
            sp.wait_ge(moe_added, ADDS * PAIRS * LAYERS)
            for t in range(NT):
                dst = outs[0][0, t * P:(t + 1) * P, :] if t < PT_ else outs[1][0, (t - PT_) * P:(t - PT_ + 1) * P, :]
                sp.dma_start(dst, x[:, t, :]).then_inc(y_out, 16)
            sp.wait_ge(y_out, 16 * NT)

        @block.gpsimd
        def _(pool):
            hnorms = 0
            for layer in range(LAYERS):
                def row_rstd(step):
                    pool.wait_ge(var_ready, step + 1)
                    nc.gpsimd.tensor_tensor(rstd[:], var[:], minus_half[:, 0:NT], ALU.pow).then_inc(rstd_ready, 1)

                row_rstd(2 * layer)
                for _ in range(2 * NG if layer == 0 else NG + 1):
                    hnorms += 1
                    pool.wait_ge(hvar_ready, hnorms)
                    nc.gpsimd.tensor_tensor(hrstd[:], hvar[:], minus_half[:], ALU.pow).then_inc(hrstd_ready, 1)
                row_rstd(2 * layer + 1)
                pool.wait_ge(slots_ready, layer + 1)
                for t in range(2):
                    pool.wait_ge(h_out[t], 16 * NT // 2 * (layer + 1))
                for e in range(NE):
                    n = layer * NE + e
                    if e >= 2:
                        pool.wait_ge(xe_turned, n - 1)
                    nc.gpsimd.indirect_dma_start(
                        out=xg[:, e % 2, :], out_offset=None, in_=h_d,
                        in_offset=bass.IndirectOffsetOnAxis(ap=take[:, e:e + 1], axis=0)).then_inc(xg_in[e % 2], 16)

        @block.scalar
        def _(act):
            turned = 0
            lots = 0
            taken = 0
            for layer in range(LAYERS):
                def sums_of_squares(step):
                    for t in range(NT):
                        n = step * NT + t
                        if step == 0:
                            act.wait_ge(x_in, 16 * NT)
                        elif step % 2:
                            act.wait_ge(attn_added, LAST_OUT * layer + LAST_OUT - NT + t + 1)
                        else:
                            act.wait_ge(moe_added, ADDS * PAIRS * layer)
                        if n >= 1:
                            act.wait_ge(sumsq_ready, n)
                        if t == 0 and step:
                            act.wait_ge(rstd_ready, step)
                        nc.scalar.activation(ps[:, 4:6, :].rearrange("p b n -> p (b n)"), x[:, t, :], ACT.Square,
                                             accum_out=sumsq[:, t:t + 1]).then_inc(sumsq_ready, 1)

                def take_transposed(step, dst):
                    for t in range(NT):
                        n = step * NT + t
                        act.wait_ge(h_turned, n + 1)
                        b = 2 * (t % 2)
                        nc.scalar.activation(dst(t), ps[:, b:b + 2, :].rearrange("p b (k n) -> p (b k) n", n=P),
                                             ACT.Copy).then_inc(hT_ready, 1)

                sums_of_squares(2 * layer)
                take_transposed(2 * layer, lambda t: hT[:, :, t * P:(t + 1) * P])

                def take_chunk(chunk):
                    kind = CHUNKS[chunk][1]
                    nonlocal taken
                    for t in range(NT):
                        n = chunk * NT + t
                        act.wait_ge(proj_done, n + 1)
                        dst = {"q": qraw, "k": kraw, "v": v}[kind]
                        taken += 1
                        nc.scalar.activation(dst[:, t, :], ps[:, 6 + n % 2, 0:GW], ACT.Copy).then_inc(qkv_taken, 1)

                def take_turned(kind):
                    nonlocal turned
                    for b in range(NT // 2):
                        act.wait_ge(qk_turned, turned + 1)
                        src = ps[:, 4 + turned % 2, :].rearrange("p (t a n) -> p t a n", t=2, n=P)
                        cols = slice(b * 2 * P, (b + 1) * 2 * P)
                        if kind == "k" and layer == 1:
                            for half in range(2):
                                for to in range(2):
                                    dst = kT[to * 64:(to + 1) * 64, half::2, cols].rearrange("p a (t n) -> p t a n", t=2)
                                    ins = nc.scalar.activation(dst, src[half * 64:(half + 1) * 64], ACT.Copy)
                        else:
                            buf = qT if kind == "q" else kT
                            dst = buf[:, 0:2, cols].rearrange("p a (t n) -> p t a n", t=2)
                            if kind == "q":
                                dst = dst[:, :, :, ::-1]
                            ins = nc.scalar.activation(dst, src, ACT.Copy)
                        ins.then_inc(qk_taken, 1)
                        turned += 1

                for g in range(NG):
                    if layer == 0:
                        for kind in "qkv":
                            take_chunk(chunk_at(0, kind, g))
                        take_turned("q")
                        take_turned("k")
                    else:
                        if g == 0:
                            take_chunk(chunk_at(1, "k", 0))
                            take_chunk(chunk_at(1, "v", 0))
                        take_chunk(chunk_at(1, "q", g))
                        if g == 0:
                            take_turned("k")
                        take_turned("q")
                    for n in range(g * NT, (g + 1) * NT):
                        unit = UNITS[layer][n]
                        u = unit_rank(layer, n)
                        act.wait_ge(negmax_ready, u + 1)
                        p = unit_view(probs[:, u % 2, :], unit, layer, BAND)
                        for h in range(GH):
                            ins = nc.scalar.activation(p[:, h, :], p[:, h, :], ACT.Exp,
                                                       bias=row[:, u % 3, GW + h:GW + h + 1],
                                                       accum_out=row[:, u % 3, GW + GH + h:GW + GH + h + 1])
                        ins.then_inc(probs_ready, 1)
                        for lot in batches_of(layer, unit):
                            act.wait_ge(probs_turned, lots + 1)
                            w = len(lot) * P
                            nc.scalar.activation(probsT[:, lots % 2, 0:w], ps[:, 4 + lots % 2, 0:w],
                                                 ACT.Copy).then_inc(probsT_ready, 1)
                            lots += 1

                for t in range(NT):
                    n = layer * NT + t
                    act.wait_ge(mix_arg_ready, n + 1)
                    w = NH if layer == 0 else 2 * NH
                    nc.scalar.activation(mix_exp[:, 0:w], mix_arg[:, 0:w], ACT.Exp).then_inc(mix_exp_ready, 1)
                    act.wait_ge(mix_turned, n + 1)
                    b = 2 * (t % 2)
                    nc.scalar.activation(hT[:, 0:KX, t * P:(t + 1) * P][:, :, ::-1],
                                         ps[:, b:b + 2, :].rearrange("p b n -> p (b n)")[:, 0:MIX].rearrange("p (k n) -> p k n", n=P),
                                         ACT.Copy).then_inc(mixT_ready, 1)

                sums_of_squares(2 * layer + 1)
                take_transposed(2 * layer + 1, lambda t: hTr[:, t % 2, :, :])
                act.wait_ge(rlog_ready, layer + 1)
                nc.scalar.activation(lexp[:], lgt[:], ACT.Exp).then_inc(rexp_ready, 1)

                def split(j, q, first=False):
                    n, slot, to = stream(layer, j, q)
                    act.wait_ge(piece_in[slot], 16 * (NE * PIECES // RAW * layer + (AHEAD + q) // RAW + 1) + 16 * (2 * PIECES // RAW) * j)
                    if not first or AHEAD + q >= SPLIT:
                        act.wait_ge(piece_used, n + (1 - SPLIT))
                    nc.scalar.activation(w_hi[:, to], ring[:, slot], ACT.Copy).then_inc(hi_split, 1)

                def turned_in(e, par):
                    act.wait_ge(xe_turned, e + 1)
                    nc.scalar.activation(xe_hi[:, par].rearrange("p (b k) c -> p b k c", b=2),
                                         ps[:, 4:6, 0:4 * C].rearrange("p b (k c) -> p b k c", c=C), ACT.Copy).then_inc(xe_hi_ready, 1)

                def silu(e, i, n):
                    act.wait_ge(piece_used, n + 1)
                    nc.scalar.activation(sg[:, i % 2, :], ps[0:C, i % 2, 0:PW], ACT.Silu).then_inc(silu_ready, 1)

                def hidden_turned(e, half):
                    act.wait_ge(hid_turned, 2 * e + (half + 1))
                    nc.scalar.activation(hid_hi[:, 4 * half:4 * half + 4, :],
                                         ps[:, 4 + half, 0:4 * C].rearrange("p (k c) -> p k c", c=C), ACT.Copy).then_inc(hid_hi_ready, 1)

                def take_y(par, half, n):
                    act.wait_ge(piece_used, n + 1)
                    cols = slice(half * BANK, (half + 1) * BANK)
                    nc.scalar.activation(y_s[par * CS:(par + 1) * CS, cols], ps[0:CS, 2 + half, :], ACT.Copy)
                    nc.scalar.activation(y_p[par * CP:(par + 1) * CP, cols], ps[CS:C, 2 + half, :], ACT.Copy).then_inc(y_ready, 1)

                def high_s(pair, j):
                    act.wait_ge(y_ready, 4 * pair + 4)
                    nc.scalar.activation(hi_s[:], y_s[:], ACT.Copy, scale=gate_s[:, bass.ds(j, 1)]).then_inc(hi_ready, 1)

                def high_p(pair, j):
                    nc.scalar.activation(hi_p[:], y_p[:], ACT.Copy, scale=gate_p[:, bass.ds(j, 1)]).then_inc(hi_ready, 1)

                def pair_body(j, first=False, last=False):
                    pair = j + layer * PAIRS
                    count = 2 * PIECES - (AHEAD if last else 0)
                    for q in range(count):
                        par, c = q // PIECES, q % PIECES
                        tail = last and par == 1
                        e = 2 * pair + par
                        n, _, _ = stream(layer, j, q)
                        if c == 5:
                            hidden_turned(e, 0)
                        if c in (1, 3, 5):
                            silu(e, (c + 1) // 2, n)
                        if c == 7 and not tail:
                            silu(e + 1, 0, n)
                        if c == (5 if tail else 6):
                            hidden_turned(e, 1)
                        if q + SPLIT < count:
                            split(j, q + SPLIT, first)
                        elif not last:
                            split(j + 1, q + SPLIT - 2 * PIECES)
                        if c == 2 and not tail:
                            turned_in(e + 1, 1 - par)
                        if par == 0 and c == 1 and not first:
                            high_s(pair - 1, j - 1)
                        if par == 0 and c == 2 and not first:
                            high_p(pair - 1, j - 1)
                        down = c - (6 if tail else 8)
                        if down in (1, 3):
                            if par == 0 and down == 1 and not first:
                                act.wait_ge(lo_ready, 2 * pair)
                            take_y(par, down // 2, n)

                turned_in(layer * NE, 0)
                for q in range(-AHEAD, SPLIT):
                    split(0, q, True)
                    if q == -1:
                        silu_at = stream(layer, 0, q)[0]
                silu(layer * NE, 0, silu_at)
                pair_body(0, first=True)
                with act.Fori(1, PAIRS - 1) as j:
                    pair_body(j)
                pair_body(PAIRS - 1, last=True)
                high_s(PAIRS * (layer + 1) - 1, PAIRS - 1)
                high_p(PAIRS * (layer + 1) - 1, PAIRS - 1)

        @block.vector
        def _(dve):
            steps = {}

            def step(ins, on):
                steps[on.name] = steps.get(on.name, 0) + 1
                ins.then_inc(on, 1)
                dve.wait_ge(on, steps[on.name])

            nc.vector.memset(minus_half[:], -0.5)
            nc.vector.memset(rb, 1.0).then_inc(rb_set, 1)
            dve.wait_ge(tab_mm, 1)
            nc.vector.tensor_copy(tab, ps[0:NH, 0:TABW // BANK, :].rearrange("p b n -> p (b n)")).then_inc(tab_cp, 1)
            dve.wait_ge(const_in, 16 * 6)

            hn = 0
            gains = 0
            for layer in range(LAYERS):
                def norm_rows(s, dst):
                    nonlocal gains
                    dve.wait_ge(sumsq_ready, NT * (s + 1))
                    nc.vector.tensor_scalar(var[:], sumsq[:], 1.0 / DM, EPS, ALU.mult, ALU.add).then_inc(var_ready, 1)
                    gains += 1
                    dve.wait_ge(gain_in, 16 * gains)
                    dve.wait_ge(rstd_ready, s + 1)
                    for t in range(NT):
                        n = NT * s + t
                        if t >= 2:
                            dve.wait_ge(h_turned, n - 1)
                            if s % 2:
                                dve.wait_ge(h_out[t % 2], 16 * (layer * NT // 2 + t // 2))
                        nc.vector.scalar_tensor_tensor(dst(t), x[:, t, :], rstd[:, t:t + 1], gain[:],
                                                       ALU.mult, ALU.mult).then_inc(h_ready, 1)

                if layer == 0:
                    dve.wait_ge(tab_out, 16)
                norm_rows(2 * layer, lambda t: probs[:, t % 2, 0:DM])

                def norm_heads(kind):
                    nonlocal hn
                    hn += 1
                    raw = (qraw if kind == "q" else kraw)[:, :, :].rearrange("p t c -> p (t c)")
                    w = NT * GW // 2
                    for i in range(2):
                        part = raw[:, i * w:(i + 1) * w]
                        step(nc.vector.tensor_tensor(sq, part, part, ALU.mult), head_sums)
                        step(nc.vector.tensor_reduce(hsum[:, i * w // HD:(i + 1) * w // HD],
                                                     sq.rearrange("p (h n) -> p h n", n=HD), AX.X, ALU.add), head_sums)
                    nc.vector.tensor_scalar(hvar[:], hsum[:], 1.0 / HD, EPS, ALU.mult, ALU.add).then_inc(hvar_ready, 1)
                    dve.wait_ge(hrstd_ready, hn)
                    heads = raw.rearrange("p (h n) -> p h n", n=HD)
                    step(nc.vector.tensor_tensor(heads, heads, hrstd[:].unsqueeze(2).to_broadcast([P, NT * GH, HD]), ALU.mult),
                         head_sums)
                    which = 2 * layer + (0 if kind == "q" else 1)
                    nc.vector.tensor_tensor(heads, heads, head_gain[:, which, :].unsqueeze(1).to_broadcast([P, NT * GH, HD]),
                                            ALU.mult).then_inc(head_normed, 1)

                def take_unit(n):
                    u = unit_rank(layer, n)
                    dve.wait_ge(unit_done, u + 1)
                    nc.vector.tensor_copy(row[:, u % 3, 0:GW], u_bank).then_inc(row_ready, 1)

                for g in range(NG):
                    if layer == 0:
                        for kind in "qk":
                            dve.wait_ge(qkv_taken, NT * (chunk_at(0, kind, g) + 1))
                            norm_heads(kind)
                    else:
                        before = FIRST_OUT[0]
                        if g == 0:
                            dve.wait_ge(qkv_taken, NT * (before + 1))
                            norm_heads("k")
                        dve.wait_ge(qkv_taken, NT * (before + 3 + g))
                        norm_heads("q")
                    n = layer * NG + g
                    dve.wait_ge(bias_in[n % 2], bias_value(n))
                    for n in range(g * NT, (g + 1) * NT):
                        unit = UNITS[layer][n]
                        u = unit_rank(layer, n)
                        dve.wait_ge(scores_done, u + 1)
                        p = unit_view(probs[:, u % 2, :], unit, layer, BAND)
                        nc.vector.scalar_tensor_tensor(p, unit_view(s_bank, unit, layer, BANK), HD ** -0.5,
                                                       bias_view(layer, unit), ALU.mult, ALU.add).then_inc(logits_ready, 1)
                        if u >= 3:
                            dve.wait_ge(*row_out_of(u - 3))
                        dve.wait_ge(logits_ready, u + 1)
                        nc.vector.tensor_reduce(row[:, u % 3, GW:GW + GH], p, AX.X, ALU.max, negate=True).then_inc(negmax_ready, 1)
                        if n > g * NT:
                            take_unit(n - 1)
                    take_unit((g + 1) * NT - 1)

                def mix(t):
                    n = layer * NT + t
                    dve.wait_ge(mix_in_s[t % 2], 16 * (n // 2 + 1))
                    mi = mix_in[t % 2].rearrange("p (g c) -> p g c", g=NG)
                    out4 = mi[:, :, 0:GW].rearrange("p g (h n) -> p g h n", n=HD)
                    neg, sums = mi[:, :, GW:GW + GH], mi[:, :, GW + GH:ROW]
                    by_group = lambda ap: ap[:, 0:NH].rearrange("p (g h) -> p g h", g=NG)
                    if layer == 0:
                        step(nc.vector.tensor_tensor(mix_top[:, 0:GH], neg[:, 0, :], neg[:, 1, :], ALU.min), mix_step)
                        step(nc.vector.tensor_tensor(mix_top[:, 0:GH], mix_top[:, 0:GH], neg[:, 2, :], ALU.min), mix_step)
                        nc.vector.tensor_tensor(by_group(mix_arg), mix_top[:, 0:GH].unsqueeze(1).to_broadcast([P, NG, GH]),
                                                neg, ALU.subtract).then_inc(mix_arg_ready, 1)
                        dve.wait_ge(mix_exp_ready, n + 1)
                        step(nc.vector.tensor_tensor(by_group(mix_w), by_group(mix_exp), sums, ALU.mult), mix_step)
                        step(nc.vector.tensor_reduce(mix_den[:, 0:GH], mix_w[:].rearrange("p (g h) -> p h g", g=NG), AX.X,
                                                     ALU.add), mix_step)
                        step(nc.vector.reciprocal(mix_rec[:, 0:GH], mix_den[:, 0:GH]), mix_step)
                        step(nc.vector.tensor_tensor(by_group(mix_c), by_group(mix_exp),
                                                     mix_rec[:, 0:GH].unsqueeze(1).to_broadcast([P, NG, GH]), ALU.mult), mix_step)
                    else:
                        if t == 0:
                            step(nc.vector.tensor_scalar(sink[:], sink[:], -1.0, None, ALU.mult), mix_step)
                        step(nc.vector.tensor_tensor(by_group(mix_top), neg, by_group(sink), ALU.min), mix_step)
                        step(nc.vector.tensor_tensor(by_group(mix_arg), by_group(mix_top), neg, ALU.subtract), mix_step)
                        nc.vector.tensor_tensor(mix_arg[:, NH:2 * NH], mix_top[:], sink[:], ALU.subtract).then_inc(mix_arg_ready, 1)
                        dve.wait_ge(mix_exp_ready, n + 1)
                        step(nc.vector.tensor_tensor(by_group(mix_w), by_group(mix_exp), sums, ALU.mult), mix_step)
                        step(nc.vector.tensor_tensor(mix_den[:], mix_w[:], mix_exp[:, NH:2 * NH], ALU.add), mix_step)
                        step(nc.vector.reciprocal(mix_rec[:], mix_den[:]), mix_step)
                        step(nc.vector.tensor_tensor(mix_c[:], mix_exp[:, 0:NH], mix_rec[:], ALU.mult), mix_step)
                    if t >= 2:
                        dve.wait_ge(mix_turned, n - 1)
                    nc.vector.tensor_tensor(probs[:, t % 2, 0:MIX].rearrange("p (g h n) -> p g h n", g=NG, n=HD), out4,
                                            by_group(mix_c).unsqueeze(3).to_broadcast([P, NG, GH, HD]),
                                            ALU.mult).then_inc(mixed_ready, 1)

                def add_out(c, t):
                    n = NT * (FIRST_OUT[layer] + c) + t
                    dve.wait_ge(proj_done, n + 1)
                    xs = x[:, t, c * GW:(c + 1) * GW]
                    nc.vector.tensor_tensor(xs, ps[:, 6 + n % 2, 0:GW], xs, ALU.add).then_inc(attn_added, 1)

                for t in range(NT):
                    mix(t)
                    if t >= 2:
                        add_out(0, t - 2)
                add_out(0, NT - 2)
                add_out(0, NT - 1)
                for c in range(1, DM // GW):
                    for t in range(NT):
                        add_out(c, t)

                dve.wait_ge(attn_added, LAST_OUT * (layer + 1))
                norm_rows(2 * layer + 1, lambda t: hrow[:, t % 2, :])
                dve.wait_ge(route_mm, NT * (layer + 1))
                lp = ps[:, 6, 0:NT * NE].rearrange("p (t e) -> p t e", e=NE)
                step(nc.vector.tensor_reduce(lmax[:], lp, AX.X, ALU.max, negate=True), route_step)
                nc.vector.tensor_tensor(lgt[:], lp, lmax[:].unsqueeze(2).to_broadcast([P, NT, NE]), ALU.add).then_inc(rlog_ready, 1)
                dve.wait_ge(rexp_ready, layer + 1)
                step(nc.vector.tensor_reduce(lsum[:], lexp[:], AX.X, ALU.add), route_step)
                step(nc.vector.reciprocal(lrec[:], lsum[:]), route_step)
                nc.vector.tensor_tensor(aff[:], lexp[:], lrec[:].unsqueeze(2).to_broadcast([P, NT, NE]),
                                        ALU.mult).then_inc(aff_ready, 1)
                nc.vector.memset(pk_i[:], 0.0)
                nc.vector.memset(pk_g[:], 0.0)
                step(nc.vector.memset(am[:], -1.0), route_step)
                dve.wait_ge(aff_turned, layer + 1)
                nc.vector.tensor_copy(am[0:NE, :], ps[0:NE, 4, :])
                step(nc.vector.tensor_copy(am[32:32 + NE, 0:SEQ], ps[0:NE, 5, 0:SEQ]), route_step)
                for r in range(CS // 8):
                    best = top[:, 8 * r:8 * r + 8]
                    step(nc.vector.max(best, am[:]), route_step)
                    step(nc.vector.max_index(topi[:, 8 * r:8 * r + 8], best, am[:]), route_step)
                    if r < CS // 8 - 1:
                        step(nc.vector.match_replace(am[:], best, am[:], -1.0), route_step)
                for dst, src in ((pk_i, topi), (pk_g, top)):
                    for n in range(2):
                        nc.vector.tensor_copy(dst[0:NE, n * CS:(n + 1) * CS], src[0:NE, :])
                    for n in range(3):
                        ins = nc.vector.tensor_copy(dst[32:32 + NE, n * CP:(n + 1) * CP], src[32:32 + NE, 0:CP])
                ins.then_inc(picks_ready, 1)
                dve.wait_ge(picks_turned, layer + 1)
                for n, (a, b) in enumerate(((slot_s, slot_p), (gate_s, gate_p))):
                    src = ps[:, 4, n * 64:n * 64 + 48]
                    for par in range(2):
                        nc.vector.tensor_copy(a[par * CS:(par + 1) * CS, :], src[par * CS:(par + 1) * CS, par:NE:2])
                        ins = nc.vector.tensor_copy(b[par * CP:(par + 1) * CP, :], src[par * CP:(par + 1) * CP, 32 + par:48:2])
                nc.vector.tensor_scalar(take[0:CS, :], ps[0:CS, 4, 0:NE], float(SEQ), None, ALU.add)
                nc.vector.tensor_copy(take[CS:C, :], ps[CS:C, 4, 32:48]).then_inc(slots_ready, 1)
                dve.wait_ge(route_in, 32 * (layer + 1))

                def split(j, q):
                    n, slot, to = stream(layer, j, q)
                    dve.wait_ge(hi_split, n + 1)
                    nc.vector.tensor_tensor(w_lo[:, to], ring[:, slot], w_hi[:, to].bitcast(F32), ALU.subtract).then_inc(lo_split, 1)

                def turned_in(e, par):
                    dve.wait_ge(xe_hi_ready, e + 1)
                    src = ps[:, 4:6, 0:4 * C].rearrange("p b (k c) -> p b k c", c=C)
                    nc.vector.tensor_tensor(xe_lo[:, par].rearrange("p (b k) c -> p b k c", b=2), src,
                                            xe_hi[:, par].bitcast(F32).rearrange("p (b k) c -> p b k c", b=2),
                                            ALU.subtract).then_inc(xe_lo_ready, 1)

                def product(e, i, first=False):
                    dve.wait_ge(silu_ready, 4 * e + (i + 1))
                    if i in (0, 2) and not first:
                        dve.wait_ge(hid_turned, 2 * e + (i // 2 - 1))
                    nc.vector.tensor_tensor(hid[:, i * PW:(i + 1) * PW], sg[:, i % 2, :], ps[0:C, i % 2, PW:2 * PW],
                                            ALU.mult).then_inc(hid_ready, 1)

                def hidden_turned(e, half):
                    dve.wait_ge(hid_hi_ready, 2 * e + (half + 1))
                    ks = slice(4 * half, 4 * half + 4)
                    nc.vector.tensor_tensor(hid_lo[:, ks, :], ps[:, 4 + half, 0:4 * C].rearrange("p (k c) -> p k c", c=C),
                                            hid_hi[:, ks, :].bitcast(F32), ALU.subtract).then_inc(hid_lo_ready, 1)

                def one_hot(j):
                    col = bass.ds(j, 1)
                    nc.vector.tensor_scalar(hot_s[:], iota[:], slot_s[:, col], None, ALU.is_equal)
                    nc.vector.tensor_scalar(hot_p[:], iota[0:2 * CP, 0:SEQ], slot_p[:, col], None, ALU.is_equal).then_inc(hot_ready, 1)

                def low_s(pair, j):
                    dve.wait_ge(hi_ready, 2 * pair + 1)
                    nc.vector.scalar_tensor_tensor(lo_s[:], y_s[:], gate_s[:, bass.ds(j, 1)], hi_s[:].bitcast(F32),
                                                   ALU.mult, ALU.subtract).then_inc(lo_ready, 1)

                def low_p(pair, j):
                    dve.wait_ge(hi_ready, 2 * pair + 2)
                    nc.vector.scalar_tensor_tensor(lo_p[:], y_p[:], gate_p[:, bass.ds(j, 1)], hi_p[:].bitcast(F32),
                                                   ALU.mult, ALU.subtract).then_inc(lo_ready, 1)

                def add_rows(pair, n, banks=(6, 7)):
                    t, half = (n // 2 + PT_) % NT, n % 2
                    dve.wait_ge(comb_done, ADDS * pair + (n + 1))
                    xs = x[:, t, half * BANK:(half + 1) * BANK]
                    nc.vector.tensor_tensor(xs, ps[:, banks[n % len(banks)], :], xs, ALU.add).then_inc(moe_added, 1)

                def pair_body(j, first=False, last=False):
                    pair = j + layer * PAIRS
                    count = 2 * PIECES - (AHEAD if last else 0)
                    for q in range(count):
                        par, c = q // PIECES, q % PIECES
                        tail = last and par == 1
                        e = 2 * pair + par
                        if not first and COMB < q <= COMB + ADDS:
                            add_rows(pair - 1, q - COMB - 1)
                        if c == 5:
                            hidden_turned(e, 0)
                        if c in (1, 3, 5):
                            product(e, (c + 1) // 2, first and c == 3 and layer == 0 and par == 0)
                        if c == 7 and not tail:
                            product(e + 1, 0)
                        if c == (5 if tail else 6):
                            hidden_turned(e, 1)
                        if q + SPLIT < count:
                            split(j, q + SPLIT)
                        elif not last:
                            split(j + 1, q + SPLIT - 2 * PIECES)
                        if c == 2 and not tail:
                            turned_in(e + 1, 1 - par)
                        if q == 2 and not first:
                            low_s(pair - 1, j - 1)
                        if q == 4 and not first:
                            low_p(pair - 1, j - 1)
                        if q == 20:
                            one_hot(j)

                turned_in(layer * NE, 0)
                for q in range(-AHEAD, SPLIT):
                    split(0, q)
                product(layer * NE, 0, first=layer == 0)
                pair_body(0, first=True)
                with dve.Fori(1, PAIRS - 1) as j:
                    pair_body(j)
                pair_body(PAIRS - 1, last=True)
                low_s(PAIRS * (layer + 1) - 1, PAIRS - 1)
                low_p(PAIRS * (layer + 1) - 1, PAIRS - 1)
                for n in range(ADDS):
                    add_rows(PAIRS * (layer + 1) - 1, n, LAST_BANKS)

        @block.tensor
        def _(pe):
            pe.wait_ge(tab_in, 32)
            pe.wait_ge(rb_set, 1)
            for b in range(TABW // BANK):
                ins = nc.tensor.matmul(ps[0:NH, b, :], rb, buckets[:, b * BANK:(b + 1) * BANK], start=True, stop=True)
            ins.then_inc(tab_mm, 1)
            pe.wait_ge(const_in, 16 * 6)
            pe.wait_ge(tab_cp, 1)

            turned = 0
            lots = 0
            normed = 0
            for layer in range(LAYERS):
                def turn_rows(s, src, then=None):
                    for t in range(NT):
                        n = NT * s + t
                        pe.wait_ge(h_ready, n + 1)
                        if t >= 2:
                            pe.wait_ge(hT_ready, n - 1)
                        for k in range(KM):
                            ins = nc.tensor.transpose(ps[:, 2 * (t % 2) + k // 4, (k % 4) * P:(k % 4 + 1) * P],
                                                      src(t)[:, k * P:(k + 1) * P], ident[:])
                        ins.then_inc(h_turned, 1)
                        if then is not None and t >= 1:
                            then(t - 1)
                    if then is not None:
                        then(NT - 1)

                turn_rows(2 * layer, lambda t: probs[:, t % 2, 0:DM])
                pe.wait_ge(hT_ready, NT * (2 * layer + 1))

                def project(chunk, tiles=range(NT)):
                    l, kind, g, _ = CHUNKS[chunk]
                    pe.wait_ge(w_in[chunk % 2], 16 * (chunk // 2 + 1))
                    units_before = layer * NU + (0 if g in (None, 0) else g * NT)
                    if units_before:
                        pe.wait_ge(row_ready, units_before)
                    for t in tiles:
                        n = chunk * NT + t
                        if n >= 2:
                            c = (n - 2) // NT
                            outs_before = sum(1 for i in range(c) if CHUNKS[i][1] == "o")
                            if CHUNKS[c][1] == "o":
                                pe.wait_ge(attn_added, outs_before * NT + (n - 2) % NT + 1)
                            else:
                                pe.wait_ge(qkv_taken, (c - outs_before) * NT + (n - 2) % NT + 1)
                        if kind == "o":
                            pe.wait_ge(mixT_ready, layer * NT + t + 1)
                        for k in range(KX if kind == "o" else KM):
                            cols = hT[:, k, t * P:(t + 1) * P] if kind == "o" else tile_rows(hT[:, k, :], l, g, t)
                            ins = nc.tensor.matmul(ps[:, 6 + n % 2, 0:GW], cols, wbuf[:, chunk % 2, k, :],
                                                   start=(k == 0), stop=(k == (KX if kind == "o" else KM) - 1))
                        ins.then_inc(proj_done, 1)

                def turn_heads(buf):
                    nonlocal turned, normed
                    normed += 1
                    pe.wait_ge(head_normed, normed)
                    for b in range(NT // 2):
                        if turned >= 2:
                            pe.wait_ge(qk_taken, turned - 1)
                        for i in range(4):
                            t, a = 2 * b + i // 2, i % 2
                            ins = nc.tensor.transpose(ps[:, 4 + turned % 2, i * P:(i + 1) * P],
                                                      buf[:, t, a * P:(a + 1) * P], ident[:])
                        ins.then_inc(qk_turned, 1)
                        turned += 1

                def scores(n):
                    unit = g, t, first, count = UNITS[layer][n]
                    u = unit_rank(layer, n)
                    if u >= 1:
                        pe.wait_ge(logits_ready, u)
                    for h in range(GH):
                        half = slice((h % 2) * HD, (h % 2 + 1) * HD)
                        kv = h // 2 if layer == 0 else (g * GH + h) // (NH // NKV)
                        for k in range(first, first + count):
                            ins = nc.tensor.matmul(block_view(s_bank, unit, layer, BANK, h, k), qT[half, h // 2, t * P:(t + 1) * P],
                                                   kT[half, kv, k * P:(k + 1) * P], start=True, stop=True)
                    ins.then_inc(scores_done, 1)

                def outputs(n):
                    nonlocal lots
                    unit = g, t, first, count = UNITS[layer][n]
                    u = unit_rank(layer, n)
                    batches = batches_of(layer, unit)
                    pe.wait_ge(probs_ready, u + 1)

                    def turn(i):
                        if lots + i >= 2:
                            pe.wait_ge(probsT_ready, lots + i - 1)
                        for m, (h, k) in enumerate(batches[i]):
                            ins = nc.tensor.transpose(ps[:, 4 + (lots + i) % 2, m * P:(m + 1) * P],
                                                      block_view(probs[:, u % 2, :], unit, layer, BAND, h, k), ident[:])
                        ins.then_inc(probs_turned, 1)

                    def times_v(i):
                        pe.wait_ge(probsT_ready, lots + i + 1)
                        if i == 0 and u >= 1:
                            pe.wait_ge(row_ready, u)
                        for m, (h, k) in enumerate(batches[i]):
                            kv = h if layer == 0 else (g * GH + h) // (NH // NKV)
                            heads = [b for b, (hh, _) in enumerate(batches[i]) if hh == h]
                            ins = nc.tensor.matmul(u_bank[:, h * HD:(h + 1) * HD], probsT[:, (lots + i) % 2, m * P:(m + 1) * P],
                                                   v[:, k, kv * HD:(kv + 1) * HD], start=(m == heads[0]), stop=(m == heads[-1]))
                        return ins

                    turn(0)
                    for i in range(len(batches)):
                        if i + 1 < len(batches):
                            turn(i + 1)
                        ins = times_v(i)
                    ins.then_inc(unit_done, 1)
                    lots += len(batches)

                for g in range(NG):
                    if layer == 0:
                        for kind in "qkv":
                            project(chunk_at(0, kind, g))
                        if lots:
                            pe.wait_ge(probsT_ready, lots)
                        turn_heads(qraw)
                        turn_heads(kraw)
                    else:
                        if g == 0:
                            project(chunk_at(1, "k", 0))
                            project(chunk_at(1, "v", 0))
                        project(chunk_at(1, "q", g))
                        pe.wait_ge(probsT_ready, lots)
                        if g == 0:
                            turn_heads(kraw)
                        turn_heads(qraw)
                    pe.wait_ge(qk_taken, turned)
                    scores(g * NT)
                    for n in range(g * NT, (g + 1) * NT):
                        if n + 1 < (g + 1) * NT:
                            scores(n + 1)
                        outputs(n)

                pe.wait_ge(row_ready, (layer + 1) * NU)

                def turn_mix(t):
                    n = layer * NT + t
                    pe.wait_ge(mixed_ready, n + 1)
                    if t >= 2:
                        pe.wait_ge(mixT_ready, n - 1)
                    for k in range(KX):
                        ins = nc.tensor.transpose(ps[:, 2 * (t % 2) + k // 4, (k % 4) * P:(k % 4 + 1) * P],
                                                  probs[:, t % 2, k * P:(k + 1) * P], ident[:])
                    ins.then_inc(mix_turned, 1)

                turn_mix(0)
                for t in range(NT):
                    if t + 1 < NT:
                        turn_mix(t + 1)
                    project(FIRST_OUT[layer], [t])
                for c in range(1, DM // GW):
                    project(FIRST_OUT[layer] + c)

                def route(t):
                    n = layer * NT + t
                    pe.wait_ge(hT_ready, NT * (2 * layer + 1) + t + 1)
                    for k in range(KM):
                        ins = nc.tensor.matmul(ps[:, 6, t * NE:(t + 1) * NE], hTr[:, t % 2, k, :], router[:, k, :],
                                               start=(k == 0), stop=(k == KM - 1))
                    ins.then_inc(route_mm, 1)

                pe.wait_ge(route_in, 32 * (layer + 1))
                turn_rows(2 * layer + 1, lambda t: hrow[:, t % 2, :], route)
                pe.wait_ge(aff_ready, layer + 1)
                for t in range(NT):
                    bank, at = (5, t) if t < PT_ else (4, t - PT_)
                    ins = nc.tensor.transpose(ps[0:NE, bank, at * P:(at + 1) * P], aff[:, t, :], ident[:])
                ins.then_inc(aff_turned, 1)
                pe.wait_ge(picks_ready, layer + 1)
                nc.tensor.transpose(ps[:, 4, 0:48], pk_i[:], ident[0:48, 0:48])
                nc.tensor.transpose(ps[:, 4, 64:112], pk_g[:], ident[0:48, 0:48]).then_inc(picks_turned, 1)
                pe.wait_ge(slots_ready, layer + 1)

                def turn_in(e, par, j):
                    pe.wait_ge(xg_in[par], 16 * (layer * PAIRS + 1) + 16 * j)
                    for k in range(KM):
                        at = (k % 4) * C
                        ins = nc.tensor.transpose(ps[:, 4 + k // 4, at:at + C], xg[:, par, k * P:(k + 1) * P], ident[0:C, 0:C])
                    ins.then_inc(xe_turned, 1)

                def turn_hidden(e, half):
                    pe.wait_ge(hid_ready, 4 * e + (2 * half + 2))
                    for k in range(4):
                        ins = nc.tensor.transpose(ps[:, 4 + half, k * C:(k + 1) * C],
                                                  hid[:, (4 * half + k) * P:(4 * half + k + 1) * P], ident[0:C, 0:C])
                    ins.then_inc(hid_turned, 1)

                def use_piece(j, q, last=False, e=None):
                    n, _, slot = stream(layer, j, q)
                    par, i = piece_of(q, last)
                    pe.wait_ge(lo_split, n + 1)
                    if i < 8:
                        out = ps[0:C, (i // 2) % 2, (i % 2) * PW:(i % 2 + 1) * PW]
                        hi, lo = xe_hi[:, par % 2], xe_lo[:, par % 2]
                    else:
                        out = ps[0:C, 2 + (i - 8) // 2, (i % 2) * PW:(i % 2 + 1) * PW]
                        hi, lo = hid_hi, hid_lo
                    for k in range(KM):
                        if k == 4 and e is not None:
                            pe.wait_ge(hid_lo_ready, 2 * e + 2)
                        nc.tensor.matmul(out, hi[:, k, :], w_hi[:, slot, k, :], start=(k == 0), stop=False)
                        nc.tensor.matmul(out, hi[:, k, :], w_lo[:, slot, k, :], start=False, stop=False)
                        ins = nc.tensor.matmul(out, lo[:, k, :], w_hi[:, slot, k, :], start=False, stop=(k == KM - 1))
                    ins.then_inc(piece_used, 1)

                def combine(pair, n, banks=(6, 7)):
                    t, half = (n // 2 + PT_) % NT, n % 2
                    if n == 0:
                        pe.wait_ge(hot_ready, pair + 1)
                        pe.wait_ge(lo_ready, 2 * pair + 2)
                    if n >= len(banks):
                        pe.wait_ge(moe_added, ADDS * pair + (n + 1 - len(banks)))
                    cols = slice(half * BANK, (half + 1) * BANK)
                    out = ps[:, banks[n % len(banks)], :]
                    hot, hi, lo = ((hot_p[:, t * P:(t + 1) * P], hi_p, lo_p) if t < PT_
                                   else (hot_s[:, (t - PT_) * P:(t - PT_ + 1) * P], hi_s, lo_s))
                    nc.tensor.matmul(out, hot, hi[:, cols], start=True, stop=False)
                    nc.tensor.matmul(out, hot, lo[:, cols], start=False, stop=True).then_inc(comb_done, 1)

                def pair_body(j, first=False, last=False):
                    pair = j + layer * PAIRS
                    count = 2 * PIECES - (AHEAD if last else 0)
                    for q in range(count):
                        par, c = q // PIECES, q % PIECES
                        tail = last and par == 1
                        e = 2 * pair + par
                        if c in (2, 4):
                            pe.wait_ge(hid_ready, 4 * e + c // 2)
                        if c == 6 and not tail:
                            pe.wait_ge(xe_lo_ready, e + 2)
                            pe.wait_ge(hid_ready, 4 * e + 3)
                        if c == (6 if tail else 8):
                            pe.wait_ge(hid_lo_ready, 2 * e + 1)
                            if not (first and par == 0):
                                pe.wait_ge(y_ready, 2 * e)
                        use_piece(j, q, last, e if c == (6 if tail else 8) else None)
                        if c == 1 and not tail:
                            turn_in(e + 1, 1 - par, j + par)
                        if c == 4:
                            if not tail:
                                pe.wait_ge(xe_lo_ready, e + 2)
                            turn_hidden(e, 0)
                        if c == (5 if tail else 6):
                            turn_hidden(e, 1)
                        if not first and COMB <= q < COMB + ADDS:
                            combine(pair - 1, q - COMB)

                turn_in(layer * NE, 0, 0)
                pe.wait_ge(xe_lo_ready, layer * NE + 1)
                for q in range(-AHEAD, 0):
                    use_piece(0, q)
                pair_body(0, first=True)
                with pe.Fori(1, PAIRS - 1) as j:
                    pair_body(j)
                pair_body(PAIRS - 1, last=True)
                for n in range(ADDS):
                    combine(PAIRS * (layer + 1) - 1, n, LAST_BANKS)
                pe.wait_ge(moe_added, ADDS * PAIRS * (layer + 1))


_OUTS = [((1, SEQ, DM), "float32"), ((1, DEC_SEQ, DM), "float32")]


def kernel(**inputs):
    import concourse.bacc as bacc
    from concourse.bass_utils import run_bass_kernel_spmd

    nc = bacc.Bacc("TRN2", target_bir_lowering=False, num_devices=1)
    arrays, tensors = {}, {}
    for name, a in {**inputs, **shape_constants()}.items():
        a = np.ascontiguousarray(a)
        arrays[f"in_{name}"] = a
        tensors[name] = nc.dram_tensor(f"in_{name}", a.shape, mybir.dt.from_np(a.dtype), kind="ExternalInput").ap()
    outs = [nc.dram_tensor(f"out_{i}", shape, mybir.dt.from_np(np.dtype(dtype)), kind="ExternalOutput").ap()
            for i, (shape, dtype) in enumerate(_OUTS)]
    build_trunk(nc, tensors, outs)
    r = run_bass_kernel_spmd(nc, [arrays], core_ids=[0])
    return tuple(r.results[0][f"out_{i}"] for i in range(len(_OUTS)))
```

```python
import math
from contextlib import ExitStack

import numpy as np

import concourse.bass as bass
from concourse import mybir

F32 = mybir.dt.float32
F32R = mybir.dt.float32r
I32 = mybir.dt.int32
U32 = mybir.dt.uint32
ACT = mybir.ActivationFunctionType
ALU = mybir.AluOpType
AX = mybir.AxisListType

P = 128
BANK = 512
DM = 1024
KM = DM // P
SEQ, DEC_SEQ = 256, 512
TOK = SEQ + DEC_SEQ
NT = TOK // P
PT_ = SEQ // P
LAYERS = 2
HD, NH, NKV = 64, 12, 4
MIX = NH * HD
KX = MIX // P
KVW = NKV * HD
GH = 4
GW = GH * HD
NG = NH // GH
DILATIONS = (1, 4, 16)
HALF_A, HALF_B = 64, 128
BUCKETS, REL_MAX = 32, 1024
EPS = 1e-6
MASKED = -1e30
BAND = 3 * P
ROW = GW + 2 * GH
NE, DE = 16, 1024
CS, CP = 2 * DEC_SEQ // NE, 2 * SEQ // NE
C = CS + CP
PAIRS = NE // 2
PIECES = 12
RAW, SPLIT = 6, 4
AHEAD = 2
PW = DE // 4
COMB = 6
TAB = {(0, 0): (0, 2 * BAND - 2 * P, HALF_A, 1, 1), (1, 0): (1536, 2 * BAND - 2 * P, HALF_B, 1, 1)}
for _g in (1, 2):
    for _r, _tiles in enumerate((PT_, NT - PT_)):
        TAB[0, _g, _r] = (2 * _g * 256 + 256 * _r, 2 * P, HALF_A, _tiles, DILATIONS[_g] // _tiles)
TABW = 2048
CHUNKS = ([(0, kind, g, n * MIX + g * GW) for g in range(NG) for n, kind in enumerate("qkv")]
          + [(0, "o", None, n * GW) for n in range(DM // GW)]
          + [(1, "k", 0, MIX), (1, "q", 0, 0), (1, "v", 0, MIX + KVW)] + [(1, "q", g, g * GW) for g in range(1, NG)]
          + [(1, "o", None, n * GW) for n in range(DM // GW)])


def t5_bucket(rel):
    half = BUCKETS // 2
    max_exact = half // 2
    n = -rel
    base = np.where(n < 0, half, 0)
    n = np.abs(n)
    large = max_exact + (np.log(np.maximum(n, 1) / max_exact)
                         / math.log(REL_MAX / max_exact) * (half - max_exact)).astype(np.int32)
    return (base + np.where(n < max_exact, n, np.minimum(large, half - 1))).astype(np.int32)


def shape_constants():
    buckets = np.zeros((BUCKETS + 1, TABW), np.float32)
    for start, width, half, stride, every in TAB.values():
        for i in range(width):
            rel = i - (BAND - P - 1 if width > 2 * P else P - 1)
            if rel % every == 0 and abs(rel) // every <= half:
                buckets[t5_bucket(np.array(rel * stride)), start + i] = 1.0
            else:
                buckets[BUCKETS, start + i] = MASKED
    return {"c_buckets": buckets, "c_ident": np.eye(P, dtype=np.float32),
            "c_iota": np.tile(np.arange(DEC_SEQ, dtype=np.float32), (P, 1))}


def units_of(layer):
    out = []
    for g in range(NG):
        for t in range(NT):
            lo, hi = (0, PT_) if t < PT_ else (PT_, NT)
            if layer == 0 and g > 0:
                out.append((g, t, t, 1))
            else:
                first = max(t - 1, lo)
                out.append((g, t, first, min(t + 2, hi) - first))
    return out


def batches_of(layer, unit):
    g, t, first, n = unit
    if layer == 0 and g > 0:
        return [[(h, t) for h in range(GH)]]
    return [[(h, k) for k in range(first, first + n)] for h in range(GH)]


def tile_rows(ap, layer, g, t):
    base, tiles, n = (0, PT_, t) if t < PT_ else (PT_ * P, NT - PT_, t - PT_)
    if layer == 0 and g > 0:
        return ap[:, base:base + tiles * P].rearrange("p (m r) -> p r m", r=tiles)[:, n, :]
    return ap[:, t * P:(t + 1) * P]


def build_trunk(nc, d, outs):
    ctx = ExitStack()
    with ctx:
        def sb(name, shape, dt=F32, scope=ctx):
            return scope.enter_context(nc.sbuf_tensor(name, shape, dt))

        def sem(name):
            return ctx.enter_context(nc.semaphore(name))

        tab_d = nc.dram_tensor("bias_rows", [NH, TABW], F32)
        tab_ap = tab_d.ap()
        unit_d = nc.dram_tensor("unit_rows", [NG, TOK, ROW], F32).ap()
        h_d = nc.dram_tensor("ffn_rows", [TOK, DM], F32).ap()

        x = sb("x", [P, NT, DM])
        gain = sb("gain", [P, DM])
        ident = sb("ident", [P, P])
        head_gain = sb("head_gain", [P, 2 * LAYERS, HD])
        sink = sb("sink", [P, NH])
        minus_half = sb("minus_half", [P, NT * GH])
        sumsq = sb("sumsq", [P, NT])
        var = sb("var", [P, NT])
        rstd = sb("rstd", [P, NT])
        hsum = sb("hsum", [P, NT * GH])
        hvar = sb("hvar", [P, NT * GH])
        hrstd = sb("hrstd", [P, NT * GH])
        mix_top = sb("mix_top", [P, NH])
        mix_arg = sb("mix_arg", [P, 2 * NH])
        mix_exp = sb("mix_exp", [P, 2 * NH])
        mix_w = sb("mix_w", [P, NH])
        mix_den = sb("mix_den", [P, NH])
        mix_rec = sb("mix_rec", [P, NH])
        mix_c = sb("mix_c", [P, NH])
        lmax = sb("lmax", [P, NT])
        lgt = sb("lgt", [P, NT, NE])
        lexp = sb("lexp", [P, NT, NE])
        lsum = sb("lsum", [P, NT])
        lrec = sb("lrec", [P, NT])
        aff = sb("aff", [P, NT, NE])
        slot_s = sb("slot_s", [P, PAIRS])
        slot_p = sb("slot_p", [2 * CP, PAIRS])
        gate_s = sb("gate_s", [P, PAIRS])
        gate_p = sb("gate_p", [2 * CP, PAIRS])
        take = sb("take", [C, NE], I32)

        with ExitStack() as at:
            hT_hi = sb("hT_hi", [P, KM, TOK], F32R, scope=at)
            hT_lo = sb("hT_lo", [P, KM, TOK], F32R, scope=at)
            wbuf = sb("wbuf", [P, 2, KM, GW], scope=at)
            c_hi = sb("c_hi", [P, 2, KM, GW], F32R, scope=at)
            c_lo = sb("c_lo", [P, 2, KM, GW], F32R, scope=at)
            sq = sb("sq", [P, NT * GW // 2], scope=at)
            qraw = sb("qraw", [P, NT, GW], scope=at)
            kraw = sb("kraw", [P, NT, GW], scope=at)
            v = sb("v", [P, 2, NT, GW], scope=at)
            qT = sb("qT", [P, 2, TOK], scope=at)
            kT = sb("kT", [P, NKV, TOK], scope=at)
            probs = sb("probs", [P, 2, GH * BAND], scope=at)
            probsT = sb("probsT", [P, 2, BANK], scope=at)
            row = sb("row", [P, 3, ROW], scope=at)
            bias = sb("bias", [P, 2, GH * BAND], scope=at)
            buckets = bias[0:BUCKETS + 1, :, :].rearrange("p a b -> p (a b)")[:, 0:TABW]
            rb = row[0:BUCKETS + 1, 0, 0:NH]
            tab = probs[0:NH, :, :].rearrange("p a b -> p (a b)")[:, 0:TABW]
            rows = v[:, :, :, :].rearrange("p a t c -> p (a t c)")[:, 0:2 * DM].rearrange("p (a c) -> p a c", a=2)
            mixed = v[:, 1].rearrange("p t c -> p (t c)").rearrange("p (a c) -> p a c", a=2)
            mix_in = [qraw[:, :, :].rearrange("p t c -> p (t c)")[:, 0:NG * ROW],
                      kraw[:, :, :].rearrange("p t c -> p (t c)")[:, 0:NG * ROW]]

        with ExitStack() as mo:
            ring = sb("ring", [P, RAW, KM, PW], scope=mo)
            w_hi = sb("w_hi", [P, SPLIT, KM, PW], F32R, scope=mo)
            w_lo = sb("w_lo", [P, SPLIT, KM, PW], F32R, scope=mo)
            router = sb("router", [P, KM, NE], scope=mo)
            iota = sb("iota", [P, DEC_SEQ], scope=mo)
            xg = sb("xg", [C, 2, DM], scope=mo)
            xe_hi = sb("xe_hi", [P, 2, KM, C], F32R, scope=mo)
            xe_lo = sb("xe_lo", [P, 2, KM, C], F32R, scope=mo)
            with ExitStack() as ro:
                hrow = sb("hrow", [P, NT, DM], scope=ro)
                hTr = sb("hTr", [P, 2, KM, P], scope=ro)
                am = sb("am", [48, DEC_SEQ], scope=ro)
                top = sb("top", [48, CS], scope=ro)
                topi = sb("topi", [48, CS], U32, scope=ro)
                pk_i = sb("pk_i", [48, P], scope=ro)
                pk_g = sb("pk_g", [48, P], scope=ro)
            sg = sb("sg", [C, 2, PW], scope=mo)
            hid = sb("hid", [C, DE], scope=mo)
            hid_hi = sb("hid_hi", [P, KM, C], F32R, scope=mo)
            hid_lo = sb("hid_lo", [P, KM, C], F32R, scope=mo)
            y_s = sb("y_s", [P, DM], scope=mo)
            y_p = sb("y_p", [2 * CP, DM], scope=mo)
            hi_s = sb("hi_s", [P, DM], F32R, scope=mo)
            hi_p = sb("hi_p", [2 * CP, DM], F32R, scope=mo)
            lo_s = sb("lo_s", [P, DM], F32R, scope=mo)
            lo_p = sb("lo_p", [2 * CP, DM], F32R, scope=mo)
            hot_s = sb("hot_s", [P, DEC_SEQ], F32R, scope=mo)
            hot_p = sb("hot_p", [2 * CP, SEQ], F32R, scope=mo)

        ps = ctx.enter_context(nc.psum_tensor("ps", [P, 8, BANK], F32))

        const_in = sem("const_in")
        tab_in = sem("tab_in")
        rb_set = sem("rb_set")
        tab_mm = sem("tab_mm")
        tab_cp = sem("tab_cp")
        tab_out = sem("tab_out")
        x_in = sem("x_in")
        gain_in = sem("gain_in")
        sumsq_ready = sem("sumsq_ready")
        var_ready = sem("var_ready")
        rstd_ready = sem("rstd_ready")
        h_ready = sem("h_ready")
        h_turned = sem("h_turned")
        hT_ready = sem("hT_ready")
        hT_lo_ready = sem("hT_lo_ready")
        w_in = [sem(f"w_in{i}") for i in range(2)]
        chunk_hi = sem("chunk_hi")
        chunk_lo = sem("chunk_lo")
        proj_done = sem("proj_done")
        qkv_taken = sem("qkv_taken")
        head_sums = sem("head_sums")
        hvar_ready = sem("hvar_ready")
        hrstd_ready = sem("hrstd_ready")
        head_normed = sem("head_normed")
        qk_turned = sem("qk_turned")
        qk_taken = sem("qk_taken")
        bias_in = [sem(f"bias_in{i}") for i in range(2)]
        scores_done = sem("scores_done")
        logits_ready = sem("logits_ready")
        negmax_ready = sem("negmax_ready")
        probs_ready = sem("probs_ready")
        probs_turned = sem("probs_turned")
        probsT_ready = sem("probsT_ready")
        unit_done = sem("unit_done")
        row_ready = sem("row_ready")
        row_out = [sem(f"row_out{i}") for i in range(3)]
        mix_in_s = [sem(f"mix_in_s{i}") for i in range(2)]
        mix_step = sem("mix_step")
        mix_arg_ready = sem("mix_arg_ready")
        mix_exp_ready = sem("mix_exp_ready")
        mixed_ready = sem("mixed_ready")
        mix_turned = sem("mix_turned")
        mixT_ready = sem("mixT_ready")
        mixT_lo_ready = sem("mixT_lo_ready")
        attn_added = sem("attn_added")
        h_out = [sem(f"h_out{i}") for i in range(2)]
        route_in = sem("route_in")
        route_mm = sem("route_mm")
        route_step = sem("route_step")
        rlog_ready = sem("rlog_ready")
        rexp_ready = sem("rexp_ready")
        aff_ready = sem("aff_ready")
        aff_turned = sem("aff_turned")
        picks_ready = sem("picks_ready")
        picks_turned = sem("picks_turned")
        slots_ready = sem("slots_ready")
        piece_in = [sem(f"piece_in{i}") for i in range(RAW)]
        hi_split = sem("hi_split")
        lo_split = sem("lo_split")
        piece_used = sem("piece_used")
        xg_in = [sem(f"xg_in{i}") for i in range(2)]
        xe_turned = sem("xe_turned")
        xe_hi_ready = sem("xe_hi_ready")
        xe_lo_ready = sem("xe_lo_ready")
        silu_ready = sem("silu_ready")
        hid_ready = sem("hid_ready")
        hid_turned = sem("hid_turned")
        hid_hi_ready = sem("hid_hi_ready")
        hid_lo_ready = sem("hid_lo_ready")
        y_ready = sem("y_ready")
        hi_ready = sem("hi_ready")
        lo_ready = sem("lo_ready")
        hot_ready = sem("hot_ready")
        comb_done = sem("comb_done")
        moe_added = sem("moe_added")
        y_out = sem("y_out")

        UNITS = [units_of(0), units_of(1)]
        NU = NG * NT
        LAST_OUT = NT * DM // GW
        ADDS = 2 * NT
        LATE = 4
        RSTD_PARTS = [[slice(0, NT)], [slice(0, LATE), slice(LATE, NT)]]

        def rstd_count(step, part):
            return sum(len(RSTD_PARTS[i % 2]) for i in range(step)) + part + 1

        HEAD_BANKS = (4, 5, 0, 1, 2, 3)
        LAST_BANKS = (6, 7, 0, 1, 2, 3)

        def w_dram(chunk):
            layer, kind, g, col = CHUNKS[chunk]
            w = d[("a" if layer == 0 else "b") + ("_w_out" if kind == "o" else "_w_in")][0]
            return w[:, col:col + GW].rearrange("(k p) n -> p k n", p=P), (KX if kind == "o" else KM)

        def chunk_at(layer, kind, g):
            return CHUNKS.index(next(c for c in CHUNKS if c[:3] == (layer, kind, g)))

        FIRST_CHUNK = [0, chunk_at(1, "k", 0)]
        FIRST_OUT = [chunk_at(0, "o", None), chunk_at(1, "o", None)]

        END_CHUNK = [FIRST_OUT[0] + DM // GW, FIRST_OUT[1] + DM // GW]

        def beside(chunk):
            _, kind, g, _ = CHUNKS[chunk]
            return kind != "o" and g > 0

        def proj_bank(n):
            return 6 if beside(n // NT) else 6 + n % 2

        SPLIT_LATE = [FIRST_OUT[0] + 2, FIRST_OUT[1] + 2]

        TILES_BESIDE = [(3, 3, 3, 3, 3, 3), (2, 2, 1, 1, 0, 0)]

        EARLY = PT_

        def tiles_beside(layer, n):
            g, i = n // NT, n % NT
            if g == NG - 1:
                return []
            tiles = [(chunk_at(layer, kind, g + 1), t) for kind in ("qkv" if layer == 0 else "q") for t in range(NT)]
            start = sum(TILES_BESIDE[layer][:i])
            return tiles[start:start + TILES_BESIDE[layer][i]]

        def ended_before(layer, n):
            if n == 0:
                return [chunk_at(layer, "v", 0)]
            return [c for c, t in tiles_beside(layer, n - 1) if t == NT - 1]

        def unit_rows(layer, g, t):
            base, tiles, n = (0, PT_, t) if t < PT_ else (PT_ * P, NT - PT_, t - PT_)
            if layer == 0 and g > 0:
                return unit_d[g, base:base + tiles * P, :].rearrange("(m r) c -> r m c", r=tiles)[tiles - 1 - n]
            at = base + (tiles - 1 - n) * P
            return unit_d[g, at:at + P, :]

        def stream(layer, j, q):
            at = AHEAD + q
            return layer * NE * PIECES + j * (2 * PIECES) + at, at % RAW, at % SPLIT

        def piece_of(q, last=False):
            if q < 0:
                return 0, AHEAD + q
            par, c = q // PIECES, q % PIECES
            if c < 6:
                return par, AHEAD + c
            if last and par == 1:
                return par, c + 2
            return (par + 1, c - 6) if c < 8 else (par, c)

        def mirror(t):
            return PT_ - 1 - t if t < PT_ else PT_ + NT - 1 - t

        def unit_rank(layer, n):
            return layer * NU + n

        def row_out_of(u):
            return row_out[u % 3], 16 * (u // 3 + 1)

        BIAS_LOADS = [1, 2, 2, 1, 1, 1]

        def bias_value(n):
            return 16 * sum(BIAS_LOADS[n % 2:n + 1:2])

        def bias_view(layer, unit):
            g, t, first, n = unit
            buf = bias[:, (layer * NG + g) % 2, :]
            if layer == 0 and g > 0:
                kind = 0 if t < PT_ else 1
                return buf[:, kind * GH * P:(kind + 1) * GH * P].rearrange("p (h c) -> p h c", h=GH)
            at = (first - (t - 1)) * P
            return buf.rearrange("p (h c) -> p h c", h=GH)[:, :, at:at + n * P]

        def unit_view(buf, unit, layer, pitch):
            g, t, first, n = unit
            at = 0 if layer == 0 and g > 0 else (first - (t - 1)) * P
            return buf[:, 0:GH * pitch].rearrange("p (h c) -> p h c", h=GH)[:, :, at:at + n * P]

        def block_view(buf, unit, layer, pitch, h, k):
            g, t, first, n = unit
            at = h * pitch + (0 if layer == 0 and g > 0 else (k - (t - 1)) * P)
            return buf[:, at:at + P]

        s_bank = ps[:, 0:GH, :].rearrange("p b n -> p (b n)")
        u_bank = ps[:, 7, GW:2 * GW]

        block = ctx.enter_context(nc.Block())

        @block.sync
        def _(sp):
            def load_chunk(chunk):
                if chunk >= 2:
                    sp.wait_ge(chunk_lo, chunk - 1)
                if chunk == FIRST_CHUNK[1] or chunk == FIRST_CHUNK[1] + 1:
                    sp.wait_ge(piece_used, NE * PIECES)
                src, k = w_dram(chunk)
                sp.dma_start(wbuf[:, chunk % 2, 0:k, :], src).then_inc(w_in[chunk % 2], 16)

            def load_bias(layer, g):
                n = layer * NG + g
                if n >= 2:
                    sp.wait_ge(logits_ready, NT * (n - 1))
                if layer and g == 0:
                    sp.wait_ge(moe_added, ADDS * PAIRS)
                buf = bias[:, n % 2, :]
                for r in range(BIAS_LOADS[n]):
                    if BIAS_LOADS[n] == 1:
                        start, cols = TAB[layer, 0][0], BAND
                    else:
                        start, cols = TAB[layer, g, r][0], P
                    dst = buf[:, r * GH * cols:(r + 1) * GH * cols].rearrange("p (h c) -> p h c", h=GH)
                    src = bass.AP(tab_ap.tensor, g * GH * TABW + start, [[1, P], [TABW, GH], [1, cols]])
                    sp.dma_start(dst, src).then_inc(bias_in[n % 2], 16)

            def load_piece(layer, e, q, first=False, last=False, base=0):
                at, slot, _ = stream(layer, 0, q)
                if not first or AHEAD + q >= RAW:
                    sp.wait_ge(lo_split, e * PIECES + (base * PIECES + at + 1 - RAW))
                par, i = piece_of(q, last)
                w, col = ((d["moe_w_down"], (i - 8) * PW) if i >= 8
                          else (d["moe_w_gate" if i % 2 == 0 else "moe_w_up"], (i // 2) * PW))
                w = w[layer, base + par:].rearrange("e (k p) n -> e p k n", p=P)
                src = w[bass.ds(e, 1), :, :, col:col + PW].rearrange("o p k n -> p (o k) n")
                sp.dma_start(ring[:, slot], src).then_inc(piece_in[slot], 16)

            sp.dma_start(x[:, 0, :], d["x_prompt"][0, 0:P, :]).then_inc(x_in, 16)
            for t in range(1, NT):
                src = (d["x_prompt"][0, t * P:(t + 1) * P, :] if t < PT_
                       else d["x_sample"][0, (t - PT_) * P:(t - PT_ + 1) * P, :])
                sp.dma_start(x[:, t, :], src).then_inc(x_in, 16)
            sp.dma_start(gain[:], bass.AP(d["norm_mix"].tensor, 0, [[0, P], [1, DM]])).then_inc(gain_in, 16)
            sp.dma_start(ident[:], d["c_ident"]).then_inc(const_in, 16)
            for n, name in enumerate(("a_q_gain", "a_k_gain", "b_q_gain", "b_k_gain")):
                sp.dma_start(head_gain[:, n, :], bass.AP(d[name].tensor, 0, [[0, P], [1, HD]])).then_inc(const_in, 16)
            sp.dma_start(sink[:], bass.AP(d["b_sink"].tensor, 0, [[0, P], [1, NH]])).then_inc(const_in, 16)
            sp.dma_start(buckets, d["c_buckets"]).then_inc(tab_in, 16)
            sp.wait_ge(rb_set, 1)
            sp.dma_start(rb[0:BUCKETS], d["rel_bias"]).then_inc(tab_in, 16)
            load_chunk(0)
            load_chunk(1)
            sp.wait_ge(tab_cp, 1)
            sp.dma_start(tab_ap, tab).then_inc(tab_out, 16)
            sp.wait_ge(tab_out, 16)

            for layer in range(LAYERS):
                first = FIRST_CHUNK[layer]
                chunk = first
                if layer == 0:
                    chunk = 2
                else:
                    load_chunk(first)
                    load_chunk(first + 1)
                    chunk = first + 2
                load_bias(layer, 0)
                load_bias(layer, 1)
                def rows_out(n):
                    for u in range(unit_rank(layer, n) - 2, unit_rank(layer, n) + 1):
                        sp.wait_ge(*row_out_of(u))

                def load_mix(t):
                    if t >= 2:
                        sp.wait_ge(mixed_ready, layer * NT + t - 1)
                    sp.dma_start(mix_in[t % 2].rearrange("p (g c) -> p g c", g=NG),
                                 unit_d[:, mirror(t) * P:(mirror(t) + 1) * P, :].rearrange("g p c -> p g c")).then_inc(mix_in_s[t % 2], 16)

                units = UNITS[layer]
                done = chunk_at(layer, "v", 0) + 1
                load_bias_at = NT + 2
                for n in range(NU):
                    done += len(ended_before(layer, n)) if n else 0
                    while chunk <= done + 3 - (1 if n else 0) and chunk < END_CHUNK[layer]:
                        load_chunk(chunk)
                        chunk += 1
                    if n == load_bias_at:
                        load_bias(layer, 2)
                    u = unit_rank(layer, n)
                    sp.wait_ge(row_ready, u + 1)
                    sp.dma_start(unit_rows(layer, units[n][0], units[n][1]),
                                 row[:, u % 3, :]).then_inc(row_out_of(u)[0], 16)
                    if n == NU - NT + EARLY - 1:
                        rows_out(n)
                        for t in range(EARLY):
                            load_mix(t)
                while chunk < END_CHUNK[layer]:
                    load_chunk(chunk)
                    chunk += 1
                rows_out(NU - 1)
                for t in range(EARLY, NT):
                    load_mix(t)
                sp.dma_start(router[:], d["moe_router"][layer].rearrange("(k p) e -> p k e", p=P)).then_inc(route_in, 16)
                sp.dma_start(iota[:], d["c_iota"]).then_inc(route_in, 16)
                sp.wait_ge(h_ready, NT * (2 * layer + 1))
                sp.dma_start(gain[:], bass.AP(d["norm_ffn"].tensor, layer * DM, [[0, P], [1, DM]])).then_inc(gain_in, 16)

                sp.wait_ge(attn_added, LAST_OUT * (layer + 1))
                for q in range(-AHEAD, SPLIT - AHEAD):
                    load_piece(layer, 0, q, first=True)
                for t in range(NT):
                    sp.wait_ge(h_ready, NT * (2 * layer + 1) + t + 1)
                    sp.dma_start(h_d[t * P:(t + 1) * P, :], hrow[:, t, :]).then_inc(h_out[t % 2], 16)
                if layer + 1 < LAYERS:
                    sp.dma_start(gain[:], bass.AP(d["norm_mix"].tensor, (layer + 1) * DM, [[0, P], [1, DM]])).then_inc(gain_in, 16)
                for q in range(SPLIT - AHEAD, 2 * PIECES):
                    load_piece(layer, 0, q, first=True)
                with sp.Fori(0, NE - 4, 2) as e:
                    for q in range(2 * PIECES):
                        load_piece(layer, e, q, base=2)
                for q in range(2 * PIECES - AHEAD):
                    load_piece(layer, NE - 2, q, last=True)
            for i in range(NT):
                t = (i + PT_) % NT
                sp.wait_ge(moe_added, ADDS * PAIRS * LAYERS - ADDS + 2 * i + 2)
                dst = outs[0][0, t * P:(t + 1) * P, :] if t < PT_ else outs[1][0, (t - PT_) * P:(t - PT_ + 1) * P, :]
                sp.dma_start(dst, x[:, t, :]).then_inc(y_out, 16)
            sp.wait_ge(y_out, 16 * NT)

        @block.gpsimd
        def _(pool):
            hnorms = 0
            for layer in range(LAYERS):
                def row_rstd(step):
                    for i, cols in enumerate(RSTD_PARTS[step % 2]):
                        pool.wait_ge(var_ready, rstd_count(step, i))
                        nc.gpsimd.tensor_tensor(rstd[:, cols], var[:, cols], minus_half[:, cols], ALU.pow).then_inc(rstd_ready, 1)

                row_rstd(2 * layer)
                for _ in range(2 * NG if layer == 0 else NG + 1):
                    hnorms += 1
                    pool.wait_ge(hvar_ready, hnorms)
                    nc.gpsimd.tensor_tensor(hrstd[:], hvar[:], minus_half[:], ALU.pow).then_inc(hrstd_ready, 1)
                row_rstd(2 * layer + 1)
                pool.wait_ge(slots_ready, layer + 1)
                for t in range(2):
                    pool.wait_ge(h_out[t], 16 * NT // 2 * (layer + 1))
                for e in range(NE):
                    n = layer * NE + e
                    if e >= 2:
                        pool.wait_ge(xe_turned, n - 1)
                    nc.gpsimd.indirect_dma_start(
                        out=xg[:, e % 2, :], out_offset=None, in_=h_d,
                        in_offset=bass.IndirectOffsetOnAxis(ap=take[:, e:e + 1], axis=0)).then_inc(xg_in[e % 2], 16)

        @block.scalar
        def _(act):
            turned = 0
            lots = 0
            for layer in range(LAYERS):
                def sums_of_squares(step):
                    for i in range(NT):
                        t = (i + PT_) % NT if step and step % 2 == 0 else i
                        n = step * NT + i
                        if step == 0:
                            act.wait_ge(x_in, 16 * NT)
                        elif step % 2:
                            act.wait_ge(attn_added, LAST_OUT * layer + LAST_OUT - NT + t + 1)
                        else:
                            act.wait_ge(moe_added, ADDS * PAIRS * layer - ADDS + 2 * i + 2)
                        if n >= 1:
                            act.wait_ge(sumsq_ready, n)
                        if i == 0 and step:
                            act.wait_ge(rstd_ready, rstd_count(step, 0) - 1)
                        nc.scalar.activation(ps[:, 4:6, :].rearrange("p b n -> p (b n)"), x[:, t, :], ACT.Square,
                                             accum_out=sumsq[:, t:t + 1]).then_inc(sumsq_ready, 1)

                def take_transposed(step, dst, then=None):
                    for t in range(NT):
                        n = step * NT + t
                        act.wait_ge(h_turned, n + 1)
                        b = 2 * (t % 2)
                        nc.scalar.activation(dst(t), ps[:, b:b + 2, :].rearrange("p b (k n) -> p (b k) n", n=P),
                                             ACT.Copy).then_inc(hT_ready, 1)
                        if then is not None and t >= 1:
                            then(t - 1)
                    if then is not None:
                        then(NT - 1)

                def high_chunk(chunk):
                    act.wait_ge(w_in[chunk % 2], 16 * (chunk // 2 + 1))
                    if chunk >= 2:
                        act.wait_ge(proj_done, NT * (chunk - 1))
                    k = KX if CHUNKS[chunk][1] == "o" else KM
                    nc.scalar.activation(c_hi[:, chunk % 2, 0:k, :], wbuf[:, chunk % 2, 0:k, :], ACT.Copy).then_inc(chunk_hi, 1)

                def take_tile(chunk, t):
                    _, kind, g, _ = CHUNKS[chunk]
                    n = chunk * NT + t
                    act.wait_ge(proj_done, n + 1)
                    dst = {"q": qraw, "k": kraw, "v": v[:, g % 2]}[kind]
                    nc.scalar.activation(dst[:, t, :], ps[:, proj_bank(n), 0:GW], ACT.Copy).then_inc(qkv_taken, 1)

                sums_of_squares(2 * layer)
                high_chunk(FIRST_CHUNK[layer])

                def take_first(t):
                    take_tile(FIRST_CHUNK[layer], t)
                    if t == 1:
                        high_chunk(FIRST_CHUNK[layer] + 1)

                take_transposed(2 * layer, lambda t: hT_hi[:, :, t * P:(t + 1) * P], take_first)

                def take_chunk(chunk):
                    for t in range(NT):
                        take_tile(chunk, t)

                def take_turned(kind):
                    nonlocal turned
                    for b in range(NT // 2):
                        act.wait_ge(qk_turned, turned + 1)
                        src = ps[:, HEAD_BANKS[turned % 6], :].rearrange("p (t a n) -> p t a n", t=2, n=P)
                        cols = slice(b * 2 * P, (b + 1) * 2 * P)
                        if kind == "k" and layer == 1:
                            for half in range(2):
                                for to in range(2):
                                    dst = kT[to * 64:(to + 1) * 64, half::2, cols].rearrange("p a (t n) -> p t a n", t=2)
                                    ins = nc.scalar.activation(dst, src[half * 64:(half + 1) * 64], ACT.Copy)
                        else:
                            buf = qT if kind == "q" else kT
                            dst = buf[:, 0:2, cols].rearrange("p a (t n) -> p t a n", t=2)
                            if kind == "q":
                                dst = dst[:, :, :, ::-1]
                            ins = nc.scalar.activation(dst, src, ACT.Copy)
                        ins.then_inc(qk_taken, 1)
                        turned += 1

                def exp_mix(t):
                    act.wait_ge(mix_arg_ready, layer * NT + t + 1)
                    w = NH if layer == 0 else 2 * NH
                    nc.scalar.activation(mix_exp[:, 0:w], mix_arg[:, 0:w], ACT.Exp).then_inc(mix_exp_ready, 1)

                first = FIRST_CHUNK[layer]
                high_chunk(first + 2)
                take_chunk(first + 1)
                high_chunk(first + 3)
                take_chunk(first + 2)
                for g in range(NG):
                    if layer == 0:
                        take_turned("q")
                        take_turned("k")
                    else:
                        if g == 0:
                            take_turned("k")
                        take_turned("q")
                    for n in range(g * NT, (g + 1) * NT):
                        unit = UNITS[layer][n]
                        u = unit_rank(layer, n)
                        act.wait_ge(negmax_ready, u + 1)
                        p = unit_view(probs[:, u % 2, :], unit, layer, BAND)
                        for h in range(GH):
                            ins = nc.scalar.activation(p[:, h, :], p[:, h, :], ACT.Exp,
                                                       bias=row[:, u % 3, GW + h:GW + h + 1],
                                                       accum_out=row[:, u % 3, GW + GH + h:GW + GH + h + 1])
                        ins.then_inc(probs_ready, 1)
                        if n >= NU - EARLY:
                            exp_mix(n - (NU - EARLY))
                        for c in ended_before(layer, n):
                            high_chunk(c + 2)
                        for c, t in tiles_beside(layer, n)[0:1]:
                            take_tile(c, t)
                        for lot in batches_of(layer, unit):
                            act.wait_ge(probs_turned, lots + 1)
                            w = len(lot) * P
                            nc.scalar.activation(probsT[:, lots % 2, 0:w], ps[:, 4 + lots % 2, 0:w],
                                                 ACT.Copy).then_inc(probsT_ready, 1)
                            lots += 1
                        for c, t in tiles_beside(layer, n)[1:]:
                            take_tile(c, t)

                for t in range(NT):
                    n = layer * NT + t
                    if t >= EARLY:
                        exp_mix(t)
                    act.wait_ge(mix_turned, n + 1)
                    b = 2 * (t % 2)
                    nc.scalar.activation(hT_hi[:, 0:KX, t * P:(t + 1) * P][:, :, ::-1],
                                         ps[:, b:b + 2, :].rearrange("p b n -> p (b n)")[:, 0:MIX].rearrange("p (k n) -> p k n", n=P),
                                         ACT.Copy).then_inc(mixT_ready, 1)
                for c in range(SPLIT_LATE[layer], END_CHUNK[layer]):
                    high_chunk(c)

                def split(j, q, first=False):
                    n, slot, to = stream(layer, j, q)
                    act.wait_ge(piece_in[slot], 16 * (NE * PIECES // RAW * layer + (AHEAD + q) // RAW + 1) + 16 * (2 * PIECES // RAW) * j)
                    if not first or AHEAD + q >= SPLIT:
                        act.wait_ge(piece_used, n + (1 - SPLIT))
                    nc.scalar.activation(w_hi[:, to], ring[:, slot], ACT.Copy).then_inc(hi_split, 1)

                sums_of_squares(2 * layer + 1)
                take_transposed(2 * layer + 1, lambda t: hTr[:, t % 2, :, :])
                act.wait_ge(rlog_ready, layer + 1)
                nc.scalar.activation(lexp[:], lgt[:], ACT.Exp).then_inc(rexp_ready, 1)
                for q in range(-AHEAD, SPLIT - AHEAD):
                    split(0, q, True)

                def turned_in(e, par):
                    act.wait_ge(xe_turned, e + 1)
                    nc.scalar.activation(xe_hi[:, par].rearrange("p (b k) c -> p b k c", b=2),
                                         ps[:, 4:6, 0:4 * C].rearrange("p b (k c) -> p b k c", c=C), ACT.Copy).then_inc(xe_hi_ready, 1)

                def silu(e, i, n):
                    act.wait_ge(piece_used, n + 1)
                    nc.scalar.activation(sg[:, i % 2, :], ps[0:C, i % 2, 0:PW], ACT.Silu).then_inc(silu_ready, 1)

                def hidden_turned(e, half):
                    act.wait_ge(hid_turned, 2 * e + (half + 1))
                    nc.scalar.activation(hid_hi[:, 4 * half:4 * half + 4, :],
                                         ps[:, 4 + half, 0:4 * C].rearrange("p (k c) -> p k c", c=C), ACT.Copy).then_inc(hid_hi_ready, 1)

                def take_y(par, half, n):
                    act.wait_ge(piece_used, n + 1)
                    cols = slice(half * BANK, (half + 1) * BANK)
                    nc.scalar.activation(y_s[par * CS:(par + 1) * CS, cols], ps[0:CS, 2 + half, :], ACT.Copy)
                    nc.scalar.activation(y_p[par * CP:(par + 1) * CP, cols], ps[CS:C, 2 + half, :], ACT.Copy).then_inc(y_ready, 1)

                def high_s(pair, j):
                    act.wait_ge(y_ready, 4 * pair + 4)
                    nc.scalar.activation(hi_s[:], y_s[:], ACT.Copy, scale=gate_s[:, bass.ds(j, 1)]).then_inc(hi_ready, 1)

                def high_p(pair, j):
                    nc.scalar.activation(hi_p[:], y_p[:], ACT.Copy, scale=gate_p[:, bass.ds(j, 1)]).then_inc(hi_ready, 1)

                def pair_body(j, first=False, last=False):
                    pair = j + layer * PAIRS
                    count = 2 * PIECES - (AHEAD if last else 0)
                    for q in range(count):
                        par, c = q // PIECES, q % PIECES
                        tail = last and par == 1
                        e = 2 * pair + par
                        n, _, _ = stream(layer, j, q)
                        if c == 5:
                            hidden_turned(e, 0)
                        if c in (1, 3, 5):
                            silu(e, (c + 1) // 2, n)
                        if c == 7 and not tail:
                            silu(e + 1, 0, n)
                        if c == (5 if tail else 6):
                            hidden_turned(e, 1)
                        if q + SPLIT < count:
                            split(j, q + SPLIT, first)
                        elif not last:
                            split(j + 1, q + SPLIT - 2 * PIECES)
                        if c == 2 and not tail:
                            turned_in(e + 1, 1 - par)
                        if par == 0 and c == 1 and not first:
                            high_s(pair - 1, j - 1)
                        if par == 0 and c == 2 and not first:
                            high_p(pair - 1, j - 1)
                        down = c - (6 if tail else 8)
                        if down in (1, 3):
                            if par == 0 and down == 1 and not first:
                                act.wait_ge(lo_ready, 2 * pair)
                            take_y(par, down // 2, n)

                turned_in(layer * NE, 0)
                for q in range(SPLIT - AHEAD, SPLIT):
                    split(0, q, True)
                silu(layer * NE, 0, stream(layer, 0, -1)[0])
                pair_body(0, first=True)
                with act.Fori(1, PAIRS - 1) as j:
                    pair_body(j)
                pair_body(PAIRS - 1, last=True)
                high_s(PAIRS * (layer + 1) - 1, PAIRS - 1)
                high_p(PAIRS * (layer + 1) - 1, PAIRS - 1)

        @block.vector
        def _(dve):
            steps = {}

            def step(ins, on):
                steps[on.name] = steps.get(on.name, 0) + 1
                ins.then_inc(on, 1)
                dve.wait_ge(on, steps[on.name])

            nc.vector.memset(minus_half[:], -0.5)
            nc.vector.memset(rb, 1.0).then_inc(rb_set, 1)
            dve.wait_ge(const_in, 16 * 6)

            hn = 0
            gains = 0
            for layer in range(LAYERS):
                def low_chunk(chunk):
                    dve.wait_ge(chunk_hi, chunk + 1)
                    k = KX if CHUNKS[chunk][1] == "o" else KM
                    nc.vector.tensor_tensor(c_lo[:, chunk % 2, 0:k, :], wbuf[:, chunk % 2, 0:k, :],
                                            c_hi[:, chunk % 2, 0:k, :].bitcast(F32), ALU.subtract).then_inc(chunk_lo, 1)

                def low_rows(t):
                    dve.wait_ge(hT_ready, 2 * layer * NT + t + 1)
                    b, cols = 2 * (t % 2), slice(t * P, (t + 1) * P)
                    nc.vector.tensor_tensor(hT_lo[:, :, cols], ps[:, b:b + 2, :].rearrange("p b (k n) -> p (b k) n", n=P),
                                            hT_hi[:, :, cols].bitcast(F32), ALU.subtract).then_inc(hT_lo_ready, 1)

                def row_means(s, part):
                    cols = RSTD_PARTS[s % 2][part]
                    dve.wait_ge(sumsq_ready, NT * s + cols.stop)
                    nc.vector.tensor_scalar(var[:, cols], sumsq[:, cols], 1.0 / DM, EPS, ALU.mult, ALU.add).then_inc(var_ready, 1)

                def scale_row(s, part, t, dst):
                    dve.wait_ge(rstd_ready, rstd_count(s, part))
                    nc.vector.scalar_tensor_tensor(dst, x[:, t, :], rstd[:, t:t + 1], gain[:], ALU.mult, ALU.mult).then_inc(h_ready, 1)

                row_means(2 * layer, 0)
                gains += 1
                dve.wait_ge(gain_in, 16 * gains)
                for t in range(NT):
                    if t >= 2:
                        dve.wait_ge(h_turned, NT * 2 * layer + t - 1)
                    scale_row(2 * layer, 0, t, rows[:, t % 2, :])
                    if layer == 0 and t == 1:
                        dve.wait_ge(tab_mm, 1)
                        nc.vector.tensor_copy(tab, ps[0:NH, 0:TABW // BANK, :].rearrange("p b n -> p (b n)")).then_inc(tab_cp, 1)
                    if t >= 1:
                        low_rows(t - 1)
                    if t in (1, 3):
                        low_chunk(FIRST_CHUNK[layer] + t // 2)
                low_rows(NT - 1)
                if layer == 0:
                    dve.wait_ge(tab_out, 16)

                def head_squares(kind):
                    nonlocal hn
                    hn += 1
                    raw = (qraw if kind == "q" else kraw)[:, :, :].rearrange("p t c -> p (t c)")
                    w = NT * GW // 2
                    for i in range(2):
                        part = raw[:, i * w:(i + 1) * w]
                        step(nc.vector.tensor_tensor(sq[:], part, part, ALU.mult), head_sums)
                        step(nc.vector.tensor_reduce(hsum[:, i * w // HD:(i + 1) * w // HD],
                                                     sq[:].rearrange("p (h n) -> p h n", n=HD), AX.X, ALU.add), head_sums)
                    nc.vector.tensor_scalar(hvar[:], hsum[:], 1.0 / HD, EPS, ALU.mult, ALU.add).then_inc(hvar_ready, 1)

                def scale_heads(kind):
                    raw = (qraw if kind == "q" else kraw)[:, :, :].rearrange("p t c -> p (t c)")
                    dve.wait_ge(hrstd_ready, hn)
                    heads = raw.rearrange("p (h n) -> p h n", n=HD)
                    step(nc.vector.tensor_tensor(heads, heads, hrstd[:].unsqueeze(2).to_broadcast([P, NT * GH, HD]), ALU.mult),
                         head_sums)
                    which = 2 * layer + (0 if kind == "q" else 1)
                    nc.vector.tensor_tensor(heads, heads, head_gain[:, which, :].unsqueeze(1).to_broadcast([P, NT * GH, HD]),
                                            ALU.mult).then_inc(head_normed, 1)

                def take_unit(n):
                    u = unit_rank(layer, n)
                    dve.wait_ge(unit_done, u + 1)
                    nc.vector.tensor_copy(row[:, u % 3, 0:GW], u_bank).then_inc(row_ready, 1)

                def taken(chunk):
                    return NT * sum(1 for c in range(chunk + 1) if CHUNKS[c][1] != "o")

                first = FIRST_CHUNK[layer]
                for c in (first, first + 1, first + 2):
                    kind = CHUNKS[c][1]
                    if kind != "v":
                        dve.wait_ge(qkv_taken, taken(c))
                        head_squares(kind)
                        scale_heads(kind)
                    if c < first + 2:
                        low_chunk(c + 2)
                by_group = lambda ap: ap[:, 0:NH].rearrange("p (g h) -> p g h", g=NG)

                def mix_args(t):
                    dve.wait_ge(mix_in_s[t % 2], 16 * ((layer * NT + t) // 2 + 1))
                    neg = mix_in[t % 2].rearrange("p (g c) -> p g c", g=NG)[:, :, GW:GW + GH]
                    if layer == 0:
                        step(nc.vector.tensor_tensor(mix_top[:, 0:GH], neg[:, 0, :], neg[:, 1, :], ALU.min), mix_step)
                        step(nc.vector.tensor_tensor(mix_top[:, 0:GH], mix_top[:, 0:GH], neg[:, 2, :], ALU.min), mix_step)
                        nc.vector.tensor_tensor(by_group(mix_arg), mix_top[:, 0:GH].unsqueeze(1).to_broadcast([P, NG, GH]),
                                                neg, ALU.subtract).then_inc(mix_arg_ready, 1)
                    else:
                        if t == 0:
                            step(nc.vector.tensor_scalar(sink[:], sink[:], -1.0, None, ALU.mult), mix_step)
                        step(nc.vector.tensor_tensor(by_group(mix_top), neg, by_group(sink), ALU.min), mix_step)
                        step(nc.vector.tensor_tensor(by_group(mix_arg), by_group(mix_top), neg, ALU.subtract), mix_step)
                        nc.vector.tensor_tensor(mix_arg[:, NH:2 * NH], mix_top[:], sink[:], ALU.subtract).then_inc(mix_arg_ready, 1)

                def mix(t):
                    n = layer * NT + t
                    mi = mix_in[t % 2].rearrange("p (g c) -> p g c", g=NG)
                    out4 = mi[:, :, 0:GW].rearrange("p g (h n) -> p g h n", n=HD)
                    sums = mi[:, :, GW + GH:ROW]
                    dve.wait_ge(mix_exp_ready, n + 1)
                    if layer == 0:
                        step(nc.vector.tensor_tensor(by_group(mix_w), by_group(mix_exp), sums, ALU.mult), mix_step)
                        step(nc.vector.tensor_reduce(mix_den[:, 0:GH], mix_w[:].rearrange("p (g h) -> p h g", g=NG), AX.X,
                                                     ALU.add), mix_step)
                        step(nc.vector.reciprocal(mix_rec[:, 0:GH], mix_den[:, 0:GH]), mix_step)
                        step(nc.vector.tensor_tensor(by_group(mix_c), by_group(mix_exp),
                                                     mix_rec[:, 0:GH].unsqueeze(1).to_broadcast([P, NG, GH]), ALU.mult), mix_step)
                    else:
                        step(nc.vector.tensor_tensor(by_group(mix_w), by_group(mix_exp), sums, ALU.mult), mix_step)
                        step(nc.vector.tensor_tensor(mix_den[:], mix_w[:], mix_exp[:, NH:2 * NH], ALU.add), mix_step)
                        step(nc.vector.reciprocal(mix_rec[:], mix_den[:]), mix_step)
                        step(nc.vector.tensor_tensor(mix_c[:], mix_exp[:, 0:NH], mix_rec[:], ALU.mult), mix_step)
                    if t >= 2:
                        dve.wait_ge(mix_turned, n - 1)
                    nc.vector.tensor_tensor(mixed[:, t % 2, :].rearrange("p (g h n) -> p g h n", g=NG, n=HD), out4,
                                            by_group(mix_c).unsqueeze(3).to_broadcast([P, NG, GH, HD]),
                                            ALU.mult).then_inc(mixed_ready, 1)

                for g in range(NG):
                    n = layer * NG + g
                    dve.wait_ge(bias_in[n % 2], bias_value(n))
                    for n in range(g * NT, (g + 1) * NT):
                        unit = UNITS[layer][n]
                        u = unit_rank(layer, n)
                        dve.wait_ge(scores_done, u + 1)
                        p = unit_view(probs[:, u % 2, :], unit, layer, BAND)
                        nc.vector.scalar_tensor_tensor(p, unit_view(s_bank, unit, layer, BANK), HD ** -0.5,
                                                       bias_view(layer, unit), ALU.mult, ALU.add).then_inc(logits_ready, 1)
                        if u >= 3:
                            dve.wait_ge(*row_out_of(u - 3))
                        dve.wait_ge(logits_ready, u + 1)
                        nc.vector.tensor_reduce(row[:, u % 3, GW:GW + GH], p, AX.X, ALU.max, negate=True).then_inc(negmax_ready, 1)
                        if n > g * NT:
                            take_unit(n - 1)
                        for c in ended_before(layer, n - 1) if n else []:
                            if n > 1 and n % NT and CHUNKS[c][1] in "qk":
                                scale_heads(CHUNKS[c][1])
                            low_chunk(c + 2)
                        for c in ended_before(layer, n):
                            if n and CHUNKS[c][1] in "qk":
                                dve.wait_ge(qkv_taken, taken(c))
                                head_squares(CHUNKS[c][1])
                                if n % NT == NT - 1:
                                    scale_heads(CHUNKS[c][1])
                        early = n - (NU - 1 - EARLY)
                        if 1 <= early < EARLY:
                            mix(early - 1)
                        if 0 <= early < EARLY:
                            mix_args(early)
                    take_unit((g + 1) * NT - 1)
                mix(EARLY - 1)

                def add_out(c, t):
                    n = NT * (FIRST_OUT[layer] + c) + t
                    dve.wait_ge(proj_done, n + 1)
                    xs = x[:, t, c * GW:(c + 1) * GW]
                    nc.vector.tensor_tensor(xs, ps[:, 6 + n % 2, 0:GW], xs, ALU.add).then_inc(attn_added, 1)

                def low_mix(t):
                    dve.wait_ge(mixT_ready, layer * NT + t + 1)
                    b, cols = 2 * (t % 2), slice(t * P, (t + 1) * P)
                    src = ps[:, b:b + 2, :].rearrange("p b n -> p (b n)")[:, 0:MIX].rearrange("p (k n) -> p k n", n=P)
                    nc.vector.tensor_tensor(hT_lo[:, 0:KX, cols][:, :, ::-1], src, hT_hi[:, 0:KX, cols][:, :, ::-1].bitcast(F32),
                                            ALU.subtract).then_inc(mixT_lo_ready, 1)

                low_mix(0)
                low_mix(1)
                for t in range(EARLY, NT):
                    mix_args(t)
                    mix(t)
                    if t > EARLY:
                        low_mix(t - 1)
                    add_out(0, t - 2)
                low_mix(NT - 1)
                add_out(0, NT - 2)
                add_out(0, NT - 1)
                for c in range(1, DM // GW):
                    if c + FIRST_OUT[layer] + 1 < END_CHUNK[layer]:
                        low_chunk(FIRST_OUT[layer] + c + 1)
                    for t in range(NT if c < DM // GW - 1 else LATE):
                        add_out(c, t)

                def split(j, q):
                    n, slot, to = stream(layer, j, q)
                    dve.wait_ge(hi_split, n + 1)
                    nc.vector.tensor_tensor(w_lo[:, to], ring[:, slot], w_hi[:, to].bitcast(F32), ALU.subtract).then_inc(lo_split, 1)

                def ffn_row(t):
                    dve.wait_ge(attn_added, LAST_OUT * (layer + 1) - NT + t + 1)
                    scale_row(2 * layer + 1, t // LATE, t, hrow[:, t, :])

                row_means(2 * layer + 1, 0)
                add_out(DM // GW - 1, LATE)
                gains += 1
                dve.wait_ge(gain_in, 16 * gains)
                ffn_row(0)
                ffn_row(1)
                add_out(DM // GW - 1, LATE + 1)
                ffn_row(2)
                ffn_row(3)
                row_means(2 * layer + 1, 1)
                ffn_row(4)
                ffn_row(5)
                dve.wait_ge(route_mm, NT * (layer + 1))
                lp = ps[:, 6, 0:NT * NE].rearrange("p (t e) -> p t e", e=NE)
                step(nc.vector.tensor_reduce(lmax[:], lp, AX.X, ALU.max, negate=True), route_step)
                nc.vector.tensor_tensor(lgt[:], lp, lmax[:].unsqueeze(2).to_broadcast([P, NT, NE]), ALU.add).then_inc(rlog_ready, 1)
                dve.wait_ge(rexp_ready, layer + 1)
                step(nc.vector.tensor_reduce(lsum[:], lexp[:], AX.X, ALU.add), route_step)
                step(nc.vector.reciprocal(lrec[:], lsum[:]), route_step)
                nc.vector.tensor_tensor(aff[:], lexp[:], lrec[:].unsqueeze(2).to_broadcast([P, NT, NE]),
                                        ALU.mult).then_inc(aff_ready, 1)
                nc.vector.memset(pk_i[:], 0.0)
                nc.vector.memset(pk_g[:], 0.0)
                step(nc.vector.memset(am[:], -1.0), route_step)
                dve.wait_ge(aff_turned, layer + 1)
                nc.vector.tensor_copy(am[0:NE, :], ps[0:NE, 4, :])
                step(nc.vector.tensor_copy(am[32:32 + NE, 0:SEQ], ps[0:NE, 5, 0:SEQ]), route_step)
                for r in range(CS // 8):
                    best = top[:, 8 * r:8 * r + 8]
                    step(nc.vector.max(best, am[:]), route_step)
                    step(nc.vector.max_index(topi[:, 8 * r:8 * r + 8], best, am[:]), route_step)
                    if r < CS // 8 - 1:
                        step(nc.vector.match_replace(am[:], best, am[:], -1.0), route_step)
                for dst, src in ((pk_i, topi), (pk_g, top)):
                    for n in range(2):
                        nc.vector.tensor_copy(dst[0:NE, n * CS:(n + 1) * CS], src[0:NE, :])
                    for n in range(3):
                        ins = nc.vector.tensor_copy(dst[32:32 + NE, n * CP:(n + 1) * CP], src[32:32 + NE, 0:CP])
                ins.then_inc(picks_ready, 1)
                dve.wait_ge(picks_turned, layer + 1)
                for n, (a, b) in enumerate(((slot_s, slot_p), (gate_s, gate_p))):
                    src = ps[:, 4, n * 64:n * 64 + 48]
                    for par in range(2):
                        nc.vector.tensor_copy(a[par * CS:(par + 1) * CS, :], src[par * CS:(par + 1) * CS, par:NE:2])
                        ins = nc.vector.tensor_copy(b[par * CP:(par + 1) * CP, :], src[par * CP:(par + 1) * CP, 32 + par:48:2])
                nc.vector.tensor_scalar(take[0:CS, :], ps[0:CS, 4, 0:NE], float(SEQ), None, ALU.add)
                nc.vector.tensor_copy(take[CS:C, :], ps[CS:C, 4, 32:48]).then_inc(slots_ready, 1)
                dve.wait_ge(route_in, 32 * (layer + 1))
                for q in range(-AHEAD, 0):
                    split(0, q)

                def turned_in(e, par):
                    dve.wait_ge(xe_hi_ready, e + 1)
                    src = ps[:, 4:6, 0:4 * C].rearrange("p b (k c) -> p b k c", c=C)
                    nc.vector.tensor_tensor(xe_lo[:, par].rearrange("p (b k) c -> p b k c", b=2), src,
                                            xe_hi[:, par].bitcast(F32).rearrange("p (b k) c -> p b k c", b=2),
                                            ALU.subtract).then_inc(xe_lo_ready, 1)

                def product(e, i, first=False):
                    dve.wait_ge(silu_ready, 4 * e + (i + 1))
                    if i in (0, 2) and not first:
                        dve.wait_ge(hid_turned, 2 * e + (i // 2 - 1))
                    nc.vector.tensor_tensor(hid[:, i * PW:(i + 1) * PW], sg[:, i % 2, :], ps[0:C, i % 2, PW:2 * PW],
                                            ALU.mult).then_inc(hid_ready, 1)

                def hidden_turned(e, half):
                    dve.wait_ge(hid_hi_ready, 2 * e + (half + 1))
                    ks = slice(4 * half, 4 * half + 4)
                    nc.vector.tensor_tensor(hid_lo[:, ks, :], ps[:, 4 + half, 0:4 * C].rearrange("p (k c) -> p k c", c=C),
                                            hid_hi[:, ks, :].bitcast(F32), ALU.subtract).then_inc(hid_lo_ready, 1)

                def one_hot(j):
                    col = bass.ds(j, 1)
                    nc.vector.tensor_scalar(hot_s[:], iota[:], slot_s[:, col], None, ALU.is_equal)
                    nc.vector.tensor_scalar(hot_p[:], iota[0:2 * CP, 0:SEQ], slot_p[:, col], None, ALU.is_equal).then_inc(hot_ready, 1)

                def low_s(pair, j):
                    dve.wait_ge(hi_ready, 2 * pair + 1)
                    nc.vector.scalar_tensor_tensor(lo_s[:], y_s[:], gate_s[:, bass.ds(j, 1)], hi_s[:].bitcast(F32),
                                                   ALU.mult, ALU.subtract).then_inc(lo_ready, 1)

                def low_p(pair, j):
                    dve.wait_ge(hi_ready, 2 * pair + 2)
                    nc.vector.scalar_tensor_tensor(lo_p[:], y_p[:], gate_p[:, bass.ds(j, 1)], hi_p[:].bitcast(F32),
                                                   ALU.mult, ALU.subtract).then_inc(lo_ready, 1)

                def add_rows(pair, n, banks=(6, 7)):
                    t, half = (n // 2 + PT_) % NT, n % 2
                    dve.wait_ge(comb_done, ADDS * pair + (n + 1))
                    xs = x[:, t, half * BANK:(half + 1) * BANK]
                    nc.vector.tensor_tensor(xs, ps[:, banks[n % len(banks)], :], xs, ALU.add).then_inc(moe_added, 1)

                def pair_body(j, first=False, last=False):
                    pair = j + layer * PAIRS
                    count = 2 * PIECES - (AHEAD if last else 0)
                    for q in range(count):
                        par, c = q // PIECES, q % PIECES
                        tail = last and par == 1
                        e = 2 * pair + par
                        if not first and COMB < q <= COMB + ADDS:
                            add_rows(pair - 1, q - COMB - 1)
                        if c == 5:
                            hidden_turned(e, 0)
                        if c in (1, 3, 5):
                            product(e, (c + 1) // 2, first and c == 3 and layer == 0 and par == 0)
                        if c == 7 and not tail:
                            product(e + 1, 0)
                        if c == (5 if tail else 6):
                            hidden_turned(e, 1)
                        if q + SPLIT < count:
                            split(j, q + SPLIT)
                        elif not last:
                            split(j + 1, q + SPLIT - 2 * PIECES)
                        if c == 2 and not tail:
                            turned_in(e + 1, 1 - par)
                        if q == 2 and not first:
                            low_s(pair - 1, j - 1)
                        if q == 4 and not first:
                            low_p(pair - 1, j - 1)
                        if q == 20:
                            one_hot(j)

                turned_in(layer * NE, 0)
                for q in range(SPLIT):
                    split(0, q)
                product(layer * NE, 0, first=layer == 0)
                pair_body(0, first=True)
                with dve.Fori(1, PAIRS - 1) as j:
                    pair_body(j)
                pair_body(PAIRS - 1, last=True)
                low_s(PAIRS * (layer + 1) - 1, PAIRS - 1)
                low_p(PAIRS * (layer + 1) - 1, PAIRS - 1)
                for n in range(ADDS):
                    add_rows(PAIRS * (layer + 1) - 1, n, LAST_BANKS)

        @block.tensor
        def _(pe):
            pe.wait_ge(tab_in, 32)
            pe.wait_ge(rb_set, 1)
            for b in range(TABW // BANK):
                ins = nc.tensor.matmul(ps[0:NH, b, :], rb, buckets[:, b * BANK:(b + 1) * BANK], start=True, stop=True)
            ins.then_inc(tab_mm, 1)
            pe.wait_ge(const_in, 16 * 6)
            pe.wait_ge(tab_cp, 1)

            turned = 0
            lots = 0
            normed = 0
            for layer in range(LAYERS):
                def turn_rows(s, src, then=None):
                    for t in range(NT):
                        n = NT * s + t
                        pe.wait_ge(h_ready, n + 1)
                        if t >= 2 and s % 2:
                            pe.wait_ge(hT_ready, n - 1)
                        elif t >= 2:
                            pe.wait_ge(hT_lo_ready, layer * NT + t - 1)
                        for k in range(KM):
                            ins = nc.tensor.transpose(ps[:, 2 * (t % 2) + k // 4, (k % 4) * P:(k % 4 + 1) * P],
                                                      src(t)[:, k * P:(k + 1) * P], ident[:])
                        ins.then_inc(h_turned, 1)
                        if then is not None and t >= 1:
                            then(t - 1)
                    if then is not None:
                        then(NT - 1)

                def project(chunk, tiles=range(NT)):
                    l, kind, g, _ = CHUNKS[chunk]
                    pe.wait_ge(chunk_lo, chunk + 1)
                    if layer and not beside(chunk):
                        pe.wait_ge(row_ready, layer * NU)
                    for t in tiles:
                        n = chunk * NT + t
                        m = n - 1 if beside(chunk) or n and beside((n - 1) // NT) else n - 2
                        if m >= 0:
                            c = m // NT
                            outs_before = sum(1 for i in range(c) if CHUNKS[i][1] == "o")
                            if CHUNKS[c][1] == "o":
                                pe.wait_ge(attn_added, outs_before * NT + m % NT + 1)
                            else:
                                pe.wait_ge(qkv_taken, (c - outs_before) * NT + m % NT + 1)
                        if kind == "o":
                            pe.wait_ge(mixT_lo_ready, layer * NT + t + 1)
                        elif chunk == FIRST_CHUNK[layer]:
                            pe.wait_ge(hT_lo_ready, layer * NT + t + 1)
                        out, w = ps[:, proj_bank(n), 0:GW], chunk % 2
                        last = (KX if kind == "o" else KM) - 1
                        for k in range(last + 1):
                            hi, lo = [part[:, k, t * P:(t + 1) * P] if kind == "o" else tile_rows(part[:, k, :], l, g, t)
                                      for part in (hT_hi, hT_lo)]
                            nc.tensor.matmul(out, hi, c_hi[:, w, k, :], start=(k == 0), stop=False)
                            nc.tensor.matmul(out, hi, c_lo[:, w, k, :], start=False, stop=False)
                            ins = nc.tensor.matmul(out, lo, c_hi[:, w, k, :], start=False, stop=(k == last))
                        ins.then_inc(proj_done, 1)

                turn_rows(2 * layer, lambda t: rows[:, t % 2, :], lambda t: project(FIRST_CHUNK[layer], [t]))

                def turn_heads(buf):
                    nonlocal turned, normed
                    normed += 1
                    pe.wait_ge(head_normed, normed)
                    for b in range(NT // 2):
                        if turned >= 6:
                            pe.wait_ge(qk_taken, turned - 5)
                        for i in range(4):
                            t, a = 2 * b + i // 2, i % 2
                            ins = nc.tensor.transpose(ps[:, HEAD_BANKS[turned % 6], i * P:(i + 1) * P],
                                                      buf[:, t, a * P:(a + 1) * P], ident[:])
                        ins.then_inc(qk_turned, 1)
                        turned += 1

                def scores(n):
                    unit = g, t, first, count = UNITS[layer][n]
                    u = unit_rank(layer, n)
                    if u >= 1:
                        pe.wait_ge(logits_ready, u)
                    for h in range(GH):
                        half = slice((h % 2) * HD, (h % 2 + 1) * HD)
                        kv = h // 2 if layer == 0 else (g * GH + h) // (NH // NKV)
                        for k in range(first, first + count):
                            ins = nc.tensor.matmul(block_view(s_bank, unit, layer, BANK, h, k), qT[half, h // 2, t * P:(t + 1) * P],
                                                   kT[half, kv, k * P:(k + 1) * P], start=True, stop=True)
                    ins.then_inc(scores_done, 1)

                def outputs(n):
                    nonlocal lots
                    unit = g, t, first, count = UNITS[layer][n]
                    u = unit_rank(layer, n)
                    batches = batches_of(layer, unit)
                    pe.wait_ge(probs_ready, u + 1)

                    def turn(i):
                        if lots + i >= 2:
                            pe.wait_ge(probsT_ready, lots + i - 1)
                        for m, (h, k) in enumerate(batches[i]):
                            ins = nc.tensor.transpose(ps[:, 4 + (lots + i) % 2, m * P:(m + 1) * P],
                                                      block_view(probs[:, u % 2, :], unit, layer, BAND, h, k), ident[:])
                        ins.then_inc(probs_turned, 1)

                    def times_v(i):
                        pe.wait_ge(probsT_ready, lots + i + 1)
                        if i == 0 and u >= 1:
                            pe.wait_ge(row_ready, u)
                        for m, (h, k) in enumerate(batches[i]):
                            kv = h if layer == 0 else (g * GH + h) // (NH // NKV)
                            heads = [b for b, (hh, _) in enumerate(batches[i]) if hh == h]
                            ins = nc.tensor.matmul(u_bank[:, h * HD:(h + 1) * HD], probsT[:, (lots + i) % 2, m * P:(m + 1) * P],
                                                   v[:, g % 2 if layer == 0 else 0, k, kv * HD:(kv + 1) * HD], start=(m == heads[0]), stop=(m == heads[-1]))
                        return ins

                    turn(0)
                    for i in range(len(batches)):
                        if i + 1 < len(batches):
                            turn(i + 1)
                        ins = times_v(i)
                    ins.then_inc(unit_done, 1)
                    lots += len(batches)

                project(FIRST_CHUNK[layer] + 1)
                project(FIRST_CHUNK[layer] + 2)
                for g in range(NG):
                    if lots:
                        pe.wait_ge(probsT_ready, lots)
                        pe.wait_ge(logits_ready, layer * NU + g * NT)
                    if layer == 0:
                        turn_heads(qraw)
                        turn_heads(kraw)
                    else:
                        if g == 0:
                            turn_heads(kraw)
                        turn_heads(qraw)
                    pe.wait_ge(qk_taken, turned)
                    scores(g * NT)
                    for n in range(g * NT, (g + 1) * NT):
                        if n + 1 < (g + 1) * NT:
                            scores(n + 1)
                        for c, t in tiles_beside(layer, n)[0:1]:
                            project(c, [t])
                        outputs(n)
                        for c, t in tiles_beside(layer, n)[1:]:
                            project(c, [t])

                pe.wait_ge(row_ready, (layer + 1) * NU)

                def turn_mix(t):
                    n = layer * NT + t
                    pe.wait_ge(mixed_ready, n + 1)
                    if t >= 2:
                        pe.wait_ge(mixT_ready, n - 1)
                    for k in range(KX):
                        ins = nc.tensor.transpose(ps[:, 2 * (t % 2) + k // 4, (k % 4) * P:(k % 4 + 1) * P],
                                                  mixed[:, t % 2, k * P:(k + 1) * P], ident[:])
                    ins.then_inc(mix_turned, 1)

                turn_mix(0)
                turn_mix(1)
                project(FIRST_OUT[layer], [0, 1])
                turn_mix(2)
                for t in range(2, NT):
                    if t + 1 < NT:
                        turn_mix(t + 1)
                    project(FIRST_OUT[layer], [t])
                for c in range(1, DM // GW):
                    project(FIRST_OUT[layer] + c)

                def route(t):
                    n = layer * NT + t
                    pe.wait_ge(hT_ready, NT * (2 * layer + 1) + t + 1)
                    for k in range(KM):
                        ins = nc.tensor.matmul(ps[:, 6, t * NE:(t + 1) * NE], hTr[:, t % 2, k, :], router[:, k, :],
                                               start=(k == 0), stop=(k == KM - 1))
                    ins.then_inc(route_mm, 1)

                pe.wait_ge(route_in, 32 * (layer + 1))
                turn_rows(2 * layer + 1, lambda t: hrow[:, t, :], route)
                pe.wait_ge(aff_ready, layer + 1)
                for t in range(NT):
                    bank, at = (5, t) if t < PT_ else (4, t - PT_)
                    ins = nc.tensor.transpose(ps[0:NE, bank, at * P:(at + 1) * P], aff[:, t, :], ident[:])
                ins.then_inc(aff_turned, 1)
                pe.wait_ge(picks_ready, layer + 1)
                nc.tensor.transpose(ps[:, 4, 0:48], pk_i[:], ident[0:48, 0:48])
                nc.tensor.transpose(ps[:, 4, 64:112], pk_g[:], ident[0:48, 0:48]).then_inc(picks_turned, 1)
                pe.wait_ge(slots_ready, layer + 1)

                def turn_in(e, par, j):
                    pe.wait_ge(xg_in[par], 16 * (layer * PAIRS + 1) + 16 * j)
                    for k in range(KM):
                        at = (k % 4) * C
                        ins = nc.tensor.transpose(ps[:, 4 + k // 4, at:at + C], xg[:, par, k * P:(k + 1) * P], ident[0:C, 0:C])
                    ins.then_inc(xe_turned, 1)

                def turn_hidden(e, half):
                    pe.wait_ge(hid_ready, 4 * e + (2 * half + 2))
                    for k in range(4):
                        ins = nc.tensor.transpose(ps[:, 4 + half, k * C:(k + 1) * C],
                                                  hid[:, (4 * half + k) * P:(4 * half + k + 1) * P], ident[0:C, 0:C])
                    ins.then_inc(hid_turned, 1)

                def use_piece(j, q, last=False, e=None):
                    n, _, slot = stream(layer, j, q)
                    par, i = piece_of(q, last)
                    pe.wait_ge(lo_split, n + 1)
                    if i < 8:
                        out = ps[0:C, (i // 2) % 2, (i % 2) * PW:(i % 2 + 1) * PW]
                        hi, lo = xe_hi[:, par % 2], xe_lo[:, par % 2]
                    else:
                        out = ps[0:C, 2 + (i - 8) // 2, (i % 2) * PW:(i % 2 + 1) * PW]
                        hi, lo = hid_hi, hid_lo
                    for k in range(KM):
                        if k == 4 and e is not None:
                            pe.wait_ge(hid_lo_ready, 2 * e + 2)
                        nc.tensor.matmul(out, hi[:, k, :], w_hi[:, slot, k, :], start=(k == 0), stop=False)
                        nc.tensor.matmul(out, hi[:, k, :], w_lo[:, slot, k, :], start=False, stop=False)
                        ins = nc.tensor.matmul(out, lo[:, k, :], w_hi[:, slot, k, :], start=False, stop=(k == KM - 1))
                    ins.then_inc(piece_used, 1)

                def combine(pair, n, banks=(6, 7)):
                    t, half = (n // 2 + PT_) % NT, n % 2
                    if n == 0:
                        pe.wait_ge(hot_ready, pair + 1)
                        pe.wait_ge(lo_ready, 2 * pair + 1)
                    if n == 2 * (NT - PT_):
                        pe.wait_ge(lo_ready, 2 * pair + 2)
                    if n >= len(banks):
                        pe.wait_ge(moe_added, ADDS * pair + (n + 1 - len(banks)))
                    cols = slice(half * BANK, (half + 1) * BANK)
                    out = ps[:, banks[n % len(banks)], :]
                    hot, hi, lo = ((hot_p[:, t * P:(t + 1) * P], hi_p, lo_p) if t < PT_
                                   else (hot_s[:, (t - PT_) * P:(t - PT_ + 1) * P], hi_s, lo_s))
                    nc.tensor.matmul(out, hot, hi[:, cols], start=True, stop=False)
                    nc.tensor.matmul(out, hot, lo[:, cols], start=False, stop=True).then_inc(comb_done, 1)

                def pair_body(j, first=False, last=False):
                    pair = j + layer * PAIRS
                    count = 2 * PIECES - (AHEAD if last else 0)
                    for q in range(count):
                        par, c = q // PIECES, q % PIECES
                        tail = last and par == 1
                        e = 2 * pair + par
                        if c in (2, 4):
                            pe.wait_ge(hid_ready, 4 * e + c // 2)
                        if c == 6 and not tail:
                            pe.wait_ge(xe_lo_ready, e + 2)
                            pe.wait_ge(hid_ready, 4 * e + 3)
                        if c == (6 if tail else 8):
                            pe.wait_ge(hid_lo_ready, 2 * e + 1)
                            if not (first and par == 0):
                                pe.wait_ge(y_ready, 2 * e)
                        use_piece(j, q, last, e if c == (6 if tail else 8) else None)
                        if c == 1 and not tail:
                            turn_in(e + 1, 1 - par, j + par)
                        if c == 4:
                            if not tail:
                                pe.wait_ge(xe_lo_ready, e + 2)
                            turn_hidden(e, 0)
                        if c == (5 if tail else 6):
                            turn_hidden(e, 1)
                        if not first and COMB <= q < COMB + ADDS:
                            combine(pair - 1, q - COMB)

                turn_in(layer * NE, 0, 0)
                pe.wait_ge(xe_lo_ready, layer * NE + 1)
                for q in range(-AHEAD, 0):
                    use_piece(0, q)
                pair_body(0, first=True)
                with pe.Fori(1, PAIRS - 1) as j:
                    pair_body(j)
                pair_body(PAIRS - 1, last=True)
                for n in range(ADDS):
                    combine(PAIRS * (layer + 1) - 1, n, LAST_BANKS)
                pe.wait_ge(moe_added, ADDS * PAIRS * (layer + 1))


_OUTS = [((1, SEQ, DM), "float32"), ((1, DEC_SEQ, DM), "float32")]


def kernel(**inputs):
    import concourse.bacc as bacc
    from concourse.bass_utils import run_bass_kernel_spmd

    nc = bacc.Bacc("TRN2", target_bir_lowering=False, num_devices=1)
    arrays, tensors = {}, {}
    for name, a in {**inputs, **shape_constants()}.items():
        a = np.ascontiguousarray(a)
        arrays[f"in_{name}"] = a
        tensors[name] = nc.dram_tensor(f"in_{name}", a.shape, mybir.dt.from_np(a.dtype), kind="ExternalInput").ap()
    outs = [nc.dram_tensor(f"out_{i}", shape, mybir.dt.from_np(np.dtype(dtype)), kind="ExternalOutput").ap()
            for i, (shape, dtype) in enumerate(_OUTS)]
    build_trunk(nc, tensors, outs)
    r = run_bass_kernel_spmd(nc, [arrays], core_ids=[0])
    return tuple(r.results[0][f"out_{i}"] for i in range(len(_OUTS)))
```
